# Optimizing a Trainium2 kernel written in Bass

```python
import jax, jax.numpy as jnp
from jax import lax
import numpy as np
import math

D_MODEL = 1024
BATCH = 1
SEQ = 256
DEPTH = 2

CHUNK = 64
HEAD_DIM = 64
SWA_HEADS = 8
SWA_KV_HEADS = 2
SWA_GROUP = SWA_HEADS // SWA_KV_HEADS
SWA_WINDOW = 128
SWA_WIN_CHUNKS = (SWA_WINDOW + CHUNK - 1) // CHUNK
RWKV_HEADS = 4
RWKV_W_RANK = 64
RWKV_A_RANK = 64
RWKV_G_RANK = 128
RWKV_GN_EPS = 64e-5
FOX_HEADS = 4
FOX_BLOCK = 128
DSA_HEADS = 4
IDX_HEADS = 4
IDX_DIM = 64
DSA_TOPK_MAX = 256
DSA_BLOCK = 128
D_FF = 2816
N_EXPERTS = 8
TOP_K = 2
D_FF_EXPERT = 1408
N_DENSE = (DEPTH + 1) // 2
N_MOE = DEPTH // 2
N_BRANCHES = 4
DN_ALPHA = (2 * DEPTH) ** 0.25
DN_BETA = (8 * DEPTH) ** -0.25
LN_EPS = 1e-5
ATTN_SCALE = HEAD_DIM ** -0.5
IDX_SCALE = IDX_DIM ** -0.5
IDX_W_SCALE = IDX_HEADS ** -0.5

SWA_Q = SWA_HEADS * HEAD_DIM
SWA_KV = SWA_KV_HEADS * HEAD_DIM
RWKV_W = RWKV_HEADS * HEAD_DIM
FOX_W = FOX_HEADS * HEAD_DIM
DSA_W = DSA_HEADS * HEAD_DIM
MIX_WIDTHS = (SWA_Q, RWKV_W, FOX_W, DSA_W)
MIX_WIDTH = SWA_Q + RWKV_W + FOX_W + DSA_W
SWA_SPLITS = (SWA_Q, SWA_KV, SWA_KV)
RWKV_SPLITS = (RWKV_W, RWKV_W, RWKV_W, RWKV_W_RANK, RWKV_A_RANK, RWKV_G_RANK)
FOX_SPLITS = (FOX_W, FOX_W, FOX_W, FOX_HEADS)
DSA_SPLITS = (DSA_W, HEAD_DIM, HEAD_DIM, IDX_HEADS * IDX_DIM, IDX_DIM, IDX_HEADS)
RWKV_IN = sum(RWKV_SPLITS)
GATE_COLS = N_BRANCHES * D_MODEL
IN_GROUPS = (sum(SWA_SPLITS), RWKV_IN, sum(FOX_SPLITS), sum(DSA_SPLITS), GATE_COLS)
D_IN = sum(IN_GROUPS)


def split_cols(t, sizes, axis=-1):
    idx = [int(i) for i in np.cumsum(sizes)[:-1]]
    return jnp.split(t, idx, axis=axis)

def layer_norm(x, g, b):
    xf = x.astype(jnp.float32)
    mu = jnp.mean(xf, axis=-1, keepdims=True)
    var = jnp.mean(jnp.square(xf - mu), axis=-1, keepdims=True)
    return ((xf - mu) * lax.rsqrt(var + LN_EPS) * g + b).astype(x.dtype)

def swa_branch(q, k, v, sinks):
    B, S, _ = q.shape
    nc = S // CHUNK
    W = SWA_WIN_CHUNKS
    q = q.reshape(B, nc, CHUNK, SWA_KV_HEADS, SWA_GROUP, HEAD_DIM)
    pad = ((0, 0), (W, 0), (0, 0), (0, 0), (0, 0))
    kp = jnp.pad(k.reshape(B, nc, CHUNK, SWA_KV_HEADS, HEAD_DIM), pad)
    vp = jnp.pad(v.reshape(B, nc, CHUNK, SWA_KV_HEADS, HEAD_DIM), pad)
    kb = jnp.concatenate([kp[:, j:j + nc] for j in range(W + 1)], axis=2)
    vb = jnp.concatenate([vp[:, j:j + nc] for j in range(W + 1)], axis=2)
    key_chunk = jnp.arange(nc)[:, None] - W + jnp.arange(W + 1)[None, :]
    valid = jnp.repeat(key_chunk >= 0, CHUNK, axis=1)
    logits = jnp.einsum('bcqhgd,bckhd->bchgqk', q, kb).astype(jnp.float32) * ATTN_SCALE
    logits = jnp.where(valid[None, :, None, None, None, :], logits, -jnp.inf)
    sink = sinks.astype(jnp.float32).reshape(1, 1, SWA_KV_HEADS, SWA_GROUP, 1, 1)
    m = jnp.maximum(jnp.max(logits, axis=-1, keepdims=True), sink)
    e = jnp.exp(logits - m)
    p = e / (jnp.sum(e, axis=-1, keepdims=True) + jnp.exp(sink - m))
    o = jnp.einsum('bchgqk,bckhd->bcqhgd', p.astype(v.dtype), vb)
    return o.reshape(B, S, SWA_Q)

def rwkv7_branch(p, mu, w0, w_up, a0, a_up, g_up, k_k, k_a, r_k, gn_g, gn_b):
    B, S, _ = p.shape
    p_prev = jnp.pad(p[:, :-1], ((0, 0), (1, 0), (0, 0)))
    p = p + mu * (p_prev - p)
    r, k, v, w_lo, a_lo, g_lo = split_cols(p, RWKV_SPLITS)
    log_w = -jnp.exp(-jax.nn.softplus(-(w0 + jnp.tanh(w_lo) @ w_up).astype(jnp.float32)) - 0.5)
    a = jax.nn.sigmoid(a0 + a_lo @ a_up)
    g = jax.nn.sigmoid(g_lo) @ g_up
    hd = lambda t: t.reshape(B, S, RWKV_HEADS, HEAD_DIM).astype(jnp.float32)
    kk = hd(k * k_k)
    kk = kk * lax.rsqrt(jnp.sum(kk * kk, axis=-1, keepdims=True) + 1e-12)
    k = k * (1.0 + (a - 1.0) * k_a)
    r_h, k_h, v_h, a_h, w_h = hd(r), hd(k), hd(v), hd(a), hd(jnp.exp(log_w))
    seq = tuple(jnp.moveaxis(t, 1, 0) for t in (r_h, w_h, k_h, v_h, kk, a_h))

    def step(state, inp):
        r_t, w_t, k_t, v_t, kk_t, a_t = inp
        sa = jnp.einsum('bhvk,bhk->bhv', state, -kk_t)
        state = (state * w_t[:, :, None, :]
                 + sa[..., None] * (kk_t * a_t)[:, :, None, :]
                 + v_t[..., None] * k_t[:, :, None, :])
        return state, jnp.einsum('bhvk,bhk->bhv', state, r_t)

    s0 = jnp.zeros((B, RWKV_HEADS, HEAD_DIM, HEAD_DIM), jnp.float32)
    _, y = lax.scan(step, s0, seq)
    y = jnp.moveaxis(y, 0, 1)
    ym = jnp.mean(y, axis=-1, keepdims=True)
    yv = jnp.mean(jnp.square(y - ym), axis=-1, keepdims=True)
    y = ((y - ym) * lax.rsqrt(yv + RWKV_GN_EPS)).reshape(B, S, RWKV_W) * gn_g + gn_b
    bonus = (jnp.sum(r_h * k_h * r_k, axis=-1, keepdims=True) * v_h).reshape(B, S, RWKV_W)
    return ((y + bonus) * g).astype(p.dtype)

def fox_branch(q, k, v, f_logit, f_bias):
    B, S, _ = q.shape
    q = q.reshape(B, S, FOX_HEADS, HEAD_DIM)
    k = k.reshape(B, S, FOX_HEADS, HEAD_DIM)
    v = v.reshape(B, S, FOX_HEADS, HEAD_DIM)
    log_f = jax.nn.log_sigmoid(f_logit.astype(jnp.float32) + f_bias)
    c = jnp.cumsum(log_f, axis=1).transpose(0, 2, 1)
    outs = []
    for blk in range(S // FOX_BLOCK):
        lo, hi = blk * FOX_BLOCK, (blk + 1) * FOX_BLOCK
        logits = jnp.einsum('bqhd,bkhd->bhqk', q[:, lo:hi], k[:, :hi]).astype(jnp.float32) * ATTN_SCALE
        logits = logits + c[:, :, lo:hi, None] - c[:, :, None, :hi]
        causal = jnp.arange(lo, hi)[:, None] >= jnp.arange(hi)[None, :]
        logits = jnp.where(causal, logits, -jnp.inf)
        p = jax.nn.softmax(logits, axis=-1)
        outs.append(jnp.einsum('bhqk,bkhd->bqhd', p.astype(v.dtype), v[:, :hi]))
    return jnp.concatenate(outs, axis=1).reshape(B, S, FOX_W)

def dsa_branch(q, k, v, q_idx, k_idx, w_idx):
    B, S, _ = q.shape
    topk = min(DSA_TOPK_MAX, S // 4)
    nb = S // DSA_BLOCK
    qT = jnp.moveaxis(q.reshape(B, nb, DSA_BLOCK, DSA_HEADS, HEAD_DIM), 1, 0)
    qiT = jnp.moveaxis(q_idx.reshape(B, nb, DSA_BLOCK, IDX_HEADS, IDX_DIM), 1, 0)
    wiT = jnp.moveaxis(w_idx.reshape(B, nb, DSA_BLOCK, IDX_HEADS), 1, 0)
    key_chunk = jnp.arange(S) // CHUNK

    def block(args):
        blk, qb, qib, wib = args
        t = blk * DSA_BLOCK + jnp.arange(DSA_BLOCK)
        admissible = key_chunk[None, :] <= (t // CHUNK)[:, None]
        rel = jax.nn.relu(jnp.einsum('bqhd,bsd->bqhs', qib, k_idx) * IDX_SCALE)
        score = jnp.einsum('bqhs,bqh->bqs', rel, wib * IDX_W_SCALE).astype(jnp.float32)
        score = jnp.where(admissible[None], score, -jnp.inf)
        top_val, top_idx = lax.top_k(score, topk)
        valid = jnp.isfinite(top_val)
        k_sel = jax.vmap(lambda kk, ii: kk[ii])(k, top_idx)
        v_sel = jax.vmap(lambda vv, ii: vv[ii])(v, top_idx)
        logits = jnp.einsum('bqhd,bqkd->bqhk', qb, k_sel).astype(jnp.float32) * ATTN_SCALE
        logits = jnp.where(valid[:, :, None, :], logits, -jnp.inf)
        p = jax.nn.softmax(logits, axis=-1)
        return jnp.einsum('bqhk,bqkd->bqhd', p.astype(v.dtype), v_sel)

    outs = lax.map(block, (jnp.arange(nb), qT, qiT, wiT))
    return jnp.moveaxis(outs, 0, 1).reshape(B, S, DSA_W)

def mixer_block(x, w_in, sinks, mu, w0, w_up, a0, a_up, g_up, k_k, k_a, r_k, gn_g, gn_b,
                f_bias, gate_bias, w_branch, w_out):
    B, S, _ = x.shape
    p_swa, p_rwkv, p_fox, p_dsa, p_gate = split_cols(x @ w_in, IN_GROUPS)
    o_swa = swa_branch(*split_cols(p_swa, SWA_SPLITS), sinks)
    o_rwkv = rwkv7_branch(p_rwkv, mu, w0, w_up, a0, a_up, g_up, k_k, k_a, r_k, gn_g, gn_b)
    o_fox = fox_branch(*split_cols(p_fox, FOX_SPLITS), f_bias)
    o_dsa = dsa_branch(*split_cols(p_dsa, DSA_SPLITS))
    gates = jax.nn.sigmoid(p_gate.reshape(B, S, N_BRANCHES, D_MODEL) + gate_bias)
    w_rows = split_cols(w_branch, MIX_WIDTHS, axis=0)
    merged = jnp.zeros_like(x)
    for i, (o, w) in enumerate(zip((o_swa, o_rwkv, o_fox, o_dsa), w_rows)):
        merged = merged + gates[:, :, i] * (o @ w)
    return merged @ w_out

def swiglu(x, w1, w3, w2):
    return (jax.nn.silu(x @ w1) * (x @ w3)) @ w2

def moe_ffn(x, router_w, router_b, w1, w3, w2):
    logits = (x @ router_w).astype(jnp.float32) + router_b
    top_val, top_idx = lax.top_k(logits, TOP_K)
    weights = jax.nn.softmax(top_val, axis=-1)
    combine = jnp.sum(jax.nn.one_hot(top_idx, N_EXPERTS, dtype=jnp.float32) * weights[..., None], axis=-2)
    y = jnp.zeros_like(x)
    for e in range(N_EXPERTS):
        y = y + combine[..., e:e + 1].astype(x.dtype) * swiglu(x, w1[e], w3[e], w2[e])
    return y

def first_inputs(seed: int = 0) -> dict:
    key = jax.random.key(seed)
    ks = iter(jax.random.split(key, 32))
    nrm = lambda shape, scale: scale * jax.random.normal(next(ks), shape, jnp.float32)
    unif = lambda shape, lo, hi: jax.random.uniform(next(ks), shape, jnp.float32, lo, hi)
    L = DEPTH
    return {
        'x': nrm((BATCH, SEQ, D_MODEL), 1.0),
        'w_in': nrm((L, D_MODEL, D_IN), D_MODEL ** -0.5),
        'swa_sinks': nrm((L, SWA_HEADS), 0.5),
        'rwkv_mu': unif((L, RWKV_IN), 0.0, 1.0),
        'rwkv_w0': unif((L, RWKV_W), -6.0, 1.0),
        'rwkv_w_up': nrm((L, RWKV_W_RANK, RWKV_W), 0.1),
        'rwkv_a0': nrm((L, RWKV_W), 0.1),
        'rwkv_a_up': nrm((L, RWKV_A_RANK, RWKV_W), RWKV_A_RANK ** -0.5),
        'rwkv_g_up': nrm((L, RWKV_G_RANK, RWKV_W), RWKV_G_RANK ** -0.5),
        'rwkv_k_k': 0.85 + nrm((L, RWKV_W), 0.05),
        'rwkv_k_a': 1.0 + nrm((L, RWKV_W), 0.05),
        'rwkv_r_k': nrm((L, RWKV_HEADS, HEAD_DIM), 0.1),
        'rwkv_gn_g': 1.0 + nrm((L, RWKV_W), 0.05),
        'rwkv_gn_b': nrm((L, RWKV_W), 0.02),
        'fox_f_bias': 2.0 + nrm((L, FOX_HEADS), 0.5),
        'gate_bias': nrm((L, N_BRANCHES, D_MODEL), 0.1),
        'w_branch': nrm((L, MIX_WIDTH, D_MODEL), (4 * HEAD_DIM) ** -0.5),
        'w_out': nrm((L, D_MODEL, D_MODEL), DN_BETA * D_MODEL ** -0.5),
        'ln_g': 1.0 + nrm((L, 2, D_MODEL), 0.05),
        'ln_b': nrm((L, 2, D_MODEL), 0.02),
        'ffn_w1': nrm((N_DENSE, D_MODEL, D_FF), D_MODEL ** -0.5),
        'ffn_w3': nrm((N_DENSE, D_MODEL, D_FF), D_MODEL ** -0.5),
        'ffn_w2': nrm((N_DENSE, D_FF, D_MODEL), DN_BETA * D_FF ** -0.5),
        'router_w': nrm((N_MOE, D_MODEL, N_EXPERTS), D_MODEL ** -0.5),
        'router_b': nrm((N_MOE, N_EXPERTS), 0.01),
        'exp_w1': nrm((N_MOE, N_EXPERTS, D_MODEL, D_FF_EXPERT), D_MODEL ** -0.5),
        'exp_w3': nrm((N_MOE, N_EXPERTS, D_MODEL, D_FF_EXPERT), D_MODEL ** -0.5),
        'exp_w2': nrm((N_MOE, N_EXPERTS, D_FF_EXPERT, D_MODEL), DN_BETA * D_FF_EXPERT ** -0.5),
    }

def first_block(x, w_in, swa_sinks, rwkv_mu, rwkv_w0, rwkv_w_up, rwkv_a0, rwkv_a_up, rwkv_g_up,
              rwkv_k_k, rwkv_k_a, rwkv_r_k, rwkv_gn_g, rwkv_gn_b, fox_f_bias, gate_bias, w_branch,
              w_out, ln_g, ln_b, ffn_w1, ffn_w3, ffn_w2, router_w, router_b, exp_w1, exp_w3, exp_w2):
    for layer in range(DEPTH):
        y = mixer_block(x, w_in[layer], swa_sinks[layer], rwkv_mu[layer], rwkv_w0[layer],
                        rwkv_w_up[layer], rwkv_a0[layer], rwkv_a_up[layer], rwkv_g_up[layer],
                        rwkv_k_k[layer], rwkv_k_a[layer], rwkv_r_k[layer], rwkv_gn_g[layer],
                        rwkv_gn_b[layer], fox_f_bias[layer], gate_bias[layer], w_branch[layer],
                        w_out[layer])
        x = layer_norm(DN_ALPHA * x + y, ln_g[layer, 0], ln_b[layer, 0])
        j = layer // 2
        if layer % 2 == 0:
            y = swiglu(x, ffn_w1[j], ffn_w3[j], ffn_w2[j])
        else:
            y = moe_ffn(x, router_w[j], router_b[j], exp_w1[j], exp_w3[j], exp_w2[j])
        x = layer_norm(DN_ALPHA * x + y, ln_g[layer, 1], ln_b[layer, 1])
    return x


MOBA_HEADS = (D_MODEL // 2) // HEAD_DIM
MOBA_WIDTH = MOBA_HEADS * HEAD_DIM
DIFF_HEADS = (D_MODEL // 2) // (2 * HEAD_DIM)
DIFF_V_DIM = 2 * HEAD_DIM
DIFF_WIDTH = DIFF_HEADS * DIFF_V_DIM
MIX_WIDTH_2 = MOBA_WIDTH + DIFF_WIDTH
IN_WIDTH = 3 * MOBA_WIDTH + 3 * DIFF_WIDTH
MOBA_BLOCK = 256
MOBA_TOPK = 3
MOBA_Q_CHUNK = 64
DENSE_Q_BLOCK = 128
ROPE_THETA = 500000.0
ROPE_DIM = HEAD_DIM // 4
D_FF_2 = -(-(8 * D_MODEL) // (3 * 256)) * 256
N_MOD = 6
EPS = 1e-6


def rms_norm(x, g):
    xf = x.astype(jnp.float32)
    y = xf * lax.rsqrt(jnp.mean(xf * xf, axis=-1, keepdims=True) + EPS)
    return (y * g.astype(jnp.float32)).astype(x.dtype)

def rope_tables(positions):
    inv = ROPE_THETA ** (-jnp.arange(0, ROPE_DIM, 2, dtype=jnp.float32) / ROPE_DIM)
    ang = positions.astype(jnp.float32)[..., None] * inv
    return jnp.cos(ang)[:, None], jnp.sin(ang)[:, None]

def apply_partial_rope(x, cos, sin):
    half = ROPE_DIM // 2
    xf = x.astype(jnp.float32)
    x1 = xf[..., :half]
    x2 = xf[..., half:ROPE_DIM]
    out = jnp.concatenate([x1 * cos - x2 * sin, x2 * cos + x1 * sin, xf[..., ROPE_DIM:]], axis=-1)
    return out.astype(x.dtype)

def moba_attention(q, k, v):
    B, H, S, dh = q.shape
    nb = -(-S // MOBA_BLOCK)
    pad = nb * MOBA_BLOCK - S
    kp = jnp.pad(k, ((0, 0), (0, 0), (0, pad), (0, 0)))
    vp = jnp.pad(v, ((0, 0), (0, 0), (0, pad), (0, 0)))
    kb = kp.reshape(B, H, nb, MOBA_BLOCK, dh)
    vb = vp.reshape(B, H, nb, MOBA_BLOCK, dh)
    k_mean = jnp.mean(kb.astype(jnp.float32), axis=3)
    topk = min(MOBA_TOPK, nb)
    n_chunks = S // MOBA_Q_CHUNK
    scale = dh ** -0.5
    b_ids = jnp.repeat(jnp.arange(B, dtype=jnp.int32), n_chunks)
    c_ids = jnp.tile(jnp.arange(n_chunks, dtype=jnp.int32), B)
    h_ids = jnp.arange(H)[:, None, None]
    blk_ids = jnp.arange(nb)

    def one_chunk(args):
        b, ci = args
        q0 = ci * MOBA_Q_CHUNK
        qblk = q0 // MOBA_BLOCK
        qpos = q0 + jnp.arange(MOBA_Q_CHUNK)
        qc = lax.dynamic_slice_in_dim(q[b], q0, MOBA_Q_CHUNK, axis=1)
        gate = jnp.einsum('hqd,hnd->hqn', qc.astype(jnp.float32), k_mean[b])
        gate = jnp.where(blk_ids < qblk, gate, -jnp.inf)
        _, idx = lax.top_k(gate, topk)
        sel_valid = idx < qblk
        k_sel = kb[b][h_ids, idx]
        v_sel = vb[b][h_ids, idx]
        s_sel = jnp.einsum('hqd,hqjkd->hqjk', qc, k_sel).astype(jnp.float32) * scale
        s_sel = jnp.where(sel_valid[..., None], s_sel, -jnp.inf)
        k_own = lax.dynamic_slice_in_dim(kp[b], qblk * MOBA_BLOCK, MOBA_BLOCK, axis=1)
        v_own = lax.dynamic_slice_in_dim(vp[b], qblk * MOBA_BLOCK, MOBA_BLOCK, axis=1)
        s_own = jnp.einsum('hqd,hkd->hqk', qc, k_own).astype(jnp.float32) * scale
        kpos = qblk * MOBA_BLOCK + jnp.arange(MOBA_BLOCK)
        s_own = jnp.where(kpos[None, :] <= qpos[:, None], s_own, -jnp.inf)
        s = jnp.concatenate([s_sel.reshape(H, MOBA_Q_CHUNK, topk * MOBA_BLOCK), s_own], axis=-1)
        p = jax.nn.softmax(s, axis=-1).astype(v.dtype)
        p_sel = p[..., :topk * MOBA_BLOCK].reshape(H, MOBA_Q_CHUNK, topk, MOBA_BLOCK)
        p_own = p[..., topk * MOBA_BLOCK:]
        return (jnp.einsum('hqjk,hqjkd->hqd', p_sel, v_sel)
                + jnp.einsum('hqk,hkd->hqd', p_own, v_own))

    out = lax.map(one_chunk, (b_ids, c_ids))
    out = out.reshape(B, n_chunks, H, MOBA_Q_CHUNK, dh).transpose(0, 2, 1, 3, 4)
    return out.reshape(B, H, S, dh)

def diff_attention(q, k, v, lam):
    B, H, _, S, dh = q.shape
    n_qb = S // DENSE_Q_BLOCK
    scale = dh ** -0.5
    kpos = jnp.arange(S)

    def one_block(ci):
        q0 = ci * DENSE_Q_BLOCK
        qc = lax.dynamic_slice_in_dim(q, q0, DENSE_Q_BLOCK, axis=3)
        s = jnp.einsum('bhcqd,bhckd->bhcqk', qc, k).astype(jnp.float32) * scale
        qpos = q0 + jnp.arange(DENSE_Q_BLOCK)
        s = jnp.where(kpos[None, :] <= qpos[:, None], s, -jnp.inf)
        a = jax.nn.softmax(s, axis=-1)
        w = (a[:, :, 0] - lam * a[:, :, 1]).astype(v.dtype)
        return jnp.einsum('bhqk,bhkd->bhqd', w, v)

    out = lax.map(one_block, jnp.arange(n_qb, dtype=jnp.int32))
    return out.transpose(1, 2, 0, 3, 4).reshape(B, H, S, v.shape[-1])

def second_inputs(seed: int = 0) -> dict:
    key = jax.random.key(seed)
    ks = jax.random.split(key, 20)
    f32 = jnp.float32
    L = DEPTH

    def nrm(k, shape, scale):
        return jax.random.normal(k, shape, f32) * scale

    def gain(k, shape):
        return 1.0 + 0.02 * jax.random.normal(k, shape, f32)

    return {
        'x': nrm(ks[0], (BATCH, SEQ, D_MODEL), 1.0),
        'c': nrm(ks[1], (BATCH, D_MODEL), 1.0),
        'positions': jnp.broadcast_to(jnp.arange(SEQ, dtype=jnp.int32)[None, :], (BATCH, SEQ)),
        'w_mod': nrm(ks[2], (L, D_MODEL, N_MOD * D_MODEL), 0.5 * D_MODEL ** -0.5),
        'b_mod': nrm(ks[3], (L, N_MOD * D_MODEL), 0.01),
        'norm_mix': gain(ks[4], (L, D_MODEL)),
        'w_in': nrm(ks[5], (L, D_MODEL, IN_WIDTH), D_MODEL ** -0.5),
        'moba_q_norm': gain(ks[6], (L, HEAD_DIM)),
        'moba_k_norm': gain(ks[7], (L, HEAD_DIM)),
        'moba_out_norm': gain(ks[8], (L, HEAD_DIM)),
        'diff_q_norm': gain(ks[9], (L, HEAD_DIM)),
        'diff_k_norm': gain(ks[10], (L, HEAD_DIM)),
        'diff_lambda': nrm(ks[11], (L, 4, HEAD_DIM), 0.1),
        'diff_subln': gain(ks[12], (L, DIFF_V_DIM)),
        'w_out': nrm(ks[13], (L, MIX_WIDTH_2, D_MODEL), MIX_WIDTH_2 ** -0.5),
        'norm_ffn': gain(ks[14], (L, D_MODEL)),
        'w_gate': nrm(ks[15], (L, D_MODEL, D_FF_2), D_MODEL ** -0.5),
        'w_up': nrm(ks[16], (L, D_MODEL, D_FF_2), D_MODEL ** -0.5),
        'w_down': nrm(ks[17], (L, D_FF_2, D_MODEL), D_FF_2 ** -0.5),
    }

def second_block(x, c, positions, w_mod, b_mod, norm_mix, w_in, moba_q_norm, moba_k_norm,
              moba_out_norm, diff_q_norm, diff_k_norm, diff_lambda, diff_subln, w_out,
              norm_ffn, w_gate, w_up, w_down):
    B, S, _ = x.shape
    cos, sin = rope_tables(positions)
    cond = jax.nn.silu(c)
    splits = [MOBA_WIDTH, 2 * MOBA_WIDTH, 3 * MOBA_WIDTH,
              3 * MOBA_WIDTH + DIFF_WIDTH, 3 * MOBA_WIDTH + 2 * DIFF_WIDTH]

    def heads(t, n, d):
        return t.reshape(B, S, n, d).transpose(0, 2, 1, 3)

    for l in range(DEPTH):
        mod = (cond @ w_mod[l] + b_mod[l])[:, None, :]
        sh_a, sc_a, g_a, sh_f, sc_f, g_f = jnp.split(mod, N_MOD, axis=-1)

        h = rms_norm(x, norm_mix[l]) * (1 + sc_a) + sh_a
        proj = h @ w_in[l]
        mq, mk, mv, dq, dk, dv = jnp.split(proj, splits, axis=-1)

        mq = apply_partial_rope(rms_norm(heads(mq, MOBA_HEADS, HEAD_DIM), moba_q_norm[l]), cos, sin)
        mk = apply_partial_rope(rms_norm(heads(mk, MOBA_HEADS, HEAD_DIM), moba_k_norm[l]), cos, sin)
        mv = heads(mv, MOBA_HEADS, HEAD_DIM)
        o_m = rms_norm(moba_attention(mq, mk, mv), moba_out_norm[l])
        o_m = o_m.transpose(0, 2, 1, 3).reshape(B, S, MOBA_WIDTH)

        dq = apply_partial_rope(rms_norm(heads(dq, 2 * DIFF_HEADS, HEAD_DIM), diff_q_norm[l]), cos, sin)
        dk = apply_partial_rope(rms_norm(heads(dk, 2 * DIFF_HEADS, HEAD_DIM), diff_k_norm[l]), cos, sin)
        dq = dq.reshape(B, DIFF_HEADS, 2, S, HEAD_DIM)
        dk = dk.reshape(B, DIFF_HEADS, 2, S, HEAD_DIM)
        dv = heads(dv, DIFF_HEADS, DIFF_V_DIM)
        lam_init = 0.8 - 0.6 * math.exp(-0.3 * l)
        lp = diff_lambda[l].astype(jnp.float32)
        lam = jnp.exp(jnp.sum(lp[0] * lp[1])) - jnp.exp(jnp.sum(lp[2] * lp[3])) + lam_init
        o_d = rms_norm(diff_attention(dq, dk, dv, lam), diff_subln[l]) * (1.0 - lam_init)
        o_d = o_d.transpose(0, 2, 1, 3).reshape(B, S, DIFF_WIDTH)

        x = x + g_a * (jnp.concatenate([o_m, o_d], axis=-1) @ w_out[l])

        h = rms_norm(x, norm_ffn[l]) * (1 + sc_f) + sh_f
        x = x + g_f * ((jax.nn.silu(h @ w_gate[l]) * (h @ w_up[l])) @ w_down[l])
    return x


def setup_inputs(seed=0):
    out = dict(first_inputs(seed))
    for name, value in second_inputs(seed + 1).items():
        if name != "x":
            out[name + "_2"] = value
    return out


def reference(
    x, w_in, swa_sinks, rwkv_mu, rwkv_w0, rwkv_w_up, rwkv_a0, rwkv_a_up, rwkv_g_up, rwkv_k_k,
    rwkv_k_a, rwkv_r_k, rwkv_gn_g, rwkv_gn_b, fox_f_bias, gate_bias, w_branch, w_out, ln_g,
    ln_b, ffn_w1, ffn_w3, ffn_w2, router_w, router_b, exp_w1, exp_w3, exp_w2, c_2, positions_2,
    w_mod_2, b_mod_2, norm_mix_2, w_in_2, moba_q_norm_2, moba_k_norm_2, moba_out_norm_2,
    diff_q_norm_2, diff_k_norm_2, diff_lambda_2, diff_subln_2, w_out_2, norm_ffn_2, w_gate_2,
    w_up_2, w_down_2,
):
    x = first_block(
        x, w_in, swa_sinks, rwkv_mu, rwkv_w0, rwkv_w_up, rwkv_a0, rwkv_a_up, rwkv_g_up,
        rwkv_k_k, rwkv_k_a, rwkv_r_k, rwkv_gn_g, rwkv_gn_b, fox_f_bias, gate_bias, w_branch,
        w_out, ln_g, ln_b, ffn_w1, ffn_w3, ffn_w2, router_w, router_b, exp_w1, exp_w3, exp_w2,
    )
    return second_block(
        x, c_2, positions_2, w_mod_2, b_mod_2, norm_mix_2, w_in_2, moba_q_norm_2, moba_k_norm_2,
        moba_out_norm_2, diff_q_norm_2, diff_k_norm_2, diff_lambda_2, diff_subln_2, w_out_2,
        norm_ffn_2, w_gate_2, w_up_2, w_down_2,
    )


_drawn_inputs = setup_inputs


def setup_inputs(seed=0):
    import zlib

    import numpy as np

    out = dict(_drawn_inputs(seed))
    spreads = {}
    factors = {'swa_sinks': 8.0,
     'rwkv_w_up': 8.0,
     'rwkv_a0': 7.995,
     'rwkv_k_k': 8.0,
     'rwkv_k_a': 3.975,
     'rwkv_gn_g': 4.98,
     'rwkv_gn_b': 7.933,
     'gate_bias': 3.769,
     'router_b': 4.769,
     'b_mod_2': 2.89,
     'norm_mix_2': 8.0,
     'moba_q_norm_2': 8.0,
     'moba_k_norm_2': 8.0,
     'moba_out_norm_2': 8.0,
     'diff_q_norm_2': 8.0,
     'diff_k_norm_2': 8.0,
     'diff_lambda_2': 4.545,
     'diff_subln_2': 8.0,
     'norm_ffn_2': 7.114}
    for name, (base, spread) in spreads.items():
        noise = np.random.default_rng([zlib.crc32(name.encode()), seed]).standard_normal(out[name].shape)
        drawn = base * np.exp(spread * noise) if base else spread * noise
        out[name] = __import__('jax').numpy.asarray(drawn.astype(out[name].dtype))
    for name, factor in factors.items():
        out[name] = (out[name] * factor).astype(out[name].dtype)
    return out
```

```python
from contextlib import ExitStack, contextmanager
import math

import numpy as np
import concourse.bass as bass
from concourse import mybir

F32 = mybir.dt.float32
U32 = mybir.dt.uint32
I32 = mybir.dt.int32
ALU = mybir.AluOpType
ACT = mybir.ActivationFunctionType
AX = mybir.AxisListType.X

P = 128
D = 1024
KT = D // P
SEQ = 256
NT = SEQ // P
DEPTH = 2
HD = 64
CH = 64
NC = SEQ // CH
FF = 1408
FT = FF // P
STEPS = (FT + 1) // 2
N_EXP = 8
IN_SWA, IN_RWKV, IN_FOX, IN_DSA, IN_GATE = 0, 768, 1792, 2564, 3272
TOPK = 64
TWO_PI_A = 6.28125
TWO_PI_B = float(np.floor((2 * math.pi - TWO_PI_A) * 2.0 ** 21) / 2.0 ** 21)
TWO_PI_C = 2 * math.pi - TWO_PI_A - TWO_PI_B
PI_IN = 3.1415925
ALPHA = (2 * DEPTH) ** 0.25
LN_EPS = 1e-5
GN_EPS = 64e-5
RMS_EPS = 1e-6
SCALE = HD ** -0.5
DECAY = math.exp(-0.5)
NEG = -1e30
TAKEN = -3e38
ROPE_HALF = 8
ROPE_THETA = 500000.0
SLOTS = 6
SLOT = 2048
UNIT = 256

PARAMS = [("mu", 8), ("w0", 2), ("a0", 2), ("k_k", 2), ("k_a", 2), ("r_k", 2), ("gn_g", 2), ("gn_b", 2),
          ("gate_b", 32), ("norm_mix", 8), ("norm_ffn", 8), ("b_mod", 48)]
GAINS = [("moba_q", 64), ("moba_k", 64), ("diff_q", 64), ("diff_k", 64), ("moba_out", 64), ("diff_sub", 128),
         ("lambda", 256)]


class Signals:

    def __init__(self, nc, ctx, known):
        self.nc, self.ctx = nc, ctx
        self.sems, self.count, self.value, self.per_turn = {}, {}, {}, {}
        self.known = known
        self.turn = None

    def sem(self, kind):
        if kind not in self.sems:
            self.sems[kind] = self.ctx.enter_context(self.nc.semaphore(kind))
        return self.sems[kind]

    def made(self, kind, *key, by=1):
        self.count[kind] = self.count.get(kind, 0) + by
        self.value[(kind, key)] = (self.count[kind], self.turn is not None)
        return self.sem(kind), by

    def also(self, kind, *key):
        self.value[(kind, key)] = (self.count[kind], self.turn is not None)

    def ready(self, kind, *key, back=0):
        value, looped = self.known.value[(kind, key)] if self.known else (1, False)
        if looped:
            step, n = self.known.per_turn[kind]
            if self.turn is not None:
                return self.sem(kind), self.turn * step + (value - back * step)
            return self.sem(kind), value + (n - 1) * step
        return self.sem(kind), value

    @contextmanager
    def turns(self, eng, n):
        before = dict(self.count)
        with eng.Fori(0, n) as turn:
            self.turn = turn
            yield turn
        self.turn = None
        for kind, c in self.count.items():
            step = c - before.get(kind, 0)
            if step:
                self.per_turn[kind] = (step, n)
                self.count[kind] += (n - 1) * step


def build(nc, a, out, known):
    with ExitStack() as ctx:
        S = Signals(nc, ctx, known)
        made, ready = S.made, S.ready

        def sb(name, shape, dt=F32):
            return ctx.enter_context(nc.sbuf_tensor(name, shape, dt))

        ring = sb("ring", [P, SLOTS, SLOT])
        x = sb("x", [P, NT, D])
        xT = sb("xT", [P, KT, SEQ])
        oT = sb("oT", [P, 10, SEQ])
        rows = sb("rows", [P, 2, D])
        par = sb("par", [P, DEPTH, sum(n for _, n in PARAMS)])
        gains = sb("gains", [P, sum(n for _, n in GAINS)])
        lora = sb("lora", [P, DEPTH, 2, 256])
        sinks = sb("sinks", [P, DEPTH, 8])
        fbias = sb("fbias", [4, DEPTH])
        router = sb("router", [P, KT, N_EXP])
        router_b = sb("router_b", [P, N_EXP])
        cond = sb("cond", [P, KT])
        pos = sb("pos", [P, NT], I32)
        ident = sb("ident", [P, P])
        block_ones = sb("block_ones", [P, P])
        mask = sb("mask", [P, 3, NT, SEQ])
        tri = sb("tri", [P, 2, CH])
        level = sb("level", [P, 6, CH])
        level0 = sb("level0", [P, CH])
        eye = sb("eye", [P, CH])
        chunk_gate = sb("chunk_gate", [P, SEQ])
        eps = sb("eps", [P, 4])
        invf = sb("invf", [P, ROPE_HALF])
        small = sb("small", [P, 256])
        ARENA = 26200
        arena = sb("arena", [P, ARENA])
        psum = ctx.enter_context(nc.psum_tensor("psum", [P, 8, 512], F32))

        top = [0]

        def view(*shape, parts=P, at=None):
            n = int(np.prod(shape))
            o = top[0] if at is None else at
            if at is None:
                top[0] += n
            assert o + n <= ARENA, (o, n)
            v = arena[0:parts, o:o + n]
            names = "abcd"[:len(shape)]
            if len(shape) > 1:
                v = v.rearrange("p (%s) -> p %s" % (" ".join(names), " ".join(names)),
                                **{k: s for k, s in zip(names, shape)})
            return v

        swa_q, swa_k, swa_v = view(4, SEQ), view(2, SEQ), view(NT, P)
        fox_q, fox_k, fox_v = view(2, SEQ), view(2, SEQ), view(NT, 256)
        fox_f = view(1, SEQ, parts=4)
        dsa_q, dsa_k, dsa_qi, dsa_ki = view(2, SEQ), view(SEQ), view(2, SEQ), view(SEQ)
        dsa_v, dsa_wi = view(NT, HD), view(NT, 4)
        branch_end = top[0]
        raw_at = top[0]
        raw = view(8, SEQ + 1)
        AB = view(2 * NC, 2, CH, at=raw_at)
        mix = view(8, SEQ)
        sw, L, Wc, Wp, Wi, av, gv, kk, sq, kp = [view(2, SEQ) for _ in range(10)]
        Bh, kh = view(2, SEQ), view(2, SEQ)
        KR = view(2, NC, 2, CH)
        GR = view(2 * NC, 2, CH)
        tanh_w = view(SEQ, at=top[0])
        T, TT, U = view(2 * NC, CH), view(2 * NC, CH), view(2 * NC, CH)
        BT = view(5, 2 * NC, CH)
        tokV, tokB, tokK = [view(2 * NC, CH) for _ in range(3)]
        RS, SA = view(2, 2, CH), view(2, 2, CH)
        Z = view(2, 2, CH)
        yv, yn = L, sw
        top[0] = branch_end
        fox_t = view(4, SEQ)
        select = view(2, 4, SEQ)
        score, picked, part = view(SEQ), view(NT, SEQ), view(SEQ)
        dsa_bias = view(NT, SEQ)
        Sm = view(3, 2, SEQ)
        PT = view(2, 2, NT, P)
        top[0] = branch_end
        wb = view(10, D)
        sig = view(2, 4, SEQ)
        prod = view(2, 2, 512)
        top[0] = 0
        sil = view(2, 512)
        gT = view(3, 512)
        mergedT = view(KT, SEQ, at=26200 - 2048)
        stat = small[:, 0:24].rearrange("p (t h s) -> p t h s", t=NT, h=2)
        mv = small[:, 24:28].rearrange("p (t s) -> p t s", t=NT)
        sd, rs = small[:, 28:30], small[:, 30:32]
        logit = small[:, 32:48].rearrange("p (t e) -> p t e", t=NT)
        top8 = small[:, 48:64].rearrange("p (t e) -> p t e", t=NT)
        idx8 = small[:, 64:80].rearrange("p (t e) -> p t e", t=NT)
        idxf = small[:, 80:96].rearrange("p (t e) -> p t e", t=NT)
        wts = small[:, 96:100].rearrange("p (t e) -> p t e", t=NT)
        e2, turn_no = small[:, 100:102], small[:, 102:103]
        comb, picks = small[:, 104:106], small[:, 106:110].rearrange("p (t e) -> p t e", t=NT)
        mx, nm, den, es, rc = [small[:, 112 + 6 * i:118 + 6 * i].rearrange("p (b h) -> p b h", b=3)
                               for i in range(5)]
        m8 = small[:, 144:152]
        ss16, rt16, ri16 = [small[:, 152 + 16 * i:168 + 16 * i] for i in range(3)]
        lam = small[:, 200:208]
        top[0] = 3000
        vtm = view(NT, D)
        qT = view(16, SEQ)
        tq, tsq = view(2, 512), view(2, 512)
        rope = view(6, NT * 4 * ROPE_HALF)
        om = view(NT, D)
        grow = view(2, D)
        condb = view(KT, P)
        modT, Amod = view(32), view(2, KT)
        cosb, sinb = view(NT, ROPE_HALF), view(NT, ROPE_HALF)
        ang = view(4, NT * ROPE_HALF)
        angi = ang[:, 3, :].bitcast(I32)
        Sm2, PT2 = view(3, 2, SEQ), view(2, 2, NT, P)
        tok_scaled = view(NT, D)
        ys_tmp = tok_scaled
        oT8 = oT[:, 0:8, :]

        def units_of(seg):
            return UNITS1 if seg == "b1" else UNITS2

        def pt_bank(i):
            return 4 + i % 2

        def in_bank(i):
            return (4 + i) % 8

        def in_copied(ready, l, i):
            return ready("act" if i in (0, 1, 3, 5, 7, 9, 10) else "dve", "in", l, i)

        poff = {}
        o = 0
        for name, n in PARAMS:
            poff[name] = (o, n)
            o += n
        goff = {}
        o = 0
        for name, n in GAINS:
            goff[name] = (o, n)
            o += n

        def prm(l, name, i=0, n=1):
            return par[:, l, poff[name][0] + i:poff[name][0] + i + n]

        def gain(name):
            return gains[:, goff[name][0]:goff[name][0] + goff[name][1]]

        def kview(w):
            return w.rearrange("(k p) c -> p k c", p=P)

        def hb(h):
            return slice(HD * (h % 2), HD * (h % 2) + HD)

        units1 = ([IN_SWA + UNIT * i for i in range(3)] + [IN_RWKV + UNIT * i for i in range(4)]
                  + [IN_FOX + UNIT * i for i in range(3)] + [IN_DSA, None, IN_DSA + 384])

        def unit_list(segment):
            kind, l = segment
            if kind == "in":
                w = kview(a["w_in"][l])
                for i, c in enumerate(units1):
                    if c is None:
                        yield ("in", l, i), [(0, 128, w[:, :, IN_DSA + 256:IN_DSA + 384]),
                                             (128, 68, w[:, :, IN_DSA + 640:IN_DSA + 708]),
                                             (196, 4, w[:, :, IN_FOX + 768:IN_FOX + 772])]
                    else:
                        yield ("in", l, i), [(0, 256, w[:, :, c:c + 256])]
            elif kind == "gate":
                w = kview(a["w_in"][l])
                for cp in range(4):
                    for b in range(4):
                        c = IN_GATE + b * D + cp * 256
                        yield ("gate", l, cp, b), [(0, 256, w[:, :, c:c + 256])]
            elif kind in ("out", "out2"):
                w = kview(a["w_out" if kind == "out" else "w_out_2"][l])
                for k in range(4):
                    yield (kind, l, k), [(None, D, w[:, 2 * k:2 * k + 2, :])]
            elif kind == "mod":
                w = kview(a["w_mod_2"][l])
                for i in range(24):
                    yield ("mod", l, i), [(0, 256, w[:, :, UNIT * i:UNIT * i + 256])]
            elif kind == "in2":
                w = kview(a["w_in_2"][l])
                for i in range(12):
                    yield ("in2", l, i), [(0, 256, w[:, :, UNIT * i:UNIT * i + 256])]

        def ffn_units(name, w1, w3, w2):
            for s in range(STEPS):
                n = min(2, FT - 2 * s)
                yield (name, "w1", s), [(0, n * P, kview(w1)[:, :, s * 256:s * 256 + n * P])]
                yield (name, "w3", s), [(0, n * P, kview(w3)[:, :, s * 256:s * 256 + n * P])]
                yield (name, "w2", s), [(None, D, kview(w2)[:, 2 * s:2 * s + n, :])]

        segments = []
        for l in range(DEPTH):
            segments += [("in", l), ("gate", l), ("out", l), ("ffn1", l) if l == 0 else ("moe", l)]
        for l in range(DEPTH):
            segments += [("mod", l), ("in2", l), ("out2", l), ("ffn2", l)]

        def piece_weights(seg, l, p):
            if seg == "ffn1":
                return [a["ffn_w1"][0][:, p * FF:(p + 1) * FF], a["ffn_w3"][0][:, p * FF:(p + 1) * FF],
                        a["ffn_w2"][0][p * FF:(p + 1) * FF, :]]
            if seg == "ffn2":
                return [a["w_gate_2"][l][:, p * FF:(p + 1) * FF], a["w_up_2"][l][:, p * FF:(p + 1) * FF],
                        a["w_down_2"][l][p * FF:(p + 1) * FF, :]]
            return [a["exp_w1"][0, p], a["exp_w3"][0, p], a["exp_w2"][0, p]]

        def slot_of():
            n = [0]

            def take():
                n[0] += 1
                return (n[0] - 1) % SLOTS
            return take

        def barrier_of(eng):
            n = [0]

            def come():
                n[0] += 1
                eng.drain()
                eng.sem_inc(S.sem("phase_over"), 1)
                eng.wait_ge(S.sem("phase_over"), 4 * n[0])
            return come

        block = ctx.enter_context(nc.Block())

        @block.sync
        def _(sp):
            take = slot_of()
            order = []

            def load(unit, parts, back=0):
                slot = take()
                if len(order) >= SLOTS:
                    old, old_back = order[-SLOTS]
                    sp.wait_ge(*ready("pe_job", "unit", *old, back=max(old_back, 0)))
                for c0, n, src in parts:
                    k = src.shape[1]
                    if c0 is None:
                        dst = ring[:, slot, 0:k * D].rearrange("p (k c) -> p k c", k=k)
                    else:
                        dst = ring[:, slot, :].rearrange("p (k c) -> p k c", k=KT)[:, :, c0:c0 + n]
                    inc = made("slot%d" % slot, "unit", *unit, by=16)
                    sp.dma_start(dst, src).then_inc(*inc)
                order.append((unit, 0))

            for seg, l in segments:
                if seg in ("ffn1", "ffn2"):
                    for p in range(2):
                        for unit, parts in ffn_units((seg, l, p), *piece_weights(seg, l, p)):
                            load(unit, parts)
                elif seg == "moe":
                    sp.wait_ge(*ready("pe_job", "unit", *order[-1][0]))
                    with S.turns(sp, N_EXP) as e:
                        here = list(ffn_units(("moe", l), a["exp_w1"][0, e], a["exp_w3"][0, e], a["exp_w2"][0, e]))
                        del order[:]
                        order.extend([(unit, 1) for unit, _ in here[-SLOTS:]])
                        for unit, parts in here:
                            load(unit, parts)
                else:
                    for unit, parts in unit_list((seg, l)):
                        load(unit, parts)
            sp.wait_ge(*ready("dve", "x", "end"))
            sp.dma_start(out[0].rearrange("(t p) d -> p t d", p=P), x[:]).then_inc(S.sem("stored"), 16)
            sp.wait_ge(S.sem("stored"), 16)

        @block.gpsimd
        def _(pool):
            barrier = barrier_of(pool)

            def step(ins):
                ins.then_inc(*made("pool"))
                pool.wait_ge(S.sem("pool"), S.count["pool"])

            def fill_where(t, pattern, cm, base, fill, op=ALU.not_equal):
                step(pool.affine_select(out=t, in_=t, compare_op=op, fill=fill, base=base,
                                        pattern=pattern, channel_multiplier=cm))

            for t in (ident, block_ones, eye, level, level0):
                step(pool.memset(t[:], 0.0))
            step(pool.memset(chunk_gate[:], 1.0))
            step(pool.memset(chunk_gate[:, 0:SEQ:CH], 0.0))
            fill_where(ident[:], [[-1, P]], 1, 0, 1.0)
            for i in range(2):
                step(pool.memset(block_ones[HD * i:HD * i + HD, HD * i:HD * i + HD], 1.0))
            step(pool.memset(tri[:], 1.0))
            for p0 in (0, CH):
                ps = slice(p0, p0 + CH)
                fill_where(eye[ps, :], [[-1, CH]], 1, 0, 1.0)
                fill_where(tri[ps, 0, :], [[1, CH]], -1, -1, 0.0, ALU.is_ge)
                fill_where(tri[ps, 1, :], [[1, CH]], -1, 0, 0.0, ALU.is_ge)
                for l in range(6):
                    B = 2 ** l
                    v = level[ps, l, :].rearrange("s (k h j) -> s k h j", h=2, j=B)[:, :, 1, :]
                    step(pool.memset(v, -1.0))
                    fill_where(v, [[-2 * B, CH // (2 * B)], [0, B]], 1, 0, 0.0, ALU.is_ge)
                    fill_where(v, [[2 * B, CH // (2 * B)], [0, B]], -1, B - 1, 0.0, ALU.is_ge)
                fill_where(level0[ps, 0:CH:2], [[-2, CH // 2]], 1, -1, -1.0)
            for i, e in enumerate((LN_EPS, GN_EPS, RMS_EPS, 1e-12)):
                step(pool.memset(eps[:, i:i + 1], e))
            for i in range(ROPE_HALF):
                inv = np.float32(ROPE_THETA) ** (-np.float32(2 * i) / np.float32(2 * ROPE_HALF))
                step(pool.memset(invf[:, i:i + 1], float(np.float32(inv))))
            step(pool.memset(mask[:], NEG))
            step(pool.memset(mask[:, 1, :, :], 0.0))
            for kind in (0, 2):
                for t in range(NT):
                    for half in range(2):
                        c = 2 * t + half
                        lo = max(0, c - 2) * CH if kind == 0 else 0
                        step(pool.memset(mask[HD * half:HD * half + HD, kind, t, lo:(c + 1) * CH], 0.0))
            for t in range(NT):
                fill_where(mask[:, 1, t, :], [[-1, SEQ]], 1, P * t, NEG, ALU.is_ge)
            for _ in range(N_BARRIERS):
                barrier()

        @block.scalar
        def _(act):
            barrier = barrier_of(act)

            def step(ins, *key):
                ins.then_inc(*made("act", *key))

            def dma(dst, src):
                act.dma_start(dst, src).then_inc(*made("param", by=16))

            def load_rows(l, g, b, *key):
                for i, r in enumerate((g, b)):
                    act.dma_start(rows[:, i, :], r.rearrange("(o d) -> o d", o=1).broadcast_to([P, D]))\
                        .then_inc(*made("rows", *key, by=16))

            act.dma_start(x[:], a["x"][0].rearrange("(t p) d -> p t d", p=P)).then_inc(*made("x_in", by=16))
            colmaj = {"mu": "rwkv_mu", "w0": "rwkv_w0", "a0": "rwkv_a0", "k_k": "rwkv_k_k", "k_a": "rwkv_k_a",
                      "gn_g": "rwkv_gn_g", "gn_b": "rwkv_gn_b", "norm_mix": "norm_mix_2",
                      "norm_ffn": "norm_ffn_2", "b_mod": "b_mod_2"}
            with nc.allow_non_contiguous_dma(reason="small parameters, one column per 128 channels"):
                for l in range(DEPTH):
                    for name, n in PARAMS:
                        if name == "r_k":
                            src = a["rwkv_r_k"][l].rearrange("(t h) d -> (h d) t", t=2)
                        elif name == "gate_b":
                            src = a["gate_bias"][l].rearrange("b (t p) -> p (b t)", p=P)
                        else:
                            src = a[colmaj[name]][l].rearrange("(t p) -> p t", p=P)
                        dma(prm(l, name, 0, n), src)
                    dma(lora[0:64, l, 0, :], a["rwkv_w_up"][l])
                    dma(lora[64:128, l, 0, :], a["rwkv_a_up"][l])
                    dma(lora[:, l, 1, :], a["rwkv_g_up"][l])
                    dma(sinks[:, l, :], a["swa_sinks"][l].rearrange("(o d) -> o d", o=1).broadcast_to([P, 8]))
                    dma(fbias[:, l:l + 1], a["fox_f_bias"][l].rearrange("(d o) -> d o", o=1))
                dma(router[:], kview(a["router_w"][0]))
                dma(router_b[:], a["router_b"].broadcast_to([P, N_EXP]))
                dma(cond[:], a["c_2"].rearrange("o (k p) -> p (o k)", p=P))
                dma(pos[:], a["positions_2"].rearrange("o (t p) -> p (o t)", p=P))
            act.wait_ge(S.sem("param"), S.count["param"])
            act.wait_ge(S.sem("x_in"), 16)
            barrier()

            def transposed(tag):
                for j in range(4):
                    act.wait_ge(*ready("pe_job", "xt", *tag, j))
                    step(act.copy(xT[:, 2 * j:2 * j + 2, :], bank_view(tag, j)), "xt", *tag, j)

            def bank_view(tag, j):
                return psum[:, j, :].rearrange("p (a b) -> p a b", a=2)

            def ffn_piece(name, l, p, key, back):
                for s in range(STEPS):
                    n = 256 * min(2, FT - 2 * s)
                    act.wait_ge(*ready("pe_job", "h1", *key, s))
                    if not (p == 0 and s < 2):
                        act.wait_ge(*ready("dve", "g", *(key if s >= 2 else back[0]), (s - 2) % STEPS,
                                           back=0 if s >= 2 else back[1]))
                    step(act.activation(sil[:, s % 2, 0:n], psum[:, (2 * s) % 4, 0:n], ACT.Silu),
                         "silu", *key, s)

            def ffn(seg, l):
                if seg == "moe":
                    with S.turns(act, N_EXP):
                        key = ("moe", l)
                        ffn_piece(seg, l, 1, key, (key, 1))
                else:
                    for p in range(2):
                        ffn_piece(seg, l, p, (seg, l, p), ((seg, l, p - 1), 0))

            def norm_roots(*key):
                act.wait_ge(*ready("dve", "var", *key))
                step(act.activation(sd, mv[:, :, 1], ACT.Sqrt, bias=eps[:, 0:1]), "sd", *key)

            def attention(l, units, Sb, PTb, seg):
                for i, u in enumerate(units):
                    nk = P * (u[2] + 1)
                    b = i % 3
                    act.wait_ge(*ready("dve", "nm", seg, l, u))
                    for h in range(2):
                        step(act.activation(Sb[:, b, h, 0:nk], Sb[:, b, h, 0:nk], ACT.Exp,
                                            bias=nm[:, b, h:h + 1], accum_out=den[:, b, h:h + 1]),
                             "exp", seg, l, u)
                    if u[0] == "swa":
                        for h in range(2):
                            hd = 2 * u[1] + h
                            step(act.activation(es[:, b, h:h + 1], sinks[:, l, hd:hd + 1], ACT.Exp,
                                                bias=nm[:, b, h:h + 1]), "exp", seg, l, u)
                    if i >= 1:
                        v = units[i - 1]
                        turned(v, l, seg, i - 1, PTb)
                turned(units[-1], l, seg, len(units) - 1, PTb)

            def turned(v, l, seg, i, PTb):
                act.wait_ge(*ready("pe_job", "pt", seg, l, v))
                if i >= 2:
                    act.wait_ge(*ready("pe_job", "o", seg, l, units_of(seg)[i - 2]))
                nh = 1 if v[0] == "diff" else 2
                n = v[2] + 1
                bank = psum[:, pt_bank(i), 0:nh * NT * P].rearrange("p (h k q) -> p h k q", h=nh, k=NT)
                step(act.copy(PTb[:, i % 2, 0:nh, 0:n, :], bank[:, :, 0:n, :]), "pt", seg, l, v)

            for l in range(DEPTH):
                load_rows(l, a["ln_g"][l, 0], a["ln_b"][l, 0], "ln1", l)
                transposed(("b1", l))
                for i, dst in ((0, swa_q[:, 0:2, :]), (1, swa_q[:, 2:4, :]), (3, raw[:, 0:2, 1:]),
                               (5, raw[:, 4:6, 1:]), (7, fox_q[:]), (9, fox_v[:]), (10, dsa_q[:])):
                    act.wait_ge(*ready("pe_job", "in", l, i))
                    step(act.copy(dst, psum[:, in_bank(i), :].rearrange("p (a b) -> p a b", a=2)), "in", l, i)
                barrier()
                act.wait_ge(*ready("dve", "mix", l))
                step(act.activation(tanh_w[0:64, :], mix[0:64, 6, :], ACT.Tanh), "tanh", l)
                step(act.activation(mix[:, 7, :], mix[:, 7, :], ACT.Sigmoid), "sig_g", l)
                act.wait_ge(*ready("pe_job", "w_up", l))
                for ct in range(2):
                    step(act.activation(sw[:, ct, :], psum[:, 0, ct * 256:ct * 256 + 256], ACT.Sigmoid,
                                        bias=prm(l, "w0", ct)), "sw", l)
                act.wait_ge(*ready("pe_job", "a_up", l))
                for ct in range(2):
                    step(act.activation(av[:, ct, :], psum[:, 1, ct * 256:ct * 256 + 256], ACT.Sigmoid,
                                        bias=prm(l, "a0", ct)), "a", l)
                act.wait_ge(*ready("pe_job", "g_up", l))
                step(act.copy(gv[:], psum[:, 2, :].rearrange("p (a b) -> p a b", a=2)), "g", l)
                act.wait_ge(*ready("pe_job", "kk", l))
                step(act.activation(sq[:], psum[:, 3, :].rearrange("p (a b) -> p a b", a=2), ACT.Sqrt,
                                    bias=eps[:, 3:4]), "kk_norm", l)
                act.wait_ge(*ready("dve", "decay", l))
                step(act.activation(Wc[:], L[:], ACT.Exp, scale=-DECAY), "W", l)
                step(act.activation(Wi[:], L[:], ACT.Exp, scale=DECAY), "W", l)
                step(act.activation(Wp[:], Wp[:], ACT.Exp, scale=-DECAY), "W", l)
                for i, t in enumerate((tokV, tokB, tokK)):
                    for g in range(2):
                        act.wait_ge(*ready("pe_job", "tok", l, i, g))
                        for odd in range(2):
                            step(act.copy(t[hb(odd), 4 * g:4 * g + 4, :],
                                          psum[0:CH, (3, 7)[g], :].rearrange("p (m o d) -> p m o d", m=4, o=2)
                                          [:, :, odd, :]), "tok", l, i, g)
                for lv in range(1, 6):
                    for g in range(2):
                        act.wait_ge(*ready("pe_job", "U", l, lv, g))
                        step(act.copy(U[:, 4 * g:4 * g + 4, :].rearrange("p m c -> p (m c)"),
                                      psum[:, 4 * g, 0:256]), "U", l, lv, g)
                for c in range(NC):
                    act.wait_ge(*ready("pe_job", "X", l, c))
                    step(act.activation(RS[:, c % 2].rearrange("p h v -> p (h v)"), psum[:, 0, 0:P],
                                        ACT.Copy, scale=-1.0), "RS", l, c)
                    act.wait_ge(*ready("pe_job", "SA", l, c))
                    step(act.copy(SA[:, c % 2].rearrange("p h v -> p (h v)"), psum[:, 1, 0:P]), "SA", l, c)
                    act.wait_ge(*ready("pe_job", "Y", l, c))
                    step(act.copy(yv[:, :, c * CH:(c + 1) * CH],
                                  psum[:, 2, 0:2 * CH].rearrange("p (a b) -> p a b", a=2)), "y", l, c)
                act.wait_ge(*ready("pe_job", "var", l))
                step(act.activation(sq[:], psum[:, 5, :].rearrange("p (a b) -> p a b", a=2), ACT.Sqrt,
                                    bias=eps[:, 1:2], scale=1.0 / HD), "gn", l)
                barrier()
                act.wait_ge(*ready("dve", "fox_abs", l))
                step(act.activation(fox_t[0:4, 1, :], fox_t[0:4, 1, :], ACT.Exp, scale=-1.0), "fox_exp", l)
                act.wait_ge(*ready("act", "fox_exp", l))
                step(act.activation(fox_t[0:4, 1, :], fox_t[0:4, 1, :], ACT.Ln, bias=1.0), "fox_ln", l)
                attention(l, UNITS1, Sm, PT, "b1")
                barrier()
                w = kview(a["w_branch"][l])
                act.dma_start(wb[:, 0:5, :], w[:, 0:5, :]).then_inc(*made("wb", l, by=16))
                act.dma_start(wb[:, 5:10, :], w[:, 5:10, :]).then_inc(*made("wb", l, by=16))
                for cp in range(4):
                    for i in range(2):
                        c = 2 * cp + i
                        for b in range(2):
                            act.wait_ge(*ready("pe_job", "gate", l, c, b))
                            if c >= 2:
                                act.wait_ge(*ready("dve", "prod", l, c - 2))
                            for j in range(2):
                                step(act.activation(sig[:, c % 2, 2 * b + j, :],
                                                    psum[:, 2 * (c % 2) + b, j * 256:j * 256 + 256], ACT.Sigmoid,
                                                    bias=prm(l, "gate_b", (2 * b + j) * KT + c)),
                                     "sig", l, c, b)
                barrier()
                norm_roots("ln1", l)
                barrier()
                load_rows(l, a["ln_g"][l, 1], a["ln_b"][l, 1], "ln2", l)
                transposed(("f1", l))
                if l == 1:
                    act.wait_ge(*ready("dve", "router_gap"))
                    step(act.activation(e2, e2, ACT.Exp), "router_exp")
                ffn("ffn1" if l == 0 else "moe", l)
                norm_roots("ln2", l)
                barrier()

            act.wait_ge(*ready("dve", "angles"))
            step(act.activation(sinb[:].rearrange("p a b -> p (a b)"), ang[:, 1, :], ACT.Sin), "rope")
            step(act.activation(cosb[:].rearrange("p a b -> p (a b)"), ang[:, 2, :], ACT.Sin), "rope")
            step(act.activation(cond[:], cond[:], ACT.Silu), "cond")
            for l in range(DEPTH):
                off = 0
                for name, key in (("moba_q_norm_2", 64), ("moba_k_norm_2", 64), ("diff_q_norm_2", 64),
                                  ("diff_k_norm_2", 64), ("moba_out_norm_2", 64), ("diff_subln_2", 128)):
                    act.dma_start(gains[:, off:off + key],
                                  a[name][l].rearrange("(o d) -> o d", o=1).broadcast_to([P, key]))\
                        .then_inc(*made("gains", l, by=16))
                    off += key
                act.dma_start(gains[:, off:off + 256], a["diff_lambda_2"][l].rearrange("i d -> (i d)")
                              .rearrange("(o d) -> o d", o=1).broadcast_to([P, 256])).then_inc(*made("gains", l, by=16))
                load_rows(l, a["b_mod_2"][l][2 * D:3 * D], a["b_mod_2"][l][5 * D:6 * D], "bmod", l)
                act.wait_ge(*ready("dve", "lam_sums", l))
                step(act.activation(lam[:, 2:4], lam[:, 0:2], ACT.Exp), "lam", l)
                barrier()
                act.wait_ge(*ready("dve", "ms", "mix", l))
                step(act.activation(sd, ss16[:, 0:2], ACT.Sqrt, bias=eps[:, 2:3], scale=1.0 / D), "rms", "mix", l)
                barrier()
                for i in range(12):
                    act.wait_ge(*ready("pe_job", "in2", l, i))
                    bank = psum[:, i % 4, :].rearrange("p (t b) -> p t b", t=2)
                    if i in (4, 5, 10, 11):
                        v0 = {4: 0, 5: 256, 10: 512, 11: 768}[i]
                        step(act.copy(vtm[:, :, v0:v0 + 256], bank), "in2", l, i)
                    else:
                        if QK.index(i) >= 2:
                            act.wait_ge(*ready("dve", "headsum", l, QK[QK.index(i) - 2]))
                        n = QK.index(i) % 2
                        step(act.activation(tsq[:, n, :], psum[:, i % 4, :], ACT.Square), "sq", l, i)
                        act.wait_ge(*ready("dve", "headsum", l, i))
                        step(act.activation(rt16[:, 8 * n:8 * n + 8], ss16[:, 8 * n:8 * n + 8], ACT.Sqrt,
                                            bias=eps[:, 2:3], scale=1.0 / HD), "headroot", l, i)
                        act.wait_ge(*ready("pe_job", "qt", l, i))
                        step(act.copy(qT[:, 2 * QK.index(i):2 * QK.index(i) + 2, :],
                                      psum[:, 4 + n, :].rearrange("p (a b) -> p a b", a=2)), "qt", l, i)
                barrier()
                attention(l, UNITS2, Sm2, PT2, "b2")
                for t in range(NT):
                    act.wait_ge(*ready("dve", "outsum", l, t))
                    step(act.activation(rt16[:, 0:8], ss16[:, 0:8], ACT.Sqrt, bias=eps[:, 2:3], scale=1.0 / HD),
                         "outroot", l, t)
                    step(act.activation(rt16[:, 8:12], ss16[:, 8:12], ACT.Sqrt, bias=eps[:, 2:3],
                                        scale=1.0 / (2 * HD)), "outroot", l, t)
                barrier()
                for j in range(4):
                    act.wait_ge(*ready("pe_job", "xt", "o2", l, j))
                    step(act.copy(oT8[:, 2 * j:2 * j + 2, :], bank_view(None, j)), "xt", "o2", l, j)
                act.wait_ge(*ready("dve", "ms", "ffn", l))
                step(act.activation(sd, ss16[:, 0:2], ACT.Sqrt, bias=eps[:, 2:3], scale=1.0 / D), "rms", "ffn", l)
                barrier()
                ffn("ffn2", l)
                barrier()

        @block.tensor
        def _(pe):
            barrier = barrier_of(pe)
            take = slot_of()
            barrier()

            def job(ins, *key):
                ins.then_inc(*made("pe_job", *key))

            def unit(*key):
                slot = take()
                pe.wait_ge(*ready("slot%d" % slot, "unit", *key))
                return ring[:, slot, :]

            def used(*key):
                S.also("pe_job", "unit", *key)

            def turn(src, tag, wait):
                for j in range(4):
                    if wait is not None:
                        pe.wait_ge(*wait)
                    for i in range(2):
                        for t in range(NT):
                            k = 2 * j + i
                            ins = pe.transpose(psum[:, j, i * 256 + t * P:i * 256 + t * P + P],
                                               src[:, t, k * P:k * P + P], ident[:])
                    job(ins, "xt", *tag, j)

            def channel_tile(dst, w, c0, m, act_t=xT):
                for k in range(KT):
                    ins = pe.matmul(dst, w[:, k * 256 + c0:k * 256 + c0 + m], act_t[:, k, :],
                                    start=(k == 0), stop=(k == KT - 1))
                return ins

            def token_tile(dst, w, c0, n, t, act_t=xT):
                for k in range(KT):
                    ins = pe.matmul(dst, act_t[:, k, t * P:t * P + P], w[:, k * 256 + c0:k * 256 + c0 + n],
                                    start=(k == 0), stop=(k == KT - 1))
                return ins

            def down(key, s, w2):
                n = min(2, FT - 2 * s)
                pe.wait_ge(*ready("dve", "g", *key, s))
                for f in range(n):
                    for t in range(NT):
                        for h in range(2):
                            ins = pe.matmul(psum[:, 4 + 2 * t + h, :],
                                            gT[:, s % 3, f * 256 + t * P:f * 256 + t * P + P],
                                            w2[:, f * D + h * 512:f * D + h * 512 + 512],
                                            start=(s == 0 and f == 0), stop=(s == STEPS - 1 and f == n - 1))
                job(ins, "down", *key, s)
                used(key, "w2", s)

            def ffn_piece(key, p, back):
                w2 = None
                for s in range(STEPS):
                    n = min(2, FT - 2 * s)
                    for i, (w, what, eng) in enumerate((("w1", "silu", "act"), ("w3", "g", "dve"))):
                        b = (2 * s + i) % 4
                        if s >= 2:
                            pe.wait_ge(*ready(eng, what, *key, s - 2))
                        elif p > 0:
                            pe.wait_ge(*ready(eng, what, *back[0], s + STEPS - 2, back=back[1]))
                        wt = unit(key, w, s)
                        for f in range(n):
                            ins = channel_tile(psum[:, b, f * 256:f * 256 + 256], wt, f * P, P)
                        job(ins, "h1" if i == 0 else "h3", *key, s)
                        used(key, w, s)
                    if s == 1 and p > 0:
                        pe.wait_ge(*ready("dve", "acc", *back[0], back=back[1]))
                    if s >= 1:
                        down(key, s - 1, w2)
                    w2 = unit(key, "w2", s)
                down(key, STEPS - 1, w2)

            def ffn(seg, l):
                if seg == "moe":
                    key = ("moe", l)
                    with S.turns(pe, N_EXP):
                        ffn_piece(key, 1, (key, 1))
                else:
                    for p in range(2):
                        ffn_piece((seg, l, p), p, ((seg, l, p - 1), 0))

            def out_rows(kind, l, src):
                for k2 in range(4):
                    w = unit(kind, l, k2)
                    for i in range(2):
                        k = 2 * k2 + i
                        for t in range(NT):
                            for h in range(2):
                                ins = pe.matmul(psum[:, 4 + 2 * t + h, :], src[:, k, t * P:t * P + P],
                                                w[:, i * D + h * 512:i * D + h * 512 + 512],
                                                start=(k == 0), stop=(k == KT - 1))
                    job(ins, kind, l, k2)
                    used(kind, l, k2)

            def scores(l, seg, i, u):
                kind, hp, qt = u
                nk = P * (qt + 1)
                if i >= 2:
                    pe.wait_ge(*ready("dve", "sm", seg, l, units_of(seg)[i - 2]))
                for h in range(2):
                    hd = 2 * hp + h
                    q, k = qk_of(kind, hp)
                    dst = psum[:, 2 * (i % 2) + h, 0:nk]
                    ins = pe.matmul(dst, q[hb(h), qt * P:qt * P + P], k[hb(h), 0:nk],
                                    start=True, stop=(kind != "fox"))
                    if kind == "fox":
                        four = slice(HD * h, HD * h + 4)
                        pe.matmul(dst, select[four, 1, hd, 0:P], fox_t[four, 3, 0:nk], start=False, stop=False)
                        ins = pe.matmul(dst, fox_t[four, 3, qt * P:qt * P + P], select[four, 0, hd, 0:nk],
                                        start=False, stop=True)
                job(ins, "s", seg, l, u)

            def qk_of(kind, hp):
                if kind == "swa":
                    return swa_q[:, hp, :], swa_k[:, hp // 2, :]
                if kind == "fox":
                    return fox_q[:, hp, :], fox_k[:, hp, :]
                if kind == "dsa":
                    return dsa_q[:, hp, :], dsa_k
                if kind == "moba":
                    return qT[:, hp, :], qT[:, 4 + hp, :]
                return qT[:, 8 + hp, :], qT[:, 12 + hp, :]

            def v_of(kind, hp, h, k):
                hd = 2 * hp + h
                if kind == "swa":
                    g = hp // 2
                    return swa_v[:, k, g * HD:g * HD + HD]
                if kind == "fox":
                    return fox_v[:, k, hd * HD:hd * HD + HD]
                if kind == "dsa":
                    return dsa_v[:, k, :]
                if kind == "moba":
                    return vtm[:, k, hd * HD:hd * HD + HD]
                return vtm[:, k, 512 + hp * P:512 + hp * P + P]

            def turn_probs(l, seg, i, u, Sb):
                kind, hp, qt = u
                pe.wait_ge(*ready("dve", "p", seg, l, u))
                if i >= 2:
                    pe.wait_ge(*ready("act", "pt", seg, l, units_of(seg)[i - 2]))
                for h in range(1 if kind == "diff" else 2):
                    for k in range(qt + 1):
                        o = (h * NT + k) * P
                        ins = pe.transpose(psum[:, pt_bank(i), o:o + P], Sb[:, i % 3, h, k * P:k * P + P], ident[:])
                job(ins, "pt", seg, l, u)

            def weigh(l, seg, i, u, PTb):
                kind, hp, qt = u
                pe.wait_ge(*ready("act", "pt", seg, l, u))
                if i >= 2:
                    pe.wait_ge(*ready("dve", "o", seg, l, units_of(seg)[i - 2]))
                b = 6 + i % 2
                for h in range(1 if kind == "diff" else 2):
                    for k in range(qt + 1):
                        probs = PTb[:, i % 2, h, k, :]
                        if seg == "b1":
                            ins = pe.matmul(psum[hb(h), b, 0:P], v_of(kind, hp, h, k), probs,
                                            start=(k == 0), stop=(k == qt))
                        else:
                            n = P if kind == "diff" else HD
                            ins = pe.matmul(psum[:, b, h * HD:h * HD + n], probs, v_of(kind, hp, h, k),
                                            start=(k == 0), stop=(k == qt))
                job(ins, "o", seg, l, u)

            def attention(l, seg, Sb, PTb):
                units = units_of(seg)
                n = len(units)
                for i in range(n + 2):
                    if i < n:
                        if units[i] == ("fox", 0, 0):
                            pe.wait_ge(*ready("dve", "fox_c", l))
                        scores(l, seg, i, units[i])
                    if 1 <= i < n + 1:
                        turn_probs(l, seg, i - 1, units[i - 1], Sb)
                    if i >= 2:
                        weigh(l, seg, i - 2, units[i - 2], PTb)

            def turn_qk(l, i):
                n = QK.index(i)
                pe.wait_ge(*ready("dve", "roped", l, i))
                if n >= 2:
                    pe.wait_ge(*ready("act", "qt", l, QK[n - 2]))
                for ct in range(2):
                    for t in range(NT):
                        ins = pe.transpose(psum[:, 4 + n % 2, ct * 256 + t * P:ct * 256 + t * P + P],
                                           tq[:, n % 2, t * 256 + ct * P:t * 256 + ct * P + P], ident[:])
                job(ins, "qt", l, i)

            for l in range(DEPTH):
                turn(x, ("b1", l), None)
                for i in range(13):
                    b = in_bank(i)
                    if i >= 4 and i < 8:
                        pe.wait_ge(*ready("act", "xt", "b1", l, i - 4))
                    elif i >= 8:
                        pe.wait_ge(*in_copied(ready, l, i - 8))
                    if i == 0:
                        pe.wait_ge(*ready("act", "xt", "b1", l, 3))
                    w = unit("in", l, i)
                    if i == 2:
                        channel_tile(psum[:, b, 0:256], w, 0, P)
                        for t in range(NT):
                            ins = token_tile(psum[:, b, 256 + t * P:256 + t * P + P], w, P, P, t)
                    elif i == 9:
                        for t in range(NT):
                            ins = token_tile(psum[:, b, t * 256:t * 256 + 256], w, 0, 256, t)
                    elif i == 11:
                        channel_tile(psum[0:HD, b, 0:256], w, 0, HD)
                        ins = channel_tile(psum[0:HD, b, 256:512], w, 128, HD)
                        job(ins, "in", l, i)
                        pe.wait_ge(*in_copied(ready, l, 5))
                        b = 1
                        for t in range(NT):
                            token_tile(psum[:, b, t * HD:t * HD + HD], w, HD, HD, t)
                            token_tile(psum[:, b, 128 + t * 4:128 + t * 4 + 4], w, 192, 4, t)
                        ins = channel_tile(psum[0:4, b, 256:512], w, 196, 4)
                        job(ins, "in", l, 13)
                        used("in", l, i)
                        continue
                    else:
                        for j in range(2):
                            ins = channel_tile(psum[:, b, j * 256:j * 256 + 256], w, j * P, P)
                    job(ins, "in", l, i)
                    used("in", l, i)
                barrier()

                pe.wait_ge(*ready("act", "tanh", l))
                for ct in range(2):
                    ins = pe.matmul(psum[:, 0, ct * 256:ct * 256 + 256], lora[0:64, l, 0, ct * P:ct * P + P],
                                    tanh_w[0:64, :], start=True, stop=True)
                job(ins, "w_up", l)
                for ct in range(2):
                    ins = pe.matmul(psum[:, 1, ct * 256:ct * 256 + 256], lora[64:128, l, 0, ct * P:ct * P + P],
                                    mix[64:128, 6, :], start=True, stop=True)
                job(ins, "a_up", l)
                pe.wait_ge(*ready("act", "sig_g", l))
                for ct in range(2):
                    ins = pe.matmul(psum[:, 2, ct * 256:ct * 256 + 256], lora[:, l, 1, ct * P:ct * P + P],
                                    mix[:, 7, :], start=True, stop=True)
                job(ins, "g_up", l)
                pe.wait_ge(*ready("dve", "kk_sq", l))
                ins = pe.matmul(psum[:, 3, :], block_ones[:], sq[:], start=True, stop=True)
                job(ins, "kk", l)
                pe.wait_ge(*ready("dve", "rkr", l))
                ins = pe.matmul(psum[:, 4, :], block_ones[:], yn[:], start=True, stop=True)
                job(ins, "bonus", l)

                def token_copy(i, g):
                    src = (mix[:, 4:6, :], Bh[:], kh[:])[i]
                    if i > 0:
                        pe.wait_ge(*ready("act", "tok", l, i - 1, g))
                    elif g == 0:
                        pe.wait_ge(*ready("act", "kk_norm", l))
                    for cc in range(2):
                        for ct in range(2):
                            c = 2 * g + cc
                            ins = pe.transpose(psum[0:CH, (3, 7)[g], cc * 256 + ct * P:cc * 256 + ct * P + P],
                                               src[:, ct, c * CH:(c + 1) * CH], ident[:])
                    job(ins, "tok", l, i, g)

                for g in range(2):
                    token_copy(0, g)
                pe.wait_ge(*ready("dve", "scaled", l))
                for i in (1, 2):
                    for g in range(2):
                        token_copy(i, g)
                pe.wait_ge(*ready("dve", "bonus", l))
                pe.wait_ge(*ready("act", "a", l))
                pe.wait_ge(*ready("act", "g", l))
                for c in range(NC):
                    b = (0, 1, 4, 5)[c]
                    for h in range(4):
                        ct, s_ = h // 2, slice(c * CH, (c + 1) * CH)
                        kr = KR[hb(h), ct, c, :, :]
                        pe.matmul(psum[hb(h), b, ct * P:ct * P + P], Bh[hb(h), ct, s_], kr, start=True, stop=True)
                        pe.matmul(psum[hb(h), b, 256 + ct * P:256 + ct * P + P], kh[hb(h), ct, s_], kr,
                                  start=True, stop=True)
                        m = 2 * c + ct
                        ins = pe.matmul(psum[hb(h), 2, m * CH:m * CH + CH], KR[hb(h), ct, c, 0, :],
                                        Bh[hb(h), ct, s_], start=True, stop=True)
                    job(ins, "gram", l, c)
                pe.wait_ge(*ready("act", "tok", l, 2, 1))
                for lv in range(1, 6):
                    for g in range(2):
                        pe.wait_ge(*(ready("dve", "BT", l) if lv == 1 else ready("dve", "T", l, lv - 1, g)))
                        for m in range(4 * g, 4 * g + 4):
                            for odd in range(2):
                                o = (m % 4) * CH
                                ins = pe.matmul(psum[hb(odd), 4 * g, o:o + CH], BT[hb(odd), lv - 1, m, :],
                                                T[hb(odd), m, :], start=True, stop=True)
                        job(ins, "U", l, lv, g)
                    for g in range(2):
                        pe.wait_ge(*ready("act", "U", l, lv, g))
                        for m in range(4 * g, 4 * g + 4):
                            for odd in range(2):
                                o = (m % 4) * CH
                                pe.matmul(psum[hb(odd), 4 * g + 1, o:o + CH], TT[hb(odd), m, :], U[hb(odd), m, :],
                                          start=True, stop=True)
                                ins = pe.matmul(psum[hb(odd), 4 * g + 1, 256 + o:256 + o + CH], U[hb(odd), m, :],
                                                TT[hb(odd), m, :], start=True, stop=True)
                        job(ins, "TUT", l, lv, g)
                for c in range(NC):
                    z = (c + 1) % 2
                    if c == 0:
                        pe.wait_ge(*ready("dve", "T", l, 5, 0))
                        pe.wait_ge(*ready("dve", "T", l, 5, 1))
                    else:
                        pe.wait_ge(*ready("dve", "Z", l, c - 1))
                    for h in range(4):
                        ct, r_ = h // 2, hb(h)
                        m, dst = 2 * c + ct, psum[r_, 0, ct * CH:ct * CH + CH]
                        if c > 0:
                            pe.matmul(dst, KR[r_, ct, c, 0, :], Z[r_, z, ct, :], start=True, stop=False)
                        ins = pe.matmul(dst, GR[r_, m, 0, :], tokV[r_, m, :], start=(c == 0), stop=True)
                    job(ins, "X", l, c)
                    pe.wait_ge(*ready("act", "RS", l, c))
                    for h in range(4):
                        ct, r_ = h // 2, hb(h)
                        ins = pe.matmul(psum[r_, 1, ct * CH:ct * CH + CH], TT[r_, 2 * c + ct, :],
                                        RS[r_, c % 2, ct, :], start=True, stop=True)
                    job(ins, "SA", l, c)
                    pe.wait_ge(*ready("act", "SA", l, c))
                    if c < NC - 1:
                        for h in range(4):
                            ct, r_ = h // 2, hb(h)
                            m, dst = 2 * c + ct, psum[r_, 3, ct * CH:ct * CH + CH]
                            pe.matmul(dst, tokB[r_, m, :], SA[r_, c % 2, ct, :], start=True, stop=False)
                            ins = pe.matmul(dst, tokK[r_, m, :], tokV[r_, m, :], start=False, stop=True)
                        job(ins, "Znew", l, c)
                    if c >= 1:
                        pe.wait_ge(*ready("act", "y", l, c - 1))
                    for h in range(4):
                        ct, r_ = h // 2, hb(h)
                        m, dst = 2 * c + ct, psum[r_, 2, ct * CH:ct * CH + CH]
                        if c > 0:
                            pe.matmul(dst, Z[r_, z, ct, :], KR[r_, ct, c, 1, :], start=True, stop=False)
                        pe.matmul(dst, SA[r_, c % 2, ct, :], AB[r_, m, 1, :], start=(c == 0), stop=False)
                        ins = pe.matmul(dst, tokV[r_, m, :], GR[r_, m, 1, :], start=False, stop=True)
                    job(ins, "Y", l, c)
                pe.wait_ge(*ready("act", "y", l, NC - 1))
                ins = pe.matmul(psum[:, 4, :], block_ones[:], yv[:], start=True, stop=True)
                job(ins, "mean", l)
                pe.wait_ge(*ready("dve", "y_sq", l))
                ins = pe.matmul(psum[:, 5, :], block_ones[:], sq[:], start=True, stop=True)
                job(ins, "var", l)
                barrier()

                for qt in range(NT):
                    nk = P * (qt + 1)
                    for h2 in range(2):
                        for h in range(2):
                            ins = pe.matmul(psum[:, 4 + 2 * qt + h, h2 * 256:h2 * 256 + nk],
                                            dsa_qi[hb(h), h2, qt * P:qt * P + P], dsa_ki[hb(h), 0:nk],
                                            start=True, stop=True)
                    job(ins, "idx", l, qt)
                pe.wait_ge(*ready("dve", "pick", l, NT - 1))
                attention(l, "b1", Sm, PT)
                barrier()

                for c in range(KT):
                    cp, i = c // 2, c % 2
                    if i == 0:
                        ws = [unit("gate", l, cp, b) for b in range(4)]
                    for b in range(2):
                        if c >= 2:
                            pe.wait_ge(*ready("act", "sig", l, c - 2, b))
                        for j in range(2):
                            ins = channel_tile(psum[:, 2 * (c % 2) + b, j * 256:j * 256 + 256], ws[2 * b + j], i * P, P)
                        job(ins, "gate", l, c, b)
                        if i == 1:
                            used("gate", l, cp, 2 * b)
                            used("gate", l, cp, 2 * b + 1)
                    if c == 0:
                        pe.wait_ge(*ready("wb", l))
                    if c >= 2:
                        pe.wait_ge(*ready("dve", "prod", l, c - 2))
                    for b in range(4):
                        rows_of = (range(0, 4), range(4, 6), range(6, 8), range(8, 10))[b]
                        dst = psum[:, 4 + 2 * (c % 2) + b // 2, (b % 2) * 256:(b % 2) * 256 + 256]
                        for k in rows_of:
                            ins = pe.matmul(dst, wb[:, k, c * P:c * P + P], oT[:, k, :],
                                            start=(k == rows_of[0]), stop=(k == rows_of[-1]))
                    job(ins, "branch", l, c)
                barrier()
                out_rows("out", l, mergedT)
                barrier()
                turn(x, ("f1", l), None)
                pe.wait_ge(*ready("act", "xt", "f1", l, 3))
                if l == 1:
                    for t in range(NT):
                        for k in range(KT):
                            ins = pe.matmul(psum[:, 4, t * 8:t * 8 + 8], xT[:, k, t * P:t * P + P], router[:, k, :],
                                            start=(k == 0), stop=(k == KT - 1))
                    job(ins, "router")
                    pe.wait_ge(*ready("dve", "router_logits"))
                ffn("ffn1" if l == 0 else "moe", l)
                barrier()

            for l in range(DEPTH):
                pe.wait_ge(*ready("dve", "condb"))
                for i in range(24):
                    w = unit("mod", l, i)
                    part_, j = divmod(i, 4)
                    if part_ in (2, 5):
                        b = 1 + 2 * (part_ // 3) + j // 2
                        for k in range(KT):
                            ins = pe.matmul(psum[:, b, (j % 2) * 256:(j % 2) * 256 + 256], condb[:, k, :],
                                            w[:, k * 256:k * 256 + 256], start=(k == 0), stop=(k == KT - 1))
                    else:
                        col = {0: 0, 1: 8, 3: 16, 4: 24}[part_] + 2 * j
                        for s in range(2):
                            for k in range(KT):
                                ins = pe.matmul(psum[:, 0, col + s:col + s + 1],
                                                w[:, k * 256 + s * P:k * 256 + s * P + P], cond[:, k:k + 1],
                                                start=(k == 0), stop=(k == KT - 1))
                    job(ins, "mod", l, i)
                    used("mod", l, i)
                barrier()
                pe.wait_ge(*ready("dve", "xs", "mix", l))
                turn(tok_scaled, ("mix", l), None)
                barrier()
                for i in range(12):
                    b = i % 4
                    if i >= 4:
                        j = i - 4
                        pe.wait_ge(*(ready("act", "in2", l, j) if j in (4, 5) else ready("dve", "normed", l, j)))
                    w = unit("in2", l, i)
                    for t in range(NT):
                        ins = token_tile(psum[:, b, t * 256:t * 256 + 256], w, 0, 256, t)
                    job(ins, "in2", l, i)
                    used("in2", l, i)
                    if i >= 1 and (i - 1) in QK:
                        turn_qk(l, i - 1)
                barrier()
                attention(l, "b2", Sm2, PT2)
                barrier()
                turn(om, ("o2", l), None)
                pe.wait_ge(*ready("act", "xt", "o2", l, 3))
                out_rows("out2", l, oT8)
                pe.wait_ge(*ready("dve", "xs", "ffn", l))
                turn(tok_scaled, ("ffn", l), None)
                barrier()
                ffn("ffn2", l)
                barrier()

        @block.vector
        def _(dve):
            barrier = barrier_of(dve)

            def step(ins, *key):
                ins.then_inc(*made("dve", *key))
                dve.wait_ge(*here("dve"))

            def here(kind):
                c = S.count[kind]
                if S.turn is None or not known:
                    return S.sem(kind), c
                return S.sem(kind), S.turn * known.per_turn[kind][0] + c

            def free(ins, *key):
                ins.then_inc(*made("dve", *key))

            def two(v):
                return v.rearrange("p (a b) -> p a b", a=2)

            barrier()

            def layer_norm(*key):
                for t in range(NT):
                    for h in range(2):
                        step(dve.bn_stats(stat[:, t, h, :], x[:, t, h * 512:h * 512 + 512]))
                    step(dve.bn_aggr(mv[:, t, :], stat[:, t, :, :].rearrange("p h s -> p (h s)")), "var", *key)
                dve.wait_ge(*ready("act", "sd", *key))
                step(dve.reciprocal(rs, sd))
                dve.wait_ge(*ready("rows", *key))
                for t in range(NT):
                    step(dve.tensor_scalar(x[:, t, :], x[:, t, :], mv[:, t, 0:1], rs[:, t:t + 1],
                                           ALU.subtract, ALU.mult))
                    step(dve.tensor_tensor(x[:, t, :], x[:, t, :], rows[:, 0, :], ALU.mult))
                    step(dve.tensor_tensor(x[:, t, :], x[:, t, :], rows[:, 1, :], ALU.add), "ln", *key)

            def ffn_piece(key, p, back, last):
                for s in range(STEPS):
                    n = 256 * min(2, FT - 2 * s)
                    dve.wait_ge(*ready("act", "silu", *key, s))
                    dve.wait_ge(*ready("pe_job", "h3", *key, s))
                    if s >= 3:
                        dve.wait_ge(*ready("pe_job", "down", *key, s - 3))
                    free(dve.tensor_tensor(gT[:, s % 3, 0:n], sil[:, s % 2, 0:n], psum[:, (2 * s + 1) % 4, 0:n],
                                           ALU.mult), "g", *key, s)
                dve.wait_ge(*ready("pe_job", "down", *key, STEPS - 1))

            def ffn(seg, l):
                if seg == "moe":
                    key = ("moe", l)
                    with S.turns(dve, N_EXP):
                        ffn_piece(key, 1, (key, 1), False)
                        for t in range(NT):
                            step(dve.scalar_tensor_tensor(out=picks[:, t, :], in0=idxf[:, t, 0:2],
                                                          scalar=turn_no, in1=wts[:, t, :], op0=ALU.is_equal,
                                                          op1=ALU.mult))
                            step(dve.tensor_reduce(comb[:, t:t + 1], picks[:, t, :], AX, ALU.add))
                        step(dve.tensor_scalar(turn_no, turn_no, 1.0, None, ALU.add))
                        for t in range(NT):
                            for h in range(2):
                                xs = x[:, t, h * 512:h * 512 + 512]
                                step(dve.scalar_tensor_tensor(out=xs, in0=psum[:, 4 + 2 * t + h, :],
                                                              scalar=comb[:, t:t + 1], in1=xs, op0=ALU.mult,
                                                              op1=ALU.add), "acc", *key)
                else:
                    for p in range(2):
                        key = (seg, l, p)
                        ffn_piece(key, p, None, p == 1)
                        for t in range(NT):
                            for h in range(2):
                                xs = x[:, t, h * 512:h * 512 + 512]
                                ys = psum[:, 4 + 2 * t + h, :]
                                if seg == "ffn1":
                                    step(dve.tensor_tensor(xs, ys, xs, ALU.add), "acc", *key)
                                else:
                                    gs = ys_tmp[:, t, h * 512:h * 512 + 512]
                                    step(dve.tensor_tensor(gs, ys, grow[:, 1, h * 512:h * 512 + 512], ALU.mult))
                                    step(dve.tensor_tensor(xs, gs, xs, ALU.add), "acc", *key)

            def scores_in(l, seg, i, u, Sb):
                kind, hp, qt = u
                nk, b = P * (qt + 1), i % 3
                dve.wait_ge(*ready("pe_job", "s", seg, l, u))
                if i >= 3:
                    dve.wait_ge(*ready("pe_job", "pt", seg, l, units_of(seg)[i - 3]))
                m = dsa_bias[:, qt, :] if kind == "dsa" else mask[:, 0 if kind == "swa" else 1, qt, :]
                s = Sb[:, b, :, 0:nk]
                step(dve.scalar_tensor_tensor(out=s, in0=psum[:, 2 * (i % 2):2 * (i % 2) + 2, 0:nk], scalar=SCALE,
                                              in1=m[:, 0:nk].unsqueeze(1).broadcast_to([P, 2, nk]),
                                              op0=ALU.mult, op1=ALU.add), "sm", seg, l, u)
                step(dve.tensor_reduce(mx[:, b, :], s, AX, ALU.max))
                if kind == "swa":
                    step(dve.tensor_tensor(mx[:, b, :], mx[:, b, :], sinks[:, l, 2 * hp:2 * hp + 2], ALU.max))
                step(dve.tensor_scalar(nm[:, b, :], mx[:, b, :], -1.0, None, ALU.mult), "nm", seg, l, u)

            def probs(l, seg, i, u, Sb):
                kind, hp, qt = u
                nk, b = P * (qt + 1), i % 3
                dve.wait_ge(*ready("act", "exp", seg, l, u))
                if kind == "swa":
                    step(dve.tensor_tensor(den[:, b, :], den[:, b, :], es[:, b, :], ALU.add))
                step(dve.reciprocal(rc[:, b, :], den[:, b, :]))
                s = Sb[:, b, :, 0:nk]
                if kind == "diff":
                    step(dve.tensor_scalar(rc[:, b, 1:2], rc[:, b, 1:2], lam[:, 5:6], None, ALU.mult))
                    step(dve.tensor_scalar(s[:, 1, :], s[:, 1, :], rc[:, b, 1:2], None, ALU.mult))
                    step(dve.scalar_tensor_tensor(out=s[:, 0, :], in0=s[:, 0, :], scalar=rc[:, b, 0:1],
                                                  in1=s[:, 1, :], op0=ALU.mult, op1=ALU.add), "p", seg, l, u)
                else:
                    step(dve.tensor_tensor(s, s, rc[:, b, :].unsqueeze(2).broadcast_to([P, 2, nk]), ALU.mult),
                         "p", seg, l, u)

            def outs(l, seg, i, u):
                kind, hp, qt = u
                dve.wait_ge(*ready("pe_job", "o", seg, l, u))
                bank = psum[:, 6 + i % 2, 0:P]
                if seg == "b1":
                    tile = {"swa": 0, "fox": 6, "dsa": 8}[kind] + hp
                    free(dve.tensor_copy(oT[:, tile, qt * P:qt * P + P], bank), "o", seg, l, u)
                else:
                    c0 = (0 if kind == "moba" else 512) + hp * P
                    step(dve.tensor_copy(om[:, qt, c0:c0 + P], bank), "o", seg, l, u)

            def attention(l, seg, Sb):
                units = units_of(seg)
                n = len(units)
                for i in range(n + 3):
                    if i < n:
                        scores_in(l, seg, i, units[i], Sb)
                    if 1 <= i < n + 1:
                        probs(l, seg, i - 1, units[i - 1], Sb)
                    if i >= 3:
                        outs(l, seg, i - 3, units[i - 3])

            for l in range(DEPTH):
                step(dve.memset(raw[:, :, 0:1], 0.0))
                for i in (2, 4, 6, 8, 11, 12, 13):
                    b = in_bank(i)
                    dve.wait_ge(*ready("pe_job", "in", l, i))
                    bank = psum[:, b, :]
                    if i == 2:
                        for g in range(2):
                            for h in range(2):
                                free(dve.tensor_copy(swa_k[hb(h), g, :], psum[hb(g), b, 0:256]))
                        free(dve.tensor_copy(swa_v[:], two(psum[:, b, 256:512])), "in", l, i)
                    elif i in (4, 6):
                        r0 = {4: 2, 6: 6}[i]
                        step(dve.tensor_copy(raw[:, r0:r0 + 2, 1:], two(bank)), "in", l, i)
                    elif i == 8:
                        free(dve.tensor_copy(fox_k[:], two(bank)), "in", l, i)
                    elif i == 11:
                        for h in range(2):
                            free(dve.tensor_copy(dsa_k[hb(h), :], psum[0:HD, b, 0:256]))
                            free(dve.tensor_copy(dsa_ki[hb(h), :], psum[0:HD, b, 256:512]), "in", l, i)
                    elif i == 12:
                        free(dve.tensor_copy(dsa_qi[:], two(bank)), "in", l, i)
                    else:
                        free(dve.tensor_copy(dsa_v[:], two(psum[:, b, 0:128])))
                        free(dve.tensor_scalar(dsa_wi[:], two(psum[:, b, 128:136]), SCALE * 0.5, None, ALU.mult))
                        free(dve.tensor_copy(fox_f[:, 0, :], psum[0:4, b, 256:512]), "in", l, i)
                barrier()
                step(dve.tensor_tensor(mix[:], raw[:, :, 0:SEQ], raw[:, :, 1:], ALU.subtract))
                for i in range(8):
                    step(dve.scalar_tensor_tensor(out=mix[:, i, :], in0=mix[:, i, :], scalar=prm(l, "mu", i),
                                                  in1=raw[:, i, 1:], op0=ALU.mult, op1=ALU.add), "mix", l)
                r, k, v = mix[:, 0:2, :], mix[:, 2:4, :], mix[:, 4:6, :]
                for ct in range(2):
                    step(dve.tensor_scalar(kk[:, ct, :], k[:, ct, :], prm(l, "k_k", ct), None, ALU.mult))
                step(dve.tensor_tensor(sq[:], kk[:], kk[:], ALU.mult), "kk_sq", l)
                dve.wait_ge(*ready("act", "sw", l))
                for ct in range(2):
                    step(dve.tensor_tensor_scan(L[:, ct, :], chunk_gate[:], sw[:, ct, :], 0.0, ALU.mult, ALU.add))
                step(dve.tensor_tensor(Wp[:], L[:], sw[:], ALU.subtract), "decay", l)
                dve.wait_ge(*ready("act", "a", l))
                for ct in range(2):
                    step(dve.tensor_scalar(kp[:, ct, :], av[:, ct, :], -1.0, prm(l, "k_a", ct), ALU.add, ALU.mult))
                step(dve.scalar_tensor_tensor(out=kp[:], in0=kp[:], scalar=1.0, in1=k, op0=ALU.add, op1=ALU.mult))
                step(dve.tensor_tensor(yn[:], r, kp[:], ALU.mult))
                for ct in range(2):
                    step(dve.tensor_scalar(yn[:, ct, :], yn[:, ct, :], prm(l, "r_k", ct), None, ALU.mult), "rkr", l)
                dve.wait_ge(*ready("act", "kk_norm", l))
                step(dve.reciprocal(sq[:], sq[:]))
                step(dve.tensor_tensor(kk[:], kk[:], sq[:], ALU.mult))
                dve.wait_ge(*ready("act", "W", l))

                def chunks(t):
                    return t.rearrange("p a (c s) -> p a c s", c=NC)
                for ct in range(2):
                    def ch(t):
                        return t[:, ct, :].rearrange("p (c s) -> p c s", c=NC)
                    step(dve.tensor_tensor(KR[:, ct, :, 0, :], ch(kk), ch(Wp), ALU.mult))
                    step(dve.tensor_tensor(KR[:, ct, :, 1, :], ch(mix[:, 0:2, :]), ch(Wc), ALU.mult))
                step(dve.tensor_tensor(Bh[:], kk[:], av[:], ALU.mult))
                step(dve.tensor_tensor(Bh[:], Bh[:], Wi[:], ALU.mult))
                step(dve.tensor_tensor(kh[:], kp[:], Wi[:], ALU.mult), "scaled", l)
                dve.wait_ge(*ready("pe_job", "bonus", l))
                step(dve.tensor_tensor(kp[:], two(psum[:, 4, :]), v, ALU.mult), "bonus", l)
                both = tri[:].rearrange("p a b -> p (a b)").unsqueeze(1).broadcast_to([P, 2, P])
                for c in range(NC):
                    dve.wait_ge(*ready("pe_job", "gram", l, c))
                    for i, dst in enumerate((AB, GR)):
                        free(dve.tensor_tensor(dst[:, 2 * c:2 * c + 2].rearrange("p m a b -> p m (a b)"),
                                               two(psum[:, (0, 1, 4, 5)[c], 256 * i:256 * i + 256]), both, ALU.mult))

                def over(m):
                    return m.unsqueeze(1).broadcast_to([P, 2 * NC, CH])
                step(dve.tensor_tensor(T[:], psum[:, 2, :].rearrange("p (m n) -> p m n", m=2 * NC), over(level0[:]),
                                       ALU.mult))
                step(dve.tensor_tensor(T[:], T[:], over(eye[:]), ALU.add))
                step(dve.tensor_tensor(TT[:], AB[:, :, 0, :], over(level[:, 0, :]), ALU.mult))
                step(dve.tensor_tensor(TT[:], TT[:], over(eye[:]), ALU.add))
                for lv in range(1, 6):
                    step(dve.tensor_tensor(BT[:, lv - 1], AB[:, :, 0, :], over(level[:, lv, :]), ALU.mult), "BT", l)
                for lv in range(1, 6):
                    for g in range(2):
                        dve.wait_ge(*ready("pe_job", "TUT", l, lv, g))
                        for i, t in enumerate((T, TT)):
                            tg = t[:, 4 * g:4 * g + 4, :].rearrange("p m c -> p (m c)")
                            free(dve.tensor_tensor(tg, tg, psum[:, 4 * g + 1, 256 * i:256 * i + 256], ALU.add),
                                 "T", l, lv, g)
                for c in range(NC - 1):
                    z = c % 2
                    dve.wait_ge(*ready("pe_job", "Znew", l, c))
                    new = two(psum[:, 3, 0:2 * CH])
                    if c > 0:
                        step(dve.tensor_tensor(Z[:, z], new, Z[:, 1 - z], ALU.add))
                        new = Z[:, z]
                    for ct in range(2):
                        e = c * CH + CH - 1
                        step(dve.tensor_scalar(Z[:, z, ct, :], new[:, ct, :], Wc[:, ct, e:e + 1], None, ALU.mult),
                             "Z", l, c)
                dve.wait_ge(*ready("pe_job", "mean", l))
                step(dve.scalar_tensor_tensor(out=yv[:], in0=two(psum[:, 4, :]), scalar=-1.0 / HD, in1=yv[:],
                                              op0=ALU.mult, op1=ALU.add))
                step(dve.tensor_tensor(sq[:], yv[:], yv[:], ALU.mult), "y_sq", l)
                dve.wait_ge(*ready("act", "gn", l))
                step(dve.reciprocal(sq[:], sq[:]))
                step(dve.tensor_tensor(yv[:], yv[:], sq[:], ALU.mult))
                for ct in range(2):
                    step(dve.tensor_scalar(yv[:, ct, :], yv[:, ct, :], prm(l, "gn_g", ct), prm(l, "gn_b", ct),
                                           ALU.mult, ALU.add))
                step(dve.tensor_tensor(yv[:], yv[:], kp[:], ALU.add))
                step(dve.tensor_tensor(oT[:, 4:6, :], yv[:], gv[:], ALU.mult))
                barrier()

                low = slice(0, 4)
                step(dve.tensor_scalar(fox_t[low, 0, :], fox_f[:, 0, :], fbias[:, l:l + 1], None, ALU.add))
                step(dve.tensor_scalar(fox_t[low, 2, :], fox_t[low, 0, :], -1.0, None, ALU.mult))
                step(dve.tensor_tensor(fox_t[low, 1, :], fox_t[low, 0, :], fox_t[low, 2, :], ALU.max), "fox_abs", l)
                step(dve.tensor_scalar(fox_t[low, 0, :], fox_t[low, 0, :], 0.0, None, ALU.min))
                for h in range(4):
                    for i, val in enumerate((1.0 / SCALE, -1.0 / SCALE)):
                        for p0 in (0, HD):
                            step(dve.tensor_scalar(select[p0:p0 + 4, i, h, :],
                                                   ident[p0:p0 + 4, p0 + h:p0 + h + 1].broadcast_to([4, SEQ]), val,
                                                   None, ALU.mult))
                dve.wait_ge(*ready("act", "fox_ln", l))
                step(dve.tensor_tensor(fox_t[low, 0, :], fox_t[low, 0, :], fox_t[low, 1, :], ALU.subtract))
                step(dve.memset(fox_t[low, 2, :], 1.0))
                step(dve.tensor_tensor_scan(fox_t[low, 3, :], fox_t[low, 2, :], fox_t[low, 0, :], 0.0, ALU.mult,
                                            ALU.add))
                step(dve.tensor_copy(fox_t[HD:HD + 4, 3, :], fox_t[low, 3, :]), "fox_c", l)
                for qt in range(NT):
                    nk = P * (qt + 1)
                    dve.wait_ge(*ready("pe_job", "idx", l, qt))
                    for h2 in range(2):
                        for h in range(2):
                            dst = score if h2 + h == 0 else part
                            step(dve.tensor_scalar(dst[:, 0:nk],
                                                   psum[:, 4 + 2 * qt + h, h2 * 256:h2 * 256 + nk], 0.0,
                                                   dsa_wi[:, qt, 2 * h2 + h:2 * h2 + h + 1], ALU.max, ALU.mult),
                                 "pick", l, qt)
                            if h2 + h:
                                step(dve.tensor_tensor(score[:, 0:nk], score[:, 0:nk], part[:, 0:nk], ALU.add))
                    step(dve.tensor_tensor(score[:, 0:nk], score[:, 0:nk], mask[:, 2, qt, 0:nk], ALU.add))
                    src = score[:, 0:nk]
                    for rnd in range(TOPK // 8):
                        step(dve.max(m8, src))
                        step(dve.match_replace(picked[:, rnd % 2, 0:nk], m8, src, TAKEN))
                        src = picked[:, rnd % 2, 0:nk]
                    step(dve.tensor_tensor(part[:, 0:nk], src, score[:, 0:nk], ALU.is_equal))
                    step(dve.tensor_scalar(dsa_bias[:, qt, 0:nk], part[:, 0:nk], NEG, None, ALU.mult))
                attention(l, "b1", Sm)
                barrier()

                for c in range(KT):
                    for b in range(2):
                        dve.wait_ge(*ready("act", "sig", l, c, b))
                    dve.wait_ge(*ready("pe_job", "branch", l, c))
                    for b in range(2):
                        step(dve.tensor_tensor(prod[:, c % 2, b, :],
                                               sig[:, c % 2, 2 * b:2 * b + 2, :].rearrange("p a b -> p (a b)"),
                                               psum[:, 4 + 2 * (c % 2) + b, :], ALU.mult), "prod", l, c)
                    step(dve.tensor_tensor(prod[:, c % 2, 0, :], prod[:, c % 2, 0, :], prod[:, c % 2, 1, :], ALU.add))
                    step(dve.tensor_tensor(mergedT[:, c, :], prod[:, c % 2, 0, 0:256], prod[:, c % 2, 0, 256:512],
                                           ALU.add), "merged", l)
                barrier()
                dve.wait_ge(*ready("pe_job", "out", l, 3))
                for t in range(NT):
                    for h in range(2):
                        xs = x[:, t, h * 512:h * 512 + 512]
                        step(dve.scalar_tensor_tensor(out=xs, in0=xs, scalar=ALPHA, in1=psum[:, 4 + 2 * t + h, :],
                                                      op0=ALU.mult, op1=ALU.add))
                layer_norm("ln1", l)
                barrier()
                dve.wait_ge(*ready("pe_job", "xt", "f1", l, 3))
                for t in range(NT):
                    step(dve.tensor_scalar(x[:, t, :], x[:, t, :], ALPHA, None, ALU.mult))
                if l == 1:
                    dve.wait_ge(*ready("pe_job", "router"))
                    step(dve.tensor_tensor(logit[:], psum[:, 4, 0:16].rearrange("p (t e) -> p t e", t=NT),
                                           router_b[:].unsqueeze(1).broadcast_to([P, NT, N_EXP]), ALU.add),
                         "router_logits")
                    for t in range(NT):
                        step(dve.max(top8[:, t, :], logit[:, t, :]))
                        step(dve.max_index(idx8[:, t, :].bitcast(U32), top8[:, t, :], logit[:, t, :]))
                    step(dve.tensor_copy(idxf[:], idx8.bitcast(U32)))
                    step(dve.tensor_tensor(e2, top8[:, :, 1], top8[:, :, 0], ALU.subtract), "router_gap")
                    dve.wait_ge(*ready("act", "router_exp"))
                    step(dve.tensor_scalar(wts[:, :, 0], e2, 1.0, None, ALU.add))
                    step(dve.reciprocal(wts[:, :, 0], wts[:, :, 0]))
                    step(dve.tensor_tensor(wts[:, :, 1], wts[:, :, 0], e2, ALU.mult))
                    step(dve.memset(turn_no, 0.0))
                ffn("ffn1" if l == 0 else "moe", l)
                layer_norm("ln2", l)
                barrier()

            step(dve.tensor_copy(ang[:, 0, 0:NT], pos[:]))
            for t in range(NT):
                step(dve.tensor_scalar(ang[:, 1, t * 8:t * 8 + 8], invf[:], ang[:, 0, t:t + 1], None, ALU.mult))
            for dst, quarter in ((1, 0.0), (2, 0.25)):
                src = ang[:, 1, :] if dst == 1 else ang[:, 0, :]
                if dst == 1:
                    step(dve.tensor_copy(ang[:, 0, :], ang[:, 1, :]))
                    src = ang[:, 0, :]
                step(dve.tensor_scalar(ang[:, dst, :], src, 1.0 / (2 * math.pi), quarter, ALU.mult, ALU.add))
                step(dve.tensor_copy(angi, ang[:, dst, :]))
                step(dve.tensor_copy(rope[:, 0, 0:16], angi))
                step(dve.tensor_scalar(ang[:, dst, :], rope[:, 0, 0:16], -TWO_PI_A, None, ALU.mult))
                step(dve.tensor_tensor(ang[:, dst, :], ang[:, dst, :], src, ALU.add))
                for cst in (TWO_PI_B, TWO_PI_C):
                    step(dve.scalar_tensor_tensor(out=ang[:, dst, :], in0=rope[:, 0, 0:16], scalar=-cst,
                                                  in1=ang[:, dst, :], op0=ALU.mult, op1=ALU.add))
                if dst == 2:
                    step(dve.tensor_scalar(ang[:, dst, :], ang[:, dst, :], math.pi / 2, None, ALU.add))
                step(dve.tensor_scalar(rope[:, 1, 0:16], ang[:, dst, :], math.pi, -2 * math.pi, ALU.is_gt, ALU.mult))
                step(dve.tensor_tensor(ang[:, dst, :], ang[:, dst, :], rope[:, 1, 0:16], ALU.add))
                step(dve.tensor_scalar(rope[:, 1, 0:16], ang[:, dst, :], -math.pi, 2 * math.pi, ALU.is_lt, ALU.mult))
                step(dve.tensor_tensor(ang[:, dst, :], ang[:, dst, :], rope[:, 1, 0:16], ALU.add))
                step(dve.tensor_scalar(ang[:, dst, :], ang[:, dst, :], PI_IN, -PI_IN, ALU.min, ALU.max), "angles")
            dve.wait_ge(*ready("act", "cond"))
            step(dve.tensor_copy(condb[:], cond[:].unsqueeze(2).broadcast_to([P, KT, P])), "condb")

            def rms_rows(which, l):
                for t in range(NT):
                    step(dve.tensor_tensor(tok_scaled[:, t, :], x[:, t, :], x[:, t, :], ALU.mult))
                    step(dve.tensor_reduce(ss16[:, t:t + 1], tok_scaled[:, t, :], AX, ALU.add), "ms", which, l)
                dve.wait_ge(*ready("act", "rms", which, l))
                step(dve.reciprocal(rs, sd))
                for t in range(NT):
                    step(dve.tensor_scalar(tok_scaled[:, t, :], x[:, t, :], rs[:, t:t + 1], None, ALU.mult),
                         "xs", which, l)

            def modulate(which, l, i):
                for j in range(4):
                    dve.wait_ge(*ready("pe_job", "xt", which, l, j))
                    for s in range(2):
                        k = 2 * j + s
                        free(dve.tensor_scalar(xT[:, k, :], psum[:, j, s * 256:s * 256 + 256], Amod[:, i, k:k + 1],
                                               modT[:, 16 * i + k:16 * i + k + 1], ALU.mult, ALU.add),
                             "modulated", which, l, j)

            for l in range(DEPTH):
                lam_init = 0.8 - 0.6 * math.exp(-0.3 * l)
                dve.wait_ge(*ready("gains", l))
                lp = gain("lambda").rearrange("p (i d) -> p i d", i=4)
                for i in range(2):
                    step(dve.tensor_tensor(lp[:, 2 * i, :], lp[:, 2 * i, :], lp[:, 2 * i + 1, :], ALU.mult))
                    step(dve.tensor_reduce(lam[:, i:i + 1], lp[:, 2 * i, :], AX, ALU.add), "lam_sums", l)
                dve.wait_ge(*ready("act", "lam", l))
                step(dve.tensor_tensor(lam[:, 4:5], lam[:, 3:4], lam[:, 2:3], ALU.subtract))
                step(dve.tensor_scalar(lam[:, 5:6], lam[:, 4:5], -lam_init, None, ALU.add))
                dve.wait_ge(*ready("pe_job", "mod", l, 23))
                for seg_, c0 in ((0, 0), (1, 24)):
                    b0 = poff["b_mod"][0] + c0
                    step(dve.tensor_tensor(modT[:, 16 * seg_:16 * seg_ + 16], psum[:, 0, 16 * seg_:16 * seg_ + 16],
                                           par[:, l, b0:b0 + 16], ALU.add))
                for i, name in enumerate(("norm_mix", "norm_ffn")):
                    step(dve.scalar_tensor_tensor(out=Amod[:, i, :], in0=modT[:, 16 * i + 8:16 * i + 16], scalar=1.0,
                                                  in1=prm(l, name, 0, 8), op0=ALU.add, op1=ALU.mult))
                dve.wait_ge(*ready("rows", "bmod", l))
                for i in range(2):
                    for h in range(2):
                        hs = slice(h * 512, h * 512 + 512)
                        step(dve.tensor_tensor(grow[:, i, hs], psum[:, 1 + 2 * i + h, :], rows[:, i, hs], ALU.add))
                barrier()
                rms_rows("mix", l)
                modulate("mix", l, 0)
                barrier()
                for i in QK:
                    n = QK.index(i)
                    g = gain(("moba_q", "moba_k", "diff_q", "diff_k")[n // 2])
                    b = n % 2
                    q4 = tq[:, b, :].rearrange("p (h d) -> p h d", d=HD)
                    s8, r8, i8 = (v[:, 8 * b:8 * b + 8] for v in (ss16, rt16, ri16))
                    dve.wait_ge(*ready("act", "sq", l, i))
                    step(dve.tensor_reduce(s8, tsq[:, b, :].rearrange("p (h d) -> p h d", d=HD), AX, ALU.add),
                         "headsum", l, i)
                    dve.wait_ge(*ready("act", "headroot", l, i))
                    step(dve.reciprocal(i8, r8))
                    if n >= 2:
                        dve.wait_ge(*ready("pe_job", "qt", l, QK[n - 2]))
                    step(dve.tensor_tensor(q4, psum[:, i % 4, :].rearrange("p (h d) -> p h d", d=HD),
                                           i8.unsqueeze(2).broadcast_to([P, 8, HD]), ALU.mult), "normed", l, i)
                    step(dve.tensor_tensor(q4, q4, g.unsqueeze(1).broadcast_to([P, 8, HD]), ALU.mult))
                    qr = tq[:, b, :].rearrange("p (t h d) -> p t h d", t=NT, d=HD)
                    x1, x2 = qr[:, :, :, 0:8], qr[:, :, :, 8:16]
                    rp = [rope[:, k, :].rearrange("p (t h d) -> p t h d", t=NT, d=ROPE_HALF) for k in range(6)]
                    for t in range(NT):
                        c_, s_ = (v[:, t, :].unsqueeze(1).broadcast_to([P, 4, 8]) for v in (cosb, sinb))
                        step(dve.tensor_tensor(rp[0][:, t], x1[:, t], c_, ALU.mult))
                        step(dve.tensor_tensor(rp[1][:, t], x2[:, t], s_, ALU.mult))
                        step(dve.tensor_tensor(rp[2][:, t], x2[:, t], c_, ALU.mult))
                        step(dve.tensor_tensor(rp[3][:, t], x1[:, t], s_, ALU.mult))
                        step(dve.tensor_tensor(x1[:, t], rp[0][:, t], rp[1][:, t], ALU.subtract))
                        step(dve.tensor_tensor(x2[:, t], rp[2][:, t], rp[3][:, t], ALU.add), "roped", l, i)
                barrier()
                attention(l, "b2", Sm2)
                for t in range(NT):
                    step(dve.tensor_tensor(ys_tmp[:, 0, :], om[:, t, :], om[:, t, :], ALU.mult))
                    step(dve.tensor_reduce(ss16[:, 0:8], ys_tmp[:, 0, 0:512].rearrange("p (h d) -> p h d", d=HD),
                                           AX, ALU.add))
                    step(dve.tensor_reduce(ss16[:, 8:12], ys_tmp[:, 0, 512:1024].rearrange("p (h d) -> p h d", d=P),
                                           AX, ALU.add), "outsum", l, t)
                    dve.wait_ge(*ready("act", "outroot", l, t))
                    step(dve.reciprocal(ri16[:, 0:12], rt16[:, 0:12]))
                    step(dve.tensor_scalar(ri16[:, 8:12], ri16[:, 8:12], 1.0 - lam_init, None, ALU.mult))
                    for c0, nh, d, r0, name in ((0, 8, HD, 0, "moba_out"), (512, 4, P, 8, "diff_sub")):
                        o4 = om[:, t, c0:c0 + 512].rearrange("p (h d) -> p h d", d=d)
                        step(dve.tensor_tensor(o4, o4, ri16[:, r0:r0 + nh].unsqueeze(2).broadcast_to([P, nh, d]),
                                               ALU.mult))
                        step(dve.tensor_tensor(o4, o4, gain(name).unsqueeze(1).broadcast_to([P, nh, d]), ALU.mult))
                barrier()
                dve.wait_ge(*ready("pe_job", "out2", l, 3))
                for t in range(NT):
                    for h in range(2):
                        hs = slice(h * 512, h * 512 + 512)
                        step(dve.tensor_tensor(tok_scaled[:, t, hs], psum[:, 4 + 2 * t + h, :], grow[:, 0, hs],
                                               ALU.mult))
                        step(dve.tensor_tensor(x[:, t, hs], x[:, t, hs], tok_scaled[:, t, hs], ALU.add))
                rms_rows("ffn", l)
                modulate("ffn", l, 1)
                barrier()
                ffn("ffn2", l)
                if l == DEPTH - 1:
                    S.also("dve", "x", "end")
                barrier()

        return S


QK = [0, 1, 2, 3, 6, 7, 8, 9]
UNITS1 = ([("swa", hp, qt) for hp in range(4) for qt in range(NT)]
          + [("fox", hp, qt) for hp in range(2) for qt in range(NT)]
          + [("dsa", hp, qt) for hp in range(2) for qt in range(NT)])
UNITS2 = ([("moba", hp, qt) for hp in range(4) for qt in range(NT)]
          + [("diff", hp, qt) for hp in range(4) for qt in range(NT)])
N_BARRIERS = 1 + DEPTH * 6 + DEPTH * 6


_INS = ["x", "w_in", "swa_sinks", "rwkv_mu", "rwkv_w0", "rwkv_w_up", "rwkv_a0", "rwkv_a_up", "rwkv_g_up",
        "rwkv_k_k", "rwkv_k_a", "rwkv_r_k", "rwkv_gn_g", "rwkv_gn_b", "fox_f_bias", "gate_bias", "w_branch",
        "w_out", "ln_g", "ln_b", "ffn_w1", "ffn_w3", "ffn_w2", "router_w", "router_b", "exp_w1", "exp_w3",
        "exp_w2", "c_2", "positions_2", "w_mod_2", "b_mod_2", "norm_mix_2", "w_in_2", "moba_q_norm_2",
        "moba_k_norm_2", "moba_out_norm_2", "diff_q_norm_2", "diff_k_norm_2", "diff_lambda_2",
        "diff_subln_2", "w_out_2", "norm_ffn_2", "w_gate_2", "w_up_2", "w_down_2"]


def program(arrays, known, bacc):
    nc = bacc.Bacc("TRN2", target_bir_lowering=False, num_devices=1)
    a = {}
    for name in _INS:
        v = arrays["in_" + name]
        a[name] = nc.dram_tensor("in_" + name, v.shape, mybir.dt.from_np(v.dtype), kind="ExternalInput").ap()
    out = nc.dram_tensor("out_0", (1, SEQ, D), F32, kind="ExternalOutput").ap()
    return nc, build(nc, a, out, known)


def kernel(**inputs):
    import concourse.bacc as bacc
    from concourse.bass_utils import run_bass_kernel_spmd as run

    arrays = {"in_" + name: np.ascontiguousarray(inputs[name]) for name in _INS}
    _, known = program(arrays, None, bacc)
    nc, _ = program(arrays, known, bacc)
    r = run(nc, [arrays], core_ids=[0])
    return r.results[0]["out_0"]
```

```python
from contextlib import ExitStack, contextmanager
import math

import numpy as np
import concourse.bass as bass
from concourse import mybir

F32 = mybir.dt.float32
U32 = mybir.dt.uint32
I32 = mybir.dt.int32
ALU = mybir.AluOpType
ACT = mybir.ActivationFunctionType
AX = mybir.AxisListType.X

P = 128
D = 1024
KT = D // P
SEQ = 256
NT = SEQ // P
DEPTH = 2
HD = 64
CH = 64
NC = SEQ // CH
FF = 1408
FT = FF // P
STEPS = (FT + 1) // 2
N_EXP = 8
IN_SWA, IN_RWKV, IN_FOX, IN_DSA, IN_GATE = 0, 768, 1792, 2564, 3272
TOPK = 64
TWO_PI_A = 6.28125
TWO_PI_B = float(np.floor((2 * math.pi - TWO_PI_A) * 2.0 ** 21) / 2.0 ** 21)
TWO_PI_C = 2 * math.pi - TWO_PI_A - TWO_PI_B
PI_IN = 3.1415925
ALPHA = (2 * DEPTH) ** 0.25
LN_EPS = 1e-5
GN_EPS = 64e-5
RMS_EPS = 1e-6
SCALE = HD ** -0.5
DECAY = math.exp(-0.5)
NEG = -1e30
TAKEN = -3e38
ROPE_HALF = 8
ROPE_THETA = 500000.0
SLOTS = 6
SLOT = 2048
UNIT = 256
PACK = 3 * P
KEYS = [(0, P), (P, SEQ)]
MOD_UNITS = 6 * D // UNIT

PARAMS = [("mu", 8), ("w0", 2), ("a0", 2), ("k_k", 2), ("k_a", 2), ("r_k", 2), ("gn_g", 2), ("gn_b", 2),
          ("gate_b", 32), ("norm_mix", 8), ("norm_ffn", 8), ("b_mod", 48)]
GAINS = [("moba_q", 64), ("moba_k", 64), ("diff_q", 64), ("diff_k", 64), ("moba_out", 64), ("diff_sub", 128),
         ("lambda", 256)]


class Signals:

    def __init__(self, nc, ctx, known):
        self.nc, self.ctx = nc, ctx
        self.sems, self.count, self.value, self.per_turn = {}, {}, {}, {}
        self.known = known
        self.turn = None

    def sem(self, kind):
        if kind not in self.sems:
            self.sems[kind] = self.ctx.enter_context(self.nc.semaphore(kind))
        return self.sems[kind]

    def made(self, kind, *key, by=1):
        self.count[kind] = self.count.get(kind, 0) + by
        self.value[(kind, key)] = (self.count[kind], self.turn is not None)
        return self.sem(kind), by

    def also(self, kind, *key):
        self.value[(kind, key)] = (self.count[kind], self.turn is not None)

    def ready(self, kind, *key, back=0):
        value, looped = self.known.value[(kind, key)] if self.known else (1, False)
        if looped:
            step, n = self.known.per_turn[kind]
            if self.turn is not None:
                return self.sem(kind), self.turn * step + (value - back * step)
            return self.sem(kind), value + (n - 1) * step
        return self.sem(kind), value

    @contextmanager
    def turns(self, eng, n):
        before = dict(self.count)
        with eng.Fori(0, n) as turn:
            self.turn = turn
            yield turn
        self.turn = None
        for kind, c in self.count.items():
            step = c - before.get(kind, 0)
            if step:
                self.per_turn[kind] = (step, n)
                self.count[kind] += (n - 1) * step


def build(nc, a, out, known):
    with ExitStack() as ctx:
        S = Signals(nc, ctx, known)
        made, ready = S.made, S.ready

        def sb(name, shape, dt=F32):
            return ctx.enter_context(nc.sbuf_tensor(name, shape, dt))

        ring = sb("ring", [P, SLOTS, SLOT])
        x = sb("x", [P, NT, D])
        xT = sb("xT", [P, KT, SEQ])
        oT = sb("oT", [P, 10, SEQ])
        rows = sb("rows", [P, 2, D])
        par = sb("par", [P, DEPTH, sum(n for _, n in PARAMS)])
        lora = sb("lora", [P, DEPTH, 2, 256])
        sinks = sb("sinks", [P, DEPTH, 8])
        fbias = sb("fbias", [4, DEPTH])
        router = sb("router", [P, KT, N_EXP])
        router_b = sb("router_b", [P, N_EXP])
        cond = sb("cond", [P, KT])
        pos = sb("pos", [P, NT], I32)
        ident = sb("ident", [P, P])
        block_ones = sb("block_ones", [P, P])
        mask = sb("mask", [P, 3, PACK])
        ones = sb("ones", [P, P])
        tri = sb("tri", [P, 2, CH])
        level = sb("level", [P, 6, CH])
        level0 = sb("level0", [P, CH])
        eye = sb("eye", [P, CH])
        chunk_gate = sb("chunk_gate", [P, SEQ])
        eps = sb("eps", [P, 4])
        invf = sb("invf", [P, ROPE_HALF])
        small = sb("small", [P, 256])
        ARENA = 27700
        arena = sb("arena", [P, ARENA])
        psum = ctx.enter_context(nc.psum_tensor("psum", [P, 8, 512], F32))

        top = [0]

        def view(*shape, parts=P, at=None):
            n = int(np.prod(shape))
            o = top[0] if at is None else at
            if at is None:
                top[0] += n
            assert o + n <= ARENA, (o, n)
            v = arena[0:parts, o:o + n]
            names = "abcd"[:len(shape)]
            if len(shape) > 1:
                v = v.rearrange("p (%s) -> p %s" % (" ".join(names), " ".join(names)),
                                **{k: s for k, s in zip(names, shape)})
            return v

        swa_q, swa_k, swa_v = view(4, SEQ), view(2, SEQ), view(NT, P)
        fox_q, fox_k, fox_v = view(2, SEQ), view(2, SEQ), view(NT, 256)
        fox_f = view(1, SEQ, parts=4)
        dsa_q, dsa_k, dsa_qi, dsa_ki = view(2, SEQ), view(SEQ), view(2, SEQ), view(SEQ)
        dsa_v, dsa_wi = view(NT, HD), view(NT, 4)
        branch_end = top[0]
        raw_at = top[0]
        raw = view(8, SEQ + 1)
        AB = view(2 * NC, 2, CH, at=raw_at)
        mix = view(8, SEQ)
        mix_at = raw_at + 8 * (SEQ + 1)
        T, TT = view(2 * NC, CH, at=top[0]), view(2 * NC, CH, at=top[0] + 2 * SEQ)
        Bh, kh = view(2, SEQ), view(2, SEQ)
        U = view(2 * NC, CH, at=top[0])
        kk, sw, L, Wc = [view(2, SEQ) for _ in range(4)]
        BT = [view(2 * NC, CH, at=o) for o in (mix_at, mix_at + 512, top[0], top[0] + 512, top[0] + 1024)]
        Wp, Wi, av, gv, sq, kp = [view(2, SEQ) for _ in range(6)]
        KR = view(2, NC, 2, CH)
        GR = view(2 * NC, 2, CH)
        tanh_w = view(SEQ, at=top[0])
        tokV, tokB, tokK = [view(2 * NC, CH) for _ in range(3)]
        RS, SA = view(2, 2, CH, at=mix_at + 6 * SEQ), view(2, 2, CH, at=mix_at + 7 * SEQ)
        Z = view(2, 2, CH)
        yv, yn = L, sw
        gate_at = ARENA - 4 * KT * SEQ
        assert top[0] <= gate_at, top[0]
        zb = view(4, KT, SEQ, at=gate_at)
        top[0] = branch_end
        fox_t = view(4, SEQ)
        score, picked, part = view(SEQ), view(NT, SEQ), view(SEQ)
        dsa_bias = view(PACK)
        Sm = view(4, 2, PACK)
        PT = view(2, 2, PACK)
        top[0] = 0
        wb = view(10, D)
        prod = view(2, 2, 512)
        mergedT = view(KT, SEQ)
        top[0] = 0
        sil = view(2, 512)
        gT = view(3, 512)
        stat = small[:, 0:24].rearrange("p (t h s) -> p t h s", t=NT, h=2)
        mv = small[:, 24:28].rearrange("p (t s) -> p t s", t=NT)
        sd, rs = small[:, 28:30], small[:, 30:32]
        logit = small[:, 32:48].rearrange("p (t e) -> p t e", t=NT)
        top8 = small[:, 48:64].rearrange("p (t e) -> p t e", t=NT)
        idx8 = small[:, 64:80].rearrange("p (t e) -> p t e", t=NT)
        idxf = small[:, 80:96].rearrange("p (t e) -> p t e", t=NT)
        wts = small[:, 96:100].rearrange("p (t e) -> p t e", t=NT)
        e2, turn_no = small[:, 100:102], small[:, 102:103]
        comb, picks = small[:, 104:106], small[:, 106:110].rearrange("p (t e) -> p t e", t=NT)
        mx, nm, den, es, rc = [small[:, 208 + 8 * i:216 + 8 * i].rearrange("p (b q h) -> p b q h", b=2, q=NT)
                               for i in range(5)]
        m8 = small[:, 144:152]
        ss16, rt16, ri16 = [small[:, 152 + 16 * i:168 + 16 * i] for i in range(3)]
        lam = small[:, 200:208]
        top[0] = 3000
        gains = view(sum(n for _, n in GAINS))
        grow = view(2, D)
        modT, Amod = view(32), view(2, KT)
        cosb, sinb = view(NT, ROPE_HALF), view(NT, ROPE_HALF)
        ang = view(4, NT * ROPE_HALF)
        vtm = view(NT, D)
        qT = view(16, SEQ)
        tq, tsq = view(2, 512), view(2, 512)
        rope = view(6, NT * 4 * ROPE_HALF)
        om = view(NT, D)
        angi = ang[:, 3, :].bitcast(I32)
        Sm2, PT2 = view(4, 2, PACK), view(2, 2, PACK)
        tok_scaled = view(NT, D)
        mod_at = ARENA - 3 * SLOT - MOD_UNITS * UNIT
        modw = view(3, SLOT, at=mod_at)
        pmod = view(MOD_UNITS, UNIT, at=mod_at + 3 * SLOT)
        ys_tmp = tok_scaled
        oT8 = oT[:, 0:8, :]

        def units_of(seg):
            return UNITS1 if seg == "b1" else UNITS2

        def o_bank(seg, i):
            return 6 if seg == "b1" else 6 + i % 2

        def in_bank(i):
            return (4 + i) % 8

        def in_copied(ready, l, i):
            return ready("act" if i in (0, 1, 3, 5, 7, 9, 10) else "dve", "in", l, i)

        poff = {}
        o = 0
        for name, n in PARAMS:
            poff[name] = (o, n)
            o += n
        goff = {}
        o = 0
        for name, n in GAINS:
            goff[name] = (o, n)
            o += n

        def prm(l, name, i=0, n=1):
            return par[:, l, poff[name][0] + i:poff[name][0] + i + n]

        def gain(name):
            return gains[:, goff[name][0]:goff[name][0] + goff[name][1]]

        def kview(w):
            return w.rearrange("(k p) c -> p k c", p=P)

        def hb(h):
            return slice(HD * (h % 2), HD * (h % 2) + HD)

        units1 = ([IN_SWA + UNIT * i for i in range(3)] + [IN_RWKV + UNIT * i for i in range(4)]
                  + [IN_FOX + UNIT * i for i in range(3)] + [IN_DSA, None, IN_DSA + 384])

        def unit_list(segment):
            kind, l = segment
            if kind == "in":
                w = kview(a["w_in"][l])
                for i, c in enumerate(units1):
                    if c is None:
                        yield ("in", l, i), [(0, 128, w[:, :, IN_DSA + 256:IN_DSA + 384]),
                                             (128, 68, w[:, :, IN_DSA + 640:IN_DSA + 708]),
                                             (196, 4, w[:, :, IN_FOX + 768:IN_FOX + 772])]
                    else:
                        yield ("in", l, i), [(0, 256, w[:, :, c:c + 256])]
            elif kind == "gate":
                w = kview(a["w_in"][l])
                for cp in range(4):
                    for b in range(4):
                        c = IN_GATE + b * D + cp * 256
                        yield ("gate", l, cp, b), [(0, 256, w[:, :, c:c + 256])]
            elif kind in ("out", "out2"):
                w = kview(a["w_out" if kind == "out" else "w_out_2"][l])
                for k in range(4):
                    yield (kind, l, k), [(None, D, w[:, 2 * k:2 * k + 2, :])]
            elif kind == "in2":
                w = kview(a["w_in_2"][l])
                for i in range(12):
                    yield ("in2", l, i), [(0, 256, w[:, :, UNIT * i:UNIT * i + 256])]

        def ffn_units(name, w1, w3, w2):
            for s in range(STEPS):
                n = min(2, FT - 2 * s)
                yield (name, "w1", s), [(0, n * P, kview(w1)[:, :, s * 256:s * 256 + n * P])]
                yield (name, "w3", s), [(0, n * P, kview(w3)[:, :, s * 256:s * 256 + n * P])]
                yield (name, "w2", s), [(None, D, kview(w2)[:, 2 * s:2 * s + n, :])]

        segments = []
        for l in range(DEPTH):
            segments += [("in", l), ("gate", l), ("out", l), ("ffn1", l) if l == 0 else ("moe", l)]
        for l in range(DEPTH):
            segments += [("in2", l), ("out2", l), ("ffn2", l)]

        def piece_weights(seg, l, p):
            if seg == "ffn1":
                return [a["ffn_w1"][0][:, p * FF:(p + 1) * FF], a["ffn_w3"][0][:, p * FF:(p + 1) * FF],
                        a["ffn_w2"][0][p * FF:(p + 1) * FF, :]]
            if seg == "ffn2":
                return [a["w_gate_2"][l][:, p * FF:(p + 1) * FF], a["w_up_2"][l][:, p * FF:(p + 1) * FF],
                        a["w_down_2"][l][p * FF:(p + 1) * FF, :]]
            return [a["exp_w1"][0, p], a["exp_w3"][0, p], a["exp_w2"][0, p]]

        def slot_of():
            n = [0]

            def take():
                n[0] += 1
                return (n[0] - 1) % SLOTS
            return take

        def barrier_of(eng):
            n = [0]

            def come():
                n[0] += 1
                eng.drain()
                eng.sem_inc(S.sem("phase_over"), 1)
                eng.wait_ge(S.sem("phase_over"), 4 * n[0])
            return come

        block = ctx.enter_context(nc.Block())

        def gate_place(j):
            return j // 4, j % 4

        @block.sync
        def _(sp):
            take = slot_of()
            order = []

            def load(unit, parts, back=0):
                slot = take()
                if len(order) >= SLOTS:
                    old, old_back = order[-SLOTS]
                    sp.wait_ge(*ready("pe_job", "unit", *old, back=max(old_back, 0)))
                for c0, n, src in parts:
                    k = src.shape[1]
                    if c0 is None:
                        dst = ring[:, slot, 0:k * D].rearrange("p (k c) -> p k c", k=k)
                    else:
                        dst = ring[:, slot, :].rearrange("p (k c) -> p k c", k=KT)[:, :, c0:c0 + n]
                    inc = made("slot%d" % slot, "unit", *unit, by=16)
                    sp.dma_start(dst, src).then_inc(*inc)
                order.append((unit, 0))

            def load_mod(l, first, j):
                sp.wait_ge(*mod_free(l, first, j))
                c = (first + j) * UNIT
                sp.dma_start(modw[:, j % 3, :].rearrange("p (k c) -> p k c", k=KT),
                             kview(a["w_mod_2"][l])[:, :, bass.ds(c, UNIT)]).then_inc(S.sem("modw%d" % (j % 3)), 16)

            def mod_free(l, first, j):
                return S.sem("mod_used"), MOD_UNITS * l + first + j + 1

            for seg, l in segments:
                if seg in ("ffn1", "ffn2"):
                    for p in range(2):
                        for n, (unit, parts) in enumerate(ffn_units((seg, l, p), *piece_weights(seg, l, p))):
                            load(unit, parts)
                            if (seg, l) == ("ffn2", 0) and n % 3 == 2:
                                if p == 0 and n == 2:
                                    sp.wait_ge(*ready("act", "silu", "ffn2", 0, 0, 0))
                                for j in range(2):
                                    load_mod(1, 0, (p * STEPS + n // 3) * 2 + j)
                elif seg == "moe":
                    sp.wait_ge(*ready("pe_job", "unit", *order[-1][0]))
                    with S.turns(sp, N_EXP) as e:
                        here = list(ffn_units(("moe", l), a["exp_w1"][0, e], a["exp_w3"][0, e], a["exp_w2"][0, e]))
                        del order[:]
                        order.extend([(unit, 1) for unit, _ in here[-SLOTS:]])
                        for n, (unit, parts) in enumerate(here):
                            load(unit, parts)
                            if n % 6 == 5:
                                load_mod(0, e * 3, n // 6)
                else:
                    for unit, parts in unit_list((seg, l)):
                        load(unit, parts)
            sp.wait_ge(*ready("dve", "x", "end"))
            sp.dma_start(out[0].rearrange("(t p) d -> p t d", p=P), x[:]).then_inc(S.sem("stored"), 16)
            sp.wait_ge(S.sem("stored"), 16)

        @block.gpsimd
        def _(pool):
            barrier = barrier_of(pool)

            def step(ins):
                ins.then_inc(*made("pool"))
                pool.wait_ge(S.sem("pool"), S.count["pool"])

            def fill_where(t, pattern, cm, base, fill, op=ALU.not_equal):
                step(pool.affine_select(out=t, in_=t, compare_op=op, fill=fill, base=base,
                                        pattern=pattern, channel_multiplier=cm))

            for t in (ident, block_ones, eye, level, level0):
                step(pool.memset(t[:], 0.0))
            step(pool.memset(ones[:], 1.0))
            step(pool.memset(chunk_gate[:], 1.0))
            step(pool.memset(chunk_gate[:, 0:SEQ:CH], 0.0))
            fill_where(ident[:], [[-1, P]], 1, 0, 1.0)
            for i in range(2):
                step(pool.memset(block_ones[HD * i:HD * i + HD, HD * i:HD * i + HD], 1.0))
            step(pool.memset(tri[:], 1.0))
            for p0 in (0, CH):
                ps = slice(p0, p0 + CH)
                fill_where(eye[ps, :], [[-1, CH]], 1, 0, 1.0)
                fill_where(tri[ps, 0, :], [[1, CH]], -1, -1, 0.0, ALU.is_ge)
                fill_where(tri[ps, 1, :], [[1, CH]], -1, 0, 0.0, ALU.is_ge)
                for l in range(6):
                    B = 2 ** l
                    v = level[ps, l, :].rearrange("s (k h j) -> s k h j", h=2, j=B)[:, :, 1, :]
                    step(pool.memset(v, -1.0))
                    fill_where(v, [[-2 * B, CH // (2 * B)], [0, B]], 1, 0, 0.0, ALU.is_ge)
                    fill_where(v, [[2 * B, CH // (2 * B)], [0, B]], -1, B - 1, 0.0, ALU.is_ge)
                fill_where(level0[ps, 0:CH:2], [[-2, CH // 2]], 1, -1, -1.0)
            for i, e in enumerate((LN_EPS, GN_EPS, RMS_EPS, 1e-12)):
                step(pool.memset(eps[:, i:i + 1], e))
            for i in range(ROPE_HALF):
                inv = np.float32(ROPE_THETA) ** (-np.float32(2 * i) / np.float32(2 * ROPE_HALF))
                step(pool.memset(invf[:, i:i + 1], float(np.float32(inv))))
            step(pool.memset(mask[:], NEG))
            step(pool.memset(mask[:, 1, :], 0.0))
            for kind in (0, 2):
                for t in range(NT):
                    for half in range(2):
                        c = 2 * t + half
                        lo = max(0, c - 2) * CH if kind == 0 else 0
                        k0 = KEYS[t][0]
                        step(pool.memset(mask[HD * half:HD * half + HD, kind, k0 + lo:k0 + (c + 1) * CH], 0.0))
            for t in range(NT):
                k0, nk = KEYS[t]
                fill_where(mask[:, 1, k0:k0 + nk], [[-1, nk]], 1, P * t, NEG, ALU.is_ge)
            def modulation(l):
                for j in range(MOD_UNITS):
                    pool.wait_ge(S.sem("modw%d" % (j % 3)), 16 * (MOD_UNITS // 3 * l + j // 3 + 1))
                    w = modw[:, j % 3, :]
                    step(pool.tensor_tensor(w.rearrange("p (k c) -> p k c", k=KT),
                                            w.rearrange("p (k c) -> p k c", k=KT),
                                            cond[:].unsqueeze(2).broadcast_to([P, KT, UNIT]), ALU.mult))
                    step(pool.tensor_tensor(w[:, 0:1024], w[:, 0:1024], w[:, 1024:2048], ALU.add))
                    step(pool.tensor_tensor(w[:, 0:512], w[:, 0:512], w[:, 512:1024], ALU.add))
                    pool.tensor_tensor(pmod[:, j, :], w[:, 0:256], w[:, 256:512], ALU.add)\
                        .then_inc(S.sem("mod_used"), 1)

            pool.sem_inc(S.sem("mod_used"), 3)
            for b in range(N_BARRIERS):
                barrier()
                if b == 2 * 6 - 1:
                    modulation(0)
                if b == 3 * 6 - 1:
                    modulation(1)

        @block.scalar
        def _(act):
            barrier = barrier_of(act)

            def step(ins, *key):
                ins.then_inc(*made("act", *key))

            def dma(dst, src):
                act.dma_start(dst, src).then_inc(*made("param", by=16))

            def load_rows(l, g, b, *key):
                for i, r in enumerate((g, b)):
                    act.dma_start(rows[:, i, :], r.rearrange("(o d) -> o d", o=1).broadcast_to([P, D]))\
                        .then_inc(*made("rows", *key, by=16))

            act.dma_start(x[:], a["x"][0].rearrange("(t p) d -> p t d", p=P)).then_inc(*made("x_in", by=16))
            colmaj = {"mu": "rwkv_mu", "w0": "rwkv_w0", "a0": "rwkv_a0", "k_k": "rwkv_k_k", "k_a": "rwkv_k_a",
                      "gn_g": "rwkv_gn_g", "gn_b": "rwkv_gn_b", "norm_mix": "norm_mix_2",
                      "norm_ffn": "norm_ffn_2", "b_mod": "b_mod_2"}
            with nc.allow_non_contiguous_dma(reason="small parameters, one column per 128 channels"):
                for l in range(DEPTH):
                    for name, n in PARAMS:
                        if name == "r_k":
                            src = a["rwkv_r_k"][l].rearrange("(t h) d -> (h d) t", t=2)
                        elif name == "gate_b":
                            src = a["gate_bias"][l].rearrange("b (t p) -> p (b t)", p=P)
                        else:
                            src = a[colmaj[name]][l].rearrange("(t p) -> p t", p=P)
                        dma(prm(l, name, 0, n), src)
                    dma(lora[0:64, l, 0, :], a["rwkv_w_up"][l])
                    dma(lora[64:128, l, 0, :], a["rwkv_a_up"][l])
                    dma(lora[:, l, 1, :], a["rwkv_g_up"][l])
                    dma(sinks[:, l, :], a["swa_sinks"][l].rearrange("(o d) -> o d", o=1).broadcast_to([P, 8]))
                    dma(fbias[:, l:l + 1], a["fox_f_bias"][l].rearrange("(d o) -> d o", o=1))
                dma(router[:], kview(a["router_w"][0]))
                dma(router_b[:], a["router_b"].broadcast_to([P, N_EXP]))
                dma(cond[:], a["c_2"].rearrange("o (k p) -> p (o k)", p=P))
                dma(pos[:], a["positions_2"].rearrange("o (t p) -> p (o t)", p=P))
            act.wait_ge(S.sem("param"), S.count["param"])
            act.wait_ge(S.sem("x_in"), 16)
            step(act.activation(cond[:], cond[:], ACT.Silu), "cond")
            barrier()

            def transposed(tag):
                for j in range(4):
                    act.wait_ge(*ready("pe_job", "xt", *tag, j))
                    step(act.copy(xT[:, 2 * j:2 * j + 2, :], bank_view(tag, j)), "xt", *tag, j)

            def bank_view(tag, j):
                return psum[:, j, :].rearrange("p (a b) -> p a b", a=2)

            def ffn_piece(name, l, p, key, back):
                for s in range(STEPS):
                    n = 256 * min(2, FT - 2 * s)
                    act.wait_ge(*ready("pe_job", "h1", *key, s))
                    if not (p == 0 and s < 2):
                        act.wait_ge(*ready("dve", "g", *(key if s >= 2 else back[0]), (s - 2) % STEPS,
                                           back=0 if s >= 2 else back[1]))
                    step(act.activation(sil[:, s % 2, 0:n], psum[:, (2 * s) % 4, 0:n], ACT.Silu),
                         "silu", *key, s)

            def ffn(seg, l):
                if seg == "moe":
                    with S.turns(act, N_EXP):
                        key = ("moe", l)
                        ffn_piece(seg, l, 1, key, (key, 1))
                else:
                    for p in range(2):
                        ffn_piece(seg, l, p, (seg, l, p), ((seg, l, p - 1), 0))

            def gates(l, n, banks):
                for _ in range(n):
                    j = gates_done[0] % 16
                    gates_done[0] += 1
                    cp, b = gate_place(j)
                    act.wait_ge(*ready("pe_job", "gate", l, j))
                    for i in range(2):
                        c = 2 * cp + i
                        step(act.activation(zb[:, b, c, :], psum[:, banks[j % len(banks)], i * 256:i * 256 + 256],
                                            ACT.Identity, bias=prm(l, "gate_b", b * KT + c)), "zb", l, j)

            gates_done = [0]

            def norm_roots(*key):
                act.wait_ge(*ready("dve", "var", *key))
                step(act.activation(sd, mv[:, :, 1], ACT.Sqrt, bias=eps[:, 0:1]), "sd", *key)

            def attention(l, units, Sb, PTb, seg):
                n = len(units)
                for i in range(n + 2):
                    if i < n:
                        u, b = units[i], i % 2
                        act.wait_ge(*ready("dve", "nm", seg, l, u))
                        for qt, (k0, nk) in enumerate(KEYS):
                            for h in range(2):
                                s = Sb[:, i % 4, h, k0:k0 + nk]
                                step(act.activation(s, s, ACT.Exp, bias=nm[:, b, qt, h:h + 1],
                                                    accum_out=den[:, b, qt, h:h + 1]), "exp", seg, l, u)
                        if u[0] == "swa":
                            step(act.activation(es[:, b], es[:, b], ACT.Exp), "exp", seg, l, u)
                    if seg == "b1" and i in G[7]:
                        gates(l, 1, (7,))
                    if i >= 2:
                        turned(units[i - 2], l, seg, i - 2, PTb)

            def turned(v, l, seg, i, PTb):
                act.wait_ge(*ready("pe_job", "pt", seg, l, v))
                if i >= 2:
                    act.wait_ge(*ready("pe_job", "o", seg, l, units_of(seg)[i - 2]))
                nh = 1 if v[0] == "diff" else 2
                step(act.copy(PTb[:, i % 2, 0:nh, :], psum[:, 4:4 + nh, 0:PACK]), "pt", seg, l, v)

            for l in range(DEPTH):
                load_rows(l, a["ln_g"][l, 0], a["ln_b"][l, 0], "ln1", l)
                transposed(("b1", l))
                for i, dst in ((0, swa_q[:, 0:2, :]), (1, swa_q[:, 2:4, :]), (3, raw[:, 0:2, 1:]),
                               (5, raw[:, 4:6, 1:]), (7, fox_q[:]), (9, fox_v[:]), (10, dsa_q[:])):
                    act.wait_ge(*ready("pe_job", "in", l, i))
                    step(act.copy(dst, psum[:, in_bank(i), :].rearrange("p (a b) -> p a b", a=2)), "in", l, i)
                barrier()
                gates(l, G[0], (6,))
                act.wait_ge(*ready("dve", "mix", l))
                step(act.activation(tanh_w[0:64, :], mix[0:64, 6, :], ACT.Tanh), "tanh", l)
                step(act.activation(mix[:, 7, :], mix[:, 7, :], ACT.Sigmoid), "sig_g", l)
                act.wait_ge(*ready("pe_job", "w_up", l))
                for ct in range(2):
                    step(act.activation(sw[:, ct, :], psum[:, 0, ct * 256:ct * 256 + 256], ACT.Sigmoid,
                                        bias=prm(l, "w0", ct)), "sw", l)
                act.wait_ge(*ready("pe_job", "a_up", l))
                for ct in range(2):
                    step(act.activation(av[:, ct, :], psum[:, 1, ct * 256:ct * 256 + 256], ACT.Sigmoid,
                                        bias=prm(l, "a0", ct)), "a", l)
                act.wait_ge(*ready("pe_job", "g_up", l))
                step(act.copy(gv[:], psum[:, 2, :].rearrange("p (a b) -> p a b", a=2)), "g", l)
                gates(l, G[1], (6,))
                act.wait_ge(*ready("pe_job", "kk", l))
                step(act.activation(sq[:], psum[:, 3, :].rearrange("p (a b) -> p a b", a=2), ACT.Sqrt,
                                    bias=eps[:, 3:4]), "kk_norm", l)
                gates(l, G[2], (6,))
                act.wait_ge(*ready("dve", "decay", l))
                step(act.activation(Wc[:], L[:], ACT.Exp, scale=-DECAY), "W", l)
                step(act.activation(Wi[:], L[:], ACT.Exp, scale=DECAY), "W", l)
                step(act.activation(Wp[:], Wp[:], ACT.Exp, scale=-DECAY), "W", l)
                for i, t in enumerate((tokV, tokB, tokK)):
                    for g in range(2):
                        if i == 1 and g == 0:
                            gates(l, G[3], (6,))
                        act.wait_ge(*ready("pe_job", "tok", l, i, g))
                        for odd in range(2):
                            step(act.copy(t[hb(odd), 4 * g:4 * g + 4, :],
                                          psum[0:CH, (3, 7)[g], :].rearrange("p (m o d) -> p m o d", m=4, o=2)
                                          [:, :, odd, :]), "tok", l, i, g)
                for lv in range(1, 6):
                    for g in range(2):
                        act.wait_ge(*ready("pe_job", "U", l, lv, g))
                        step(act.copy(U[:, 4 * g:4 * g + 4, :].rearrange("p m c -> p (m c)"),
                                      psum[:, 4 * g, 0:256]), "U", l, lv, g)
                    gates(l, G[4][lv - 1], (6, 7))
                for c in range(NC):
                    act.wait_ge(*ready("pe_job", "X", l, c))
                    step(act.activation(RS[:, c % 2].rearrange("p h v -> p (h v)"), psum[:, 0, 0:P],
                                        ACT.Copy, scale=-1.0), "RS", l, c)
                    gates(l, G[5][c], (6, 7))
                    act.wait_ge(*ready("pe_job", "SA", l, c))
                    step(act.copy(SA[:, c % 2].rearrange("p h v -> p (h v)"), psum[:, 1, 0:P]), "SA", l, c)
                    act.wait_ge(*ready("pe_job", "Y", l, c))
                    step(act.copy(yv[:, :, c * CH:(c + 1) * CH],
                                  psum[:, 2, 0:2 * CH].rearrange("p (a b) -> p a b", a=2)), "y", l, c)
                act.wait_ge(*ready("pe_job", "var", l))
                step(act.activation(sq[:], psum[:, 5, :].rearrange("p (a b) -> p a b", a=2), ACT.Sqrt,
                                    bias=eps[:, 1:2], scale=1.0 / HD), "gn", l)
                barrier()
                act.wait_ge(*ready("dve", "fox_abs", l))
                step(act.activation(fox_t[0:4, 1, :], fox_t[0:4, 1, :], ACT.Exp, scale=-1.0), "fox_exp", l)
                act.wait_ge(*ready("act", "fox_exp", l))
                step(act.activation(fox_t[0:4, 1, :], fox_t[0:4, 1, :], ACT.Ln, bias=1.0), "fox_ln", l)
                gates(l, G[6], (0, 1))
                attention(l, UNITS1, Sm, PT, "b1")
                barrier()
                w = kview(a["w_branch"][l])
                act.dma_start(wb[:, 0:5, :], w[:, 0:5, :]).then_inc(*made("wb", l, by=16))
                act.dma_start(wb[:, 5:10, :], w[:, 5:10, :]).then_inc(*made("wb", l, by=16))
                for c in range(KT):
                    step(act.activation(zb[:, :, c, :], zb[:, :, c, :], ACT.Sigmoid), "sig", l, c)
                barrier()
                norm_roots("ln1", l)
                barrier()
                load_rows(l, a["ln_g"][l, 1], a["ln_b"][l, 1], "ln2", l)
                transposed(("f1", l))
                if l == 1:
                    act.wait_ge(*ready("dve", "router_gap"))
                    step(act.activation(e2, e2, ACT.Exp), "router_exp")
                ffn("ffn1" if l == 0 else "moe", l)
                norm_roots("ln2", l)
                barrier()

            act.wait_ge(*ready("dve", "angles"))
            step(act.activation(sinb[:].rearrange("p a b -> p (a b)"), ang[:, 1, :], ACT.Sin), "rope")
            step(act.activation(cosb[:].rearrange("p a b -> p (a b)"), ang[:, 2, :], ACT.Sin), "rope")
            for l in range(DEPTH):
                off = 0
                for name, key in (("moba_q_norm_2", 64), ("moba_k_norm_2", 64), ("diff_q_norm_2", 64),
                                  ("diff_k_norm_2", 64), ("moba_out_norm_2", 64), ("diff_subln_2", 128)):
                    act.dma_start(gains[:, off:off + key],
                                  a[name][l].rearrange("(o d) -> o d", o=1).broadcast_to([P, key]))\
                        .then_inc(*made("gains", l, by=16))
                    off += key
                act.dma_start(gains[:, off:off + 256], a["diff_lambda_2"][l].rearrange("i d -> (i d)")
                              .rearrange("(o d) -> o d", o=1).broadcast_to([P, 256])).then_inc(*made("gains", l, by=16))
                load_rows(l, a["b_mod_2"][l][2 * D:3 * D], a["b_mod_2"][l][5 * D:6 * D], "bmod", l)
                act.wait_ge(*ready("dve", "lam_sums", l))
                step(act.activation(lam[:, 2:4], lam[:, 0:2], ACT.Exp), "lam", l)
                barrier()
                act.wait_ge(*ready("dve", "ms", "mix", l))
                step(act.activation(sd, ss16[:, 0:2], ACT.Sqrt, bias=eps[:, 2:3], scale=1.0 / D), "rms", "mix", l)
                barrier()
                for i in range(12):
                    act.wait_ge(*ready("pe_job", "in2", l, i))
                    bank = psum[:, i % 4, :].rearrange("p (t b) -> p t b", t=2)
                    if i in (4, 5, 10, 11):
                        v0 = {4: 0, 5: 256, 10: 512, 11: 768}[i]
                        step(act.copy(vtm[:, :, v0:v0 + 256], bank), "in2", l, i)
                    else:
                        if QK.index(i) >= 2:
                            act.wait_ge(*ready("dve", "headsum", l, QK[QK.index(i) - 2]))
                        n = QK.index(i) % 2
                        step(act.activation(tsq[:, n, :], psum[:, i % 4, :], ACT.Square), "sq", l, i)
                        act.wait_ge(*ready("dve", "headsum", l, i))
                        step(act.activation(rt16[:, 8 * n:8 * n + 8], ss16[:, 8 * n:8 * n + 8], ACT.Sqrt,
                                            bias=eps[:, 2:3], scale=1.0 / HD), "headroot", l, i)
                        act.wait_ge(*ready("pe_job", "qt", l, i))
                        step(act.copy(qT[:, 2 * QK.index(i):2 * QK.index(i) + 2, :],
                                      psum[:, 4 + n, :].rearrange("p (a b) -> p a b", a=2)), "qt", l, i)
                barrier()
                attention(l, UNITS2, Sm2, PT2, "b2")
                for t in range(NT):
                    act.wait_ge(*ready("dve", "outsum", l, t))
                    step(act.activation(rt16[:, 0:8], ss16[:, 0:8], ACT.Sqrt, bias=eps[:, 2:3], scale=1.0 / HD),
                         "outroot", l, t)
                    step(act.activation(rt16[:, 8:12], ss16[:, 8:12], ACT.Sqrt, bias=eps[:, 2:3],
                                        scale=1.0 / (2 * HD)), "outroot", l, t)
                barrier()
                for j in range(4):
                    act.wait_ge(*ready("pe_job", "xt", "o2", l, j))
                    step(act.copy(oT8[:, 2 * j:2 * j + 2, :], bank_view(None, j)), "xt", "o2", l, j)
                act.wait_ge(*ready("dve", "ms", "ffn", l))
                step(act.activation(sd, ss16[:, 0:2], ACT.Sqrt, bias=eps[:, 2:3], scale=1.0 / D), "rms", "ffn", l)
                barrier()
                ffn("ffn2", l)
                barrier()

        @block.tensor
        def _(pe):
            barrier = barrier_of(pe)
            take = slot_of()
            barrier()

            def job(ins, *key):
                ins.then_inc(*made("pe_job", *key))

            def unit(*key):
                slot = take()
                pe.wait_ge(*ready("slot%d" % slot, "unit", *key))
                return ring[:, slot, :]

            def used(*key):
                S.also("pe_job", "unit", *key)

            def turn(src, tag, wait):
                for j in range(4):
                    if wait is not None:
                        pe.wait_ge(*wait)
                    for i in range(2):
                        for t in range(NT):
                            k = 2 * j + i
                            ins = pe.transpose(psum[:, j, i * 256 + t * P:i * 256 + t * P + P],
                                               src[:, t, k * P:k * P + P], ident[:])
                    job(ins, "xt", *tag, j)

            def gates(l, n, banks):
                for _ in range(n):
                    j = gates_done[0] % 16
                    gates_done[0] += 1
                    bank = banks[j % len(banks)]
                    if bank in gate_in:
                        pe.wait_ge(*ready("act", "zb", l, gate_in[bank]))
                    w = unit("gate", l, *gate_place(j))
                    for i in range(2):
                        ins = channel_tile(psum[:, bank, i * 256:i * 256 + 256], w, i * P, P)
                    job(ins, "gate", l, j)
                    used("gate", l, *gate_place(j))
                    gate_in[bank] = j

            gates_done, gate_in = [0], {}

            def channel_tile(dst, w, c0, m, act_t=xT):
                for k in range(KT):
                    ins = pe.matmul(dst, w[:, k * 256 + c0:k * 256 + c0 + m], act_t[:, k, :],
                                    start=(k == 0), stop=(k == KT - 1))
                return ins

            def token_tile(dst, w, c0, n, t, act_t=xT):
                for k in range(KT):
                    ins = pe.matmul(dst, act_t[:, k, t * P:t * P + P], w[:, k * 256 + c0:k * 256 + c0 + n],
                                    start=(k == 0), stop=(k == KT - 1))
                return ins

            def down(key, s, w2):
                n = min(2, FT - 2 * s)
                pe.wait_ge(*ready("dve", "g", *key, s))
                for f in range(n):
                    for t in range(NT):
                        for h in range(2):
                            ins = pe.matmul(psum[:, 4 + 2 * t + h, :],
                                            gT[:, s % 3, f * 256 + t * P:f * 256 + t * P + P],
                                            w2[:, f * D + h * 512:f * D + h * 512 + 512],
                                            start=(s == 0 and f == 0), stop=(s == STEPS - 1 and f == n - 1))
                job(ins, "down", *key, s)
                used(key, "w2", s)

            def ffn_piece(key, p, back):
                w2 = None
                for s in range(STEPS):
                    n = min(2, FT - 2 * s)
                    for i, (w, what, eng) in enumerate((("w1", "silu", "act"), ("w3", "g", "dve"))):
                        b = (2 * s + i) % 4
                        if s >= 2:
                            pe.wait_ge(*ready(eng, what, *key, s - 2))
                        elif p > 0:
                            pe.wait_ge(*ready(eng, what, *back[0], s + STEPS - 2, back=back[1]))
                        wt = unit(key, w, s)
                        for f in range(n):
                            ins = channel_tile(psum[:, b, f * 256:f * 256 + 256], wt, f * P, P)
                        job(ins, "h1" if i == 0 else "h3", *key, s)
                        used(key, w, s)
                    if s == 1 and p > 0:
                        pe.wait_ge(*ready("dve", "acc", *back[0], back=back[1]))
                    if s >= 1:
                        down(key, s - 1, w2)
                    w2 = unit(key, "w2", s)
                down(key, STEPS - 1, w2)

            def ffn(seg, l):
                if seg == "moe":
                    key = ("moe", l)
                    with S.turns(pe, N_EXP):
                        ffn_piece(key, 1, (key, 1))
                else:
                    for p in range(2):
                        ffn_piece((seg, l, p), p, ((seg, l, p - 1), 0))

            def out_rows(kind, l, src):
                for k2 in range(4):
                    w = unit(kind, l, k2)
                    for i in range(2):
                        k = 2 * k2 + i
                        for t in range(NT):
                            for h in range(2):
                                ins = pe.matmul(psum[:, 4 + 2 * t + h, :], src[:, k, t * P:t * P + P],
                                                w[:, i * D + h * 512:i * D + h * 512 + 512],
                                                start=(k == 0), stop=(k == KT - 1))
                    job(ins, kind, l, k2)
                    used(kind, l, k2)

            def scores(l, seg, i, u):
                kind, hp = u
                if i >= 2:
                    pe.wait_ge(*ready("dve", "sm", seg, l, units_of(seg)[i - 2]))
                q, k = qk_of(kind, hp)
                for h in range(2):
                    hd = 2 * hp + h
                    four = slice(HD * h, HD * h + 4)
                    head = ident[four, HD * h + hd:HD * h + hd + 1]
                    for qt, (k0, nk) in enumerate(KEYS):
                        dst = psum[:, 2 * (i % 2) + h, k0:k0 + nk]
                        ins = pe.matmul(dst, q[hb(h), qt * P:qt * P + P], k[hb(h), 0:nk],
                                        start=True, stop=(kind != "fox"))
                        if kind == "fox":
                            pe.matmul(dst, head.broadcast_to([4, P]), fox_t[four, 1, 0:nk], start=False, stop=False)
                            ins = pe.matmul(dst, fox_t[four, 0, qt * P:qt * P + P], head.broadcast_to([4, nk]),
                                            start=False, stop=True)
                job(ins, "s", seg, l, u)

            def qk_of(kind, hp):
                if kind == "swa":
                    return swa_q[:, hp, :], swa_k[:, hp // 2, :]
                if kind == "fox":
                    return fox_q[:, hp, :], fox_k[:, hp, :]
                if kind == "dsa":
                    return dsa_q[:, hp, :], dsa_k
                if kind == "moba":
                    return qT[:, hp, :], qT[:, 4 + hp, :]
                return qT[:, 8 + hp, :], qT[:, 12 + hp, :]

            def v_of(kind, hp, h, k):
                hd = 2 * hp + h
                if kind == "swa":
                    g = hp // 2
                    return swa_v[:, k, g * HD:g * HD + HD]
                if kind == "fox":
                    return fox_v[:, k, hd * HD:hd * HD + HD]
                if kind == "dsa":
                    return dsa_v[:, k, :]
                if kind == "moba":
                    return vtm[:, k, hd * HD:hd * HD + HD]
                return vtm[:, k, 512 + hp * P:512 + hp * P + P]

            def turn_probs(l, seg, i, u, Sb):
                kind, hp = u
                pe.wait_ge(*ready("dve", "p", seg, l, u))
                if i >= 1:
                    pe.wait_ge(*ready("act", "pt", seg, l, units_of(seg)[i - 1]))
                for h in range(1 if kind == "diff" else 2):
                    for o in range(0, PACK, P):
                        ins = pe.transpose(psum[:, 4 + h, o:o + P], Sb[:, i % 4, h, o:o + P], ident[:])
                job(ins, "pt", seg, l, u)

            def weigh(l, seg, i, u, PTb):
                kind, hp = u
                pe.wait_ge(*ready("act", "pt", seg, l, u))
                lag = 1 if seg == "b1" else 2
                if i >= lag:
                    pe.wait_ge(*ready("dve", "o", seg, l, units_of(seg)[i - lag]))
                b = o_bank(seg, i)
                for qt, (k0, nk) in enumerate(KEYS):
                    for h in range(1 if kind == "diff" else 2):
                        for k in range(qt + 1):
                            probs = PTb[:, i % 2, h, k0 + k * P:k0 + k * P + P]
                            if seg == "b1":
                                ins = pe.matmul(psum[hb(h), b, qt * P:qt * P + P], v_of(kind, hp, h, k), probs,
                                                start=(k == 0), stop=(k == qt))
                            else:
                                n = P if kind == "diff" else HD
                                o = qt * P + h * HD
                                ins = pe.matmul(psum[:, b, o:o + n], probs, v_of(kind, hp, h, k),
                                                start=(k == 0), stop=(k == qt))
                job(ins, "o", seg, l, u)

            def attention(l, seg, Sb, PTb):
                units = units_of(seg)
                n = len(units)
                for i in range(n + 3):
                    if i < n:
                        if units[i] == ("fox", 0):
                            pe.wait_ge(*ready("dve", "fox_c", l))
                        scores(l, seg, i, units[i])
                    if seg == "b1" and i in G[7]:
                        gates(l, 1, (7,))
                    if 2 <= i < n + 2:
                        turn_probs(l, seg, i - 2, units[i - 2], Sb)
                    if i >= 3:
                        weigh(l, seg, i - 3, units[i - 3], PTb)

            def turn_qk(l, i):
                n = QK.index(i)
                pe.wait_ge(*ready("dve", "roped", l, i))
                if n >= 2:
                    pe.wait_ge(*ready("act", "qt", l, QK[n - 2]))
                for ct in range(2):
                    for t in range(NT):
                        ins = pe.transpose(psum[:, 4 + n % 2, ct * 256 + t * P:ct * 256 + t * P + P],
                                           tq[:, n % 2, t * 256 + ct * P:t * 256 + ct * P + P], ident[:])
                job(ins, "qt", l, i)

            for l in range(DEPTH):
                turn(x, ("b1", l), None)
                for i in range(13):
                    b = in_bank(i)
                    if i >= 4 and i < 8:
                        pe.wait_ge(*ready("act", "xt", "b1", l, i - 4))
                    elif i >= 8:
                        pe.wait_ge(*in_copied(ready, l, i - 8))
                    if i == 0:
                        pe.wait_ge(*ready("act", "xt", "b1", l, 3))
                    w = unit("in", l, i)
                    if i == 2:
                        channel_tile(psum[:, b, 0:256], w, 0, P)
                        for t in range(NT):
                            ins = token_tile(psum[:, b, 256 + t * P:256 + t * P + P], w, P, P, t)
                    elif i == 9:
                        for t in range(NT):
                            ins = token_tile(psum[:, b, t * 256:t * 256 + 256], w, 0, 256, t)
                    elif i == 11:
                        channel_tile(psum[0:HD, b, 0:256], w, 0, HD)
                        ins = channel_tile(psum[0:HD, b, 256:512], w, 128, HD)
                        job(ins, "in", l, i)
                        pe.wait_ge(*in_copied(ready, l, 5))
                        b = 1
                        for t in range(NT):
                            token_tile(psum[:, b, t * HD:t * HD + HD], w, HD, HD, t)
                            token_tile(psum[:, b, 128 + t * 4:128 + t * 4 + 4], w, 192, 4, t)
                        ins = channel_tile(psum[0:4, b, 256:512], w, 196, 4)
                        job(ins, "in", l, 13)
                        used("in", l, i)
                        continue
                    else:
                        for j in range(2):
                            ins = channel_tile(psum[:, b, j * 256:j * 256 + 256], w, j * P, P)
                    job(ins, "in", l, i)
                    used("in", l, i)
                barrier()

                gate_in.clear()
                gates(l, G[0], (6,))
                pe.wait_ge(*ready("act", "tanh", l))
                for ct in range(2):
                    ins = pe.matmul(psum[:, 0, ct * 256:ct * 256 + 256], lora[0:64, l, 0, ct * P:ct * P + P],
                                    tanh_w[0:64, :], start=True, stop=True)
                job(ins, "w_up", l)
                for ct in range(2):
                    ins = pe.matmul(psum[:, 1, ct * 256:ct * 256 + 256], lora[64:128, l, 0, ct * P:ct * P + P],
                                    mix[64:128, 6, :], start=True, stop=True)
                job(ins, "a_up", l)
                pe.wait_ge(*ready("act", "sig_g", l))
                for ct in range(2):
                    ins = pe.matmul(psum[:, 2, ct * 256:ct * 256 + 256], lora[:, l, 1, ct * P:ct * P + P],
                                    mix[:, 7, :], start=True, stop=True)
                job(ins, "g_up", l)
                gates(l, G[1], (6,))
                pe.wait_ge(*ready("dve", "kk_sq", l))
                ins = pe.matmul(psum[:, 3, :], block_ones[:], sq[:], start=True, stop=True)
                job(ins, "kk", l)
                gates(l, G[2], (6,))
                pe.wait_ge(*ready("dve", "rkr", l))
                ins = pe.matmul(psum[:, 4, :], block_ones[:], yn[:], start=True, stop=True)
                job(ins, "bonus", l)

                def token_copy(i, g):
                    src = (mix[:, 4:6, :], Bh[:], kh[:])[i]
                    if i > 0:
                        pe.wait_ge(*ready("act", "tok", l, i - 1, g))
                    elif g == 0:
                        pe.wait_ge(*ready("act", "kk_norm", l))
                    for cc in range(2):
                        for ct in range(2):
                            c = 2 * g + cc
                            ins = pe.transpose(psum[0:CH, (3, 7)[g], cc * 256 + ct * P:cc * 256 + ct * P + P],
                                               src[:, ct, c * CH:(c + 1) * CH], ident[:])
                    job(ins, "tok", l, i, g)

                for g in range(2):
                    token_copy(0, g)
                gates(l, G[3], (6,))
                pe.wait_ge(*ready("dve", "scaled", l))
                for i in (1, 2):
                    for g in range(2):
                        token_copy(i, g)
                pe.wait_ge(*ready("dve", "bonus", l))
                pe.wait_ge(*ready("act", "a", l))
                pe.wait_ge(*ready("act", "g", l))
                for c in range(NC):
                    b = (0, 1, 4, 5)[c]
                    for h in range(4):
                        ct, s_ = h // 2, slice(c * CH, (c + 1) * CH)
                        kr = KR[hb(h), ct, c, :, :]
                        pe.matmul(psum[hb(h), b, ct * P:ct * P + P], Bh[hb(h), ct, s_], kr, start=True, stop=True)
                        pe.matmul(psum[hb(h), b, 256 + ct * P:256 + ct * P + P], kh[hb(h), ct, s_], kr,
                                  start=True, stop=True)
                        m = 2 * c + ct
                        ins = pe.matmul(psum[hb(h), 2, m * CH:m * CH + CH], KR[hb(h), ct, c, 0, :],
                                        Bh[hb(h), ct, s_], start=True, stop=True)
                    job(ins, "gram", l, c)
                pe.wait_ge(*ready("act", "tok", l, 2, 1))
                for lv in range(1, 6):
                    for g in range(2):
                        pe.wait_ge(*(ready("dve", "BT", l) if lv == 1 else ready("dve", "T", l, lv - 1, g)))
                        for m in range(4 * g, 4 * g + 4):
                            for odd in range(2):
                                o = (m % 4) * CH
                                ins = pe.matmul(psum[hb(odd), 4 * g, o:o + CH], BT[lv - 1][hb(odd), m, :],
                                                T[hb(odd), m, :], start=True, stop=True)
                        job(ins, "U", l, lv, g)
                    gates(l, G[4][lv - 1], (6, 7))
                    for g in range(2):
                        pe.wait_ge(*ready("act", "U", l, lv, g))
                        for m in range(4 * g, 4 * g + 4):
                            for odd in range(2):
                                o = (m % 4) * CH
                                pe.matmul(psum[hb(odd), 4 * g + 1, o:o + CH], TT[hb(odd), m, :], U[hb(odd), m, :],
                                          start=True, stop=True)
                                ins = pe.matmul(psum[hb(odd), 4 * g + 1, 256 + o:256 + o + CH], U[hb(odd), m, :],
                                                TT[hb(odd), m, :], start=True, stop=True)
                        job(ins, "TUT", l, lv, g)
                for c in range(NC):
                    z = (c + 1) % 2
                    if c == 0:
                        pe.wait_ge(*ready("dve", "T", l, 5, 0))
                        pe.wait_ge(*ready("dve", "T", l, 5, 1))
                    else:
                        pe.wait_ge(*ready("dve", "Z", l, c - 1))
                    for h in range(4):
                        ct, r_ = h // 2, hb(h)
                        m, dst = 2 * c + ct, psum[r_, 0, ct * CH:ct * CH + CH]
                        if c > 0:
                            pe.matmul(dst, KR[r_, ct, c, 0, :], Z[r_, z, ct, :], start=True, stop=False)
                        ins = pe.matmul(dst, GR[r_, m, 0, :], tokV[r_, m, :], start=(c == 0), stop=True)
                    job(ins, "X", l, c)
                    gates(l, G[5][c], (6, 7))
                    pe.wait_ge(*ready("act", "RS", l, c))
                    for h in range(4):
                        ct, r_ = h // 2, hb(h)
                        ins = pe.matmul(psum[r_, 1, ct * CH:ct * CH + CH], TT[r_, 2 * c + ct, :],
                                        RS[r_, c % 2, ct, :], start=True, stop=True)
                    job(ins, "SA", l, c)
                    pe.wait_ge(*ready("act", "SA", l, c))
                    if c < NC - 1:
                        for h in range(4):
                            ct, r_ = h // 2, hb(h)
                            m, dst = 2 * c + ct, psum[r_, 3, ct * CH:ct * CH + CH]
                            pe.matmul(dst, tokB[r_, m, :], SA[r_, c % 2, ct, :], start=True, stop=False)
                            ins = pe.matmul(dst, tokK[r_, m, :], tokV[r_, m, :], start=False, stop=True)
                        job(ins, "Znew", l, c)
                    if c >= 1:
                        pe.wait_ge(*ready("act", "y", l, c - 1))
                    for h in range(4):
                        ct, r_ = h // 2, hb(h)
                        m, dst = 2 * c + ct, psum[r_, 2, ct * CH:ct * CH + CH]
                        if c > 0:
                            pe.matmul(dst, Z[r_, z, ct, :], KR[r_, ct, c, 1, :], start=True, stop=False)
                        pe.matmul(dst, SA[r_, c % 2, ct, :], AB[r_, m, 1, :], start=(c == 0), stop=False)
                        ins = pe.matmul(dst, tokV[r_, m, :], GR[r_, m, 1, :], start=False, stop=True)
                    job(ins, "Y", l, c)
                pe.wait_ge(*ready("act", "y", l, NC - 1))
                ins = pe.matmul(psum[:, 4, :], block_ones[:], yv[:], start=True, stop=True)
                job(ins, "mean", l)
                pe.wait_ge(*ready("dve", "y_sq", l))
                ins = pe.matmul(psum[:, 5, :], block_ones[:], sq[:], start=True, stop=True)
                job(ins, "var", l)
                barrier()

                gate_in.clear()
                for qt in range(NT):
                    nk = P * (qt + 1)
                    for h2 in range(2):
                        for h in range(2):
                            ins = pe.matmul(psum[:, 4 + 2 * qt + h, h2 * 256:h2 * 256 + nk],
                                            dsa_qi[hb(h), h2, qt * P:qt * P + P], dsa_ki[hb(h), 0:nk],
                                            start=True, stop=True)
                    job(ins, "idx", l, qt)
                gates(l, G[6], (0, 1))
                for b in (0, 1):
                    if b in gate_in:
                        pe.wait_ge(*ready("act", "zb", l, gate_in[b]))
                pe.wait_ge(*ready("dve", "pick", l, NT - 1))
                attention(l, "b1", Sm, PT)
                barrier()

                pe.wait_ge(*ready("wb", l))
                for c in range(KT):
                    if c >= 2:
                        pe.wait_ge(*ready("dve", "prod", l, c - 2))
                    for b in range(4):
                        rows_of = (range(0, 4), range(4, 6), range(6, 8), range(8, 10))[b]
                        dst = psum[:, 4 + 2 * (c % 2) + b // 2, (b % 2) * 256:(b % 2) * 256 + 256]
                        for k in rows_of:
                            ins = pe.matmul(dst, wb[:, k, c * P:c * P + P], oT[:, k, :],
                                            start=(k == rows_of[0]), stop=(k == rows_of[-1]))
                    job(ins, "branch", l, c)
                barrier()
                out_rows("out", l, mergedT)
                barrier()
                turn(x, ("f1", l), None)
                pe.wait_ge(*ready("act", "xt", "f1", l, 3))
                if l == 1:
                    for t in range(NT):
                        for k in range(KT):
                            ins = pe.matmul(psum[:, 4, t * 8:t * 8 + 8], xT[:, k, t * P:t * P + P], router[:, k, :],
                                            start=(k == 0), stop=(k == KT - 1))
                    job(ins, "router")
                    pe.wait_ge(*ready("dve", "router_logits"))
                ffn("ffn1" if l == 0 else "moe", l)
                barrier()

            for l in range(DEPTH):
                for j in range(MOD_UNITS):
                    part_, q = divmod(j, 4)
                    if part_ in (2, 5):
                        b = 1 + 2 * (part_ // 3) + q // 2
                        ins = pe.matmul(psum[:, b, (q % 2) * 256:(q % 2) * 256 + 256], ones[:], pmod[:, j, :],
                                        start=True, stop=True)
                    else:
                        col = {0: 0, 1: 8, 3: 16, 4: 24}[part_] + 2 * q
                        for s in range(2):
                            ins = pe.matmul(psum[:, 0, col + s:col + s + 1], pmod[:, j, s * P:s * P + P],
                                            ones[:, 0:1], start=True, stop=True)
                job(ins, "mod", l)
                barrier()
                pe.wait_ge(*ready("dve", "xs", "mix", l))
                turn(tok_scaled, ("mix", l), None)
                barrier()
                for i in range(12):
                    b = i % 4
                    if i >= 4:
                        j = i - 4
                        pe.wait_ge(*(ready("act", "in2", l, j) if j in (4, 5) else ready("dve", "normed", l, j)))
                    w = unit("in2", l, i)
                    for t in range(NT):
                        ins = token_tile(psum[:, b, t * 256:t * 256 + 256], w, 0, 256, t)
                    job(ins, "in2", l, i)
                    used("in2", l, i)
                    if i >= 1 and (i - 1) in QK:
                        turn_qk(l, i - 1)
                barrier()
                attention(l, "b2", Sm2, PT2)
                barrier()
                turn(om, ("o2", l), None)
                pe.wait_ge(*ready("act", "xt", "o2", l, 3))
                out_rows("out2", l, oT8)
                pe.wait_ge(*ready("dve", "xs", "ffn", l))
                turn(tok_scaled, ("ffn", l), None)
                barrier()
                ffn("ffn2", l)
                barrier()

        @block.vector
        def _(dve):
            barrier = barrier_of(dve)

            def step(ins, *key):
                ins.then_inc(*made("dve", *key))
                dve.wait_ge(*here("dve"))

            def here(kind):
                c = S.count[kind]
                if S.turn is None or not known:
                    return S.sem(kind), c
                return S.sem(kind), S.turn * known.per_turn[kind][0] + c

            def free(ins, *key):
                ins.then_inc(*made("dve", *key))

            def two(v):
                return v.rearrange("p (a b) -> p a b", a=2)

            barrier()

            def layer_norm(*key):
                for t in range(NT):
                    for h in range(2):
                        step(dve.bn_stats(stat[:, t, h, :], x[:, t, h * 512:h * 512 + 512]))
                    step(dve.bn_aggr(mv[:, t, :], stat[:, t, :, :].rearrange("p h s -> p (h s)")), "var", *key)
                dve.wait_ge(*ready("act", "sd", *key))
                step(dve.reciprocal(rs, sd))
                dve.wait_ge(*ready("rows", *key))
                for t in range(NT):
                    step(dve.tensor_scalar(x[:, t, :], x[:, t, :], mv[:, t, 0:1], rs[:, t:t + 1],
                                           ALU.subtract, ALU.mult))
                    step(dve.tensor_tensor(x[:, t, :], x[:, t, :], rows[:, 0, :], ALU.mult))
                    step(dve.tensor_tensor(x[:, t, :], x[:, t, :], rows[:, 1, :], ALU.add), "ln", *key)

            def ffn_piece(key, p, back, last):
                for s in range(STEPS):
                    n = 256 * min(2, FT - 2 * s)
                    dve.wait_ge(*ready("act", "silu", *key, s))
                    dve.wait_ge(*ready("pe_job", "h3", *key, s))
                    if s >= 3:
                        dve.wait_ge(*ready("pe_job", "down", *key, s - 3))
                    free(dve.tensor_tensor(gT[:, s % 3, 0:n], sil[:, s % 2, 0:n], psum[:, (2 * s + 1) % 4, 0:n],
                                           ALU.mult), "g", *key, s)
                dve.wait_ge(*ready("pe_job", "down", *key, STEPS - 1))

            def ffn(seg, l):
                if seg == "moe":
                    key = ("moe", l)
                    with S.turns(dve, N_EXP):
                        ffn_piece(key, 1, (key, 1), False)
                        for t in range(NT):
                            step(dve.scalar_tensor_tensor(out=picks[:, t, :], in0=idxf[:, t, 0:2],
                                                          scalar=turn_no, in1=wts[:, t, :], op0=ALU.is_equal,
                                                          op1=ALU.mult))
                            step(dve.tensor_reduce(comb[:, t:t + 1], picks[:, t, :], AX, ALU.add))
                        step(dve.tensor_scalar(turn_no, turn_no, 1.0, None, ALU.add))
                        for t in range(NT):
                            for h in range(2):
                                xs = x[:, t, h * 512:h * 512 + 512]
                                step(dve.scalar_tensor_tensor(out=xs, in0=psum[:, 4 + 2 * t + h, :],
                                                              scalar=comb[:, t:t + 1], in1=xs, op0=ALU.mult,
                                                              op1=ALU.add), "acc", *key)
                else:
                    for p in range(2):
                        key = (seg, l, p)
                        ffn_piece(key, p, None, p == 1)
                        for t in range(NT):
                            for h in range(2):
                                xs = x[:, t, h * 512:h * 512 + 512]
                                ys = psum[:, 4 + 2 * t + h, :]
                                if seg == "ffn1":
                                    step(dve.tensor_tensor(xs, ys, xs, ALU.add), "acc", *key)
                                else:
                                    gs = vtm[:, t, h * 512:h * 512 + 512]
                                    step(dve.tensor_tensor(gs, ys, grow[:, 1, h * 512:h * 512 + 512], ALU.mult))
                                    step(dve.tensor_tensor(xs, gs, xs, ALU.add), "acc", *key)

            def scores_in(l, seg, i, u, Sb):
                kind, hp = u
                b = i % 2
                dve.wait_ge(*ready("pe_job", "s", seg, l, u))
                if i >= 4:
                    dve.wait_ge(*ready("pe_job", "pt", seg, l, units_of(seg)[i - 4]))
                m = dsa_bias if kind == "dsa" else mask[:, 0 if kind == "swa" else 1, :]
                s = Sb[:, i % 4]
                step(dve.scalar_tensor_tensor(out=s, in0=psum[:, 2 * b:2 * b + 2, 0:PACK], scalar=SCALE,
                                              in1=m.unsqueeze(1).broadcast_to([P, 2, PACK]),
                                              op0=ALU.mult, op1=ALU.add), "sm", seg, l, u)
                for qt, (k0, nk) in enumerate(KEYS):
                    step(dve.tensor_reduce(mx[:, b, qt, :], s[:, :, k0:k0 + nk], AX, ALU.max))
                if kind == "swa":
                    sink = sinks[:, l, 2 * hp:2 * hp + 2].unsqueeze(1).broadcast_to([P, NT, 2])
                    step(dve.tensor_tensor(mx[:, b], mx[:, b], sink, ALU.max))
                    step(dve.tensor_tensor(es[:, b], sink, mx[:, b], ALU.subtract))
                step(dve.tensor_scalar(nm[:, b], mx[:, b], -1.0, None, ALU.mult), "nm", seg, l, u)

            def probs(l, seg, i, u, Sb):
                kind, hp = u
                b = i % 2
                dve.wait_ge(*ready("act", "exp", seg, l, u))
                if kind == "swa":
                    step(dve.tensor_tensor(den[:, b], den[:, b], es[:, b], ALU.add))
                step(dve.reciprocal(rc[:, b], den[:, b]))
                if kind == "diff":
                    step(dve.tensor_scalar(rc[:, b, :, 1], rc[:, b, :, 1], lam[:, 5:6], None, ALU.mult))
                for qt, (k0, nk) in enumerate(KEYS):
                    s = Sb[:, i % 4, :, k0:k0 + nk]
                    if kind == "diff":
                        step(dve.tensor_scalar(s[:, 1, :], s[:, 1, :], rc[:, b, qt, 1:2], None, ALU.mult))
                        step(dve.scalar_tensor_tensor(out=s[:, 0, :], in0=s[:, 0, :], scalar=rc[:, b, qt, 0:1],
                                                      in1=s[:, 1, :], op0=ALU.mult, op1=ALU.add), "p", seg, l, u)
                    else:
                        free(dve.tensor_tensor(s, s, rc[:, b, qt, :].unsqueeze(2).broadcast_to([P, 2, nk]),
                                               ALU.mult), "p", seg, l, u)

            def outs(l, seg, i, u):
                kind, hp = u
                dve.wait_ge(*ready("pe_job", "o", seg, l, u))
                bank = psum[:, o_bank(seg, i), 0:SEQ]
                if seg == "b1":
                    tile = {"swa": 0, "fox": 6, "dsa": 8}[kind] + hp
                    free(dve.tensor_copy(oT[:, tile, :], bank), "o", seg, l, u)
                else:
                    c0 = (0 if kind == "moba" else 512) + hp * P
                    step(dve.tensor_copy(om[:, :, c0:c0 + P], two(bank)), "o", seg, l, u)

            def attention(l, seg, Sb):
                units = units_of(seg)
                n = len(units)
                for i in range(n + 4):
                    if i < n:
                        scores_in(l, seg, i, units[i], Sb)
                    if i >= 4:
                        outs(l, seg, i - 4, units[i - 4])
                    if 1 <= i < n + 1:
                        probs(l, seg, i - 1, units[i - 1], Sb)

            for l in range(DEPTH):
                step(dve.memset(raw[:, :, 0:1], 0.0))
                for i in (2, 4, 6, 8, 11, 12, 13):
                    b = in_bank(i)
                    dve.wait_ge(*ready("pe_job", "in", l, i))
                    bank = psum[:, b, :]
                    if i == 2:
                        for g in range(2):
                            for h in range(2):
                                free(dve.tensor_copy(swa_k[hb(h), g, :], psum[hb(g), b, 0:256]))
                        free(dve.tensor_copy(swa_v[:], two(psum[:, b, 256:512])), "in", l, i)
                    elif i in (4, 6):
                        r0 = {4: 2, 6: 6}[i]
                        step(dve.tensor_copy(raw[:, r0:r0 + 2, 1:], two(bank)), "in", l, i)
                    elif i == 8:
                        free(dve.tensor_copy(fox_k[:], two(bank)), "in", l, i)
                    elif i == 11:
                        for h in range(2):
                            free(dve.tensor_copy(dsa_k[hb(h), :], psum[0:HD, b, 0:256]))
                            free(dve.tensor_copy(dsa_ki[hb(h), :], psum[0:HD, b, 256:512]), "in", l, i)
                    elif i == 12:
                        free(dve.tensor_copy(dsa_qi[:], two(bank)), "in", l, i)
                    else:
                        free(dve.tensor_copy(dsa_v[:], two(psum[:, b, 0:128])))
                        free(dve.tensor_scalar(dsa_wi[:], two(psum[:, b, 128:136]), SCALE * 0.5, None, ALU.mult))
                        free(dve.tensor_copy(fox_f[:, 0, :], psum[0:4, b, 256:512]), "in", l, i)
                barrier()
                step(dve.tensor_tensor(mix[:], raw[:, :, 0:SEQ], raw[:, :, 1:], ALU.subtract))
                for i in range(8):
                    step(dve.scalar_tensor_tensor(out=mix[:, i, :], in0=mix[:, i, :], scalar=prm(l, "mu", i),
                                                  in1=raw[:, i, 1:], op0=ALU.mult, op1=ALU.add), "mix", l)
                r, k, v = mix[:, 0:2, :], mix[:, 2:4, :], mix[:, 4:6, :]
                for ct in range(2):
                    step(dve.tensor_scalar(kk[:, ct, :], k[:, ct, :], prm(l, "k_k", ct), None, ALU.mult))
                step(dve.tensor_tensor(sq[:], kk[:], kk[:], ALU.mult), "kk_sq", l)
                dve.wait_ge(*ready("act", "sw", l))
                for ct in range(2):
                    step(dve.tensor_tensor_scan(L[:, ct, :], chunk_gate[:], sw[:, ct, :], 0.0, ALU.mult, ALU.add))
                step(dve.tensor_tensor(Wp[:], L[:], sw[:], ALU.subtract), "decay", l)
                dve.wait_ge(*ready("act", "a", l))
                for ct in range(2):
                    step(dve.tensor_scalar(kp[:, ct, :], av[:, ct, :], -1.0, prm(l, "k_a", ct), ALU.add, ALU.mult))
                step(dve.scalar_tensor_tensor(out=kp[:], in0=kp[:], scalar=1.0, in1=k, op0=ALU.add, op1=ALU.mult))
                step(dve.tensor_tensor(yn[:], r, kp[:], ALU.mult))
                for ct in range(2):
                    step(dve.tensor_scalar(yn[:, ct, :], yn[:, ct, :], prm(l, "r_k", ct), None, ALU.mult), "rkr", l)
                dve.wait_ge(*ready("act", "kk_norm", l))
                step(dve.reciprocal(sq[:], sq[:]))
                step(dve.tensor_tensor(kk[:], kk[:], sq[:], ALU.mult))
                dve.wait_ge(*ready("act", "W", l))

                def chunks(t):
                    return t.rearrange("p a (c s) -> p a c s", c=NC)
                for ct in range(2):
                    def ch(t):
                        return t[:, ct, :].rearrange("p (c s) -> p c s", c=NC)
                    step(dve.tensor_tensor(KR[:, ct, :, 0, :], ch(kk), ch(Wp), ALU.mult))
                    step(dve.tensor_tensor(KR[:, ct, :, 1, :], ch(mix[:, 0:2, :]), ch(Wc), ALU.mult))
                step(dve.tensor_tensor(Bh[:], kk[:], av[:], ALU.mult))
                step(dve.tensor_tensor(Bh[:], Bh[:], Wi[:], ALU.mult))
                step(dve.tensor_tensor(kh[:], kp[:], Wi[:], ALU.mult), "scaled", l)
                dve.wait_ge(*ready("pe_job", "bonus", l))
                step(dve.tensor_tensor(kp[:], two(psum[:, 4, :]), v, ALU.mult), "bonus", l)
                both = tri[:].rearrange("p a b -> p (a b)").unsqueeze(1).broadcast_to([P, 2, P])
                for c in range(NC):
                    dve.wait_ge(*ready("pe_job", "gram", l, c))
                    for i, dst in enumerate((AB, GR)):
                        free(dve.tensor_tensor(dst[:, 2 * c:2 * c + 2].rearrange("p m a b -> p m (a b)"),
                                               two(psum[:, (0, 1, 4, 5)[c], 256 * i:256 * i + 256]), both, ALU.mult))

                def over(m):
                    return m.unsqueeze(1).broadcast_to([P, 2 * NC, CH])
                step(dve.tensor_tensor(T[:], psum[:, 2, :].rearrange("p (m n) -> p m n", m=2 * NC), over(level0[:]),
                                       ALU.mult))
                step(dve.tensor_tensor(T[:], T[:], over(eye[:]), ALU.add))
                step(dve.tensor_tensor(TT[:], AB[:, :, 0, :], over(level[:, 0, :]), ALU.mult))
                step(dve.tensor_tensor(TT[:], TT[:], over(eye[:]), ALU.add))
                for lv in range(1, 6):
                    step(dve.tensor_tensor(BT[lv - 1][:], AB[:, :, 0, :], over(level[:, lv, :]), ALU.mult), "BT", l)
                for lv in range(1, 6):
                    for g in range(2):
                        dve.wait_ge(*ready("pe_job", "TUT", l, lv, g))
                        for i, t in enumerate((T, TT)):
                            tg = t[:, 4 * g:4 * g + 4, :].rearrange("p m c -> p (m c)")
                            free(dve.tensor_tensor(tg, tg, psum[:, 4 * g + 1, 256 * i:256 * i + 256], ALU.add),
                                 "T", l, lv, g)
                for c in range(NC - 1):
                    z = c % 2
                    dve.wait_ge(*ready("pe_job", "Znew", l, c))
                    new = two(psum[:, 3, 0:2 * CH])
                    if c > 0:
                        step(dve.tensor_tensor(Z[:, z], new, Z[:, 1 - z], ALU.add))
                        new = Z[:, z]
                    for ct in range(2):
                        e = c * CH + CH - 1
                        step(dve.tensor_scalar(Z[:, z, ct, :], new[:, ct, :], Wc[:, ct, e:e + 1], None, ALU.mult),
                             "Z", l, c)
                dve.wait_ge(*ready("pe_job", "mean", l))
                step(dve.scalar_tensor_tensor(out=yv[:], in0=two(psum[:, 4, :]), scalar=-1.0 / HD, in1=yv[:],
                                              op0=ALU.mult, op1=ALU.add))
                step(dve.tensor_tensor(sq[:], yv[:], yv[:], ALU.mult), "y_sq", l)
                dve.wait_ge(*ready("act", "gn", l))
                step(dve.reciprocal(sq[:], sq[:]))
                step(dve.tensor_tensor(yv[:], yv[:], sq[:], ALU.mult))
                for ct in range(2):
                    step(dve.tensor_scalar(yv[:, ct, :], yv[:, ct, :], prm(l, "gn_g", ct), prm(l, "gn_b", ct),
                                           ALU.mult, ALU.add))
                step(dve.tensor_tensor(yv[:], yv[:], kp[:], ALU.add))
                step(dve.tensor_tensor(oT[:, 4:6, :], yv[:], gv[:], ALU.mult))
                barrier()

                low = slice(0, 4)
                step(dve.tensor_scalar(fox_t[low, 0, :], fox_f[:, 0, :], fbias[:, l:l + 1], None, ALU.add))
                step(dve.tensor_scalar(fox_t[low, 2, :], fox_t[low, 0, :], -1.0, None, ALU.mult))
                step(dve.tensor_tensor(fox_t[low, 1, :], fox_t[low, 0, :], fox_t[low, 2, :], ALU.max), "fox_abs", l)
                step(dve.tensor_scalar(fox_t[low, 0, :], fox_t[low, 0, :], 0.0, None, ALU.min))
                dve.wait_ge(*ready("act", "fox_ln", l))
                step(dve.tensor_tensor(fox_t[low, 0, :], fox_t[low, 0, :], fox_t[low, 1, :], ALU.subtract))
                step(dve.memset(fox_t[low, 2, :], 1.0))
                step(dve.tensor_tensor_scan(fox_t[low, 3, :], fox_t[low, 2, :], fox_t[low, 0, :], 0.0, ALU.mult,
                                            ALU.add))
                for i, val in enumerate((1.0 / SCALE, -1.0 / SCALE)):
                    for four in (low, slice(HD, HD + 4)):
                        step(dve.tensor_scalar(fox_t[four, i, :], fox_t[low, 3, :], val, None, ALU.mult), "fox_c", l)
                for qt, (k0, nk) in enumerate(KEYS):
                    dve.wait_ge(*ready("pe_job", "idx", l, qt))
                    for h2 in range(2):
                        for h in range(2):
                            dst = score if h2 + h == 0 else part
                            step(dve.tensor_scalar(dst[:, 0:nk],
                                                   psum[:, 4 + 2 * qt + h, h2 * 256:h2 * 256 + nk], 0.0,
                                                   dsa_wi[:, qt, 2 * h2 + h:2 * h2 + h + 1], ALU.max, ALU.mult),
                                 "pick", l, qt)
                            if h2 + h:
                                step(dve.tensor_tensor(score[:, 0:nk], score[:, 0:nk], part[:, 0:nk], ALU.add))
                    step(dve.tensor_tensor(score[:, 0:nk], score[:, 0:nk], mask[:, 2, k0:k0 + nk], ALU.add))
                    src = score[:, 0:nk]
                    for rnd in range(TOPK // 8):
                        step(dve.max(m8, src))
                        step(dve.match_replace(picked[:, rnd % 2, 0:nk], m8, src, TAKEN))
                        src = picked[:, rnd % 2, 0:nk]
                    step(dve.tensor_tensor(part[:, 0:nk], src, score[:, 0:nk], ALU.is_equal))
                    step(dve.tensor_scalar(dsa_bias[:, k0:k0 + nk], part[:, 0:nk], NEG, None, ALU.mult))
                attention(l, "b1", Sm)
                barrier()

                for c in range(KT):
                    dve.wait_ge(*ready("act", "sig", l, c))
                    dve.wait_ge(*ready("pe_job", "branch", l, c))
                    for b in range(2):
                        step(dve.tensor_tensor(two(prod[:, c % 2, b, :]), zb[:, 2 * b:2 * b + 2, c, :],
                                               two(psum[:, 4 + 2 * (c % 2) + b, :]), ALU.mult), "prod", l, c)
                    step(dve.tensor_tensor(prod[:, c % 2, 0, :], prod[:, c % 2, 0, :], prod[:, c % 2, 1, :], ALU.add))
                    step(dve.tensor_tensor(mergedT[:, c, :], prod[:, c % 2, 0, 0:256], prod[:, c % 2, 0, 256:512],
                                           ALU.add), "merged", l)
                barrier()
                dve.wait_ge(*ready("pe_job", "out", l, 3))
                for t in range(NT):
                    for h in range(2):
                        xs = x[:, t, h * 512:h * 512 + 512]
                        step(dve.scalar_tensor_tensor(out=xs, in0=xs, scalar=ALPHA, in1=psum[:, 4 + 2 * t + h, :],
                                                      op0=ALU.mult, op1=ALU.add))
                layer_norm("ln1", l)
                barrier()
                dve.wait_ge(*ready("pe_job", "xt", "f1", l, 3))
                for t in range(NT):
                    step(dve.tensor_scalar(x[:, t, :], x[:, t, :], ALPHA, None, ALU.mult))
                if l == 1:
                    dve.wait_ge(*ready("pe_job", "router"))
                    step(dve.tensor_tensor(logit[:], psum[:, 4, 0:16].rearrange("p (t e) -> p t e", t=NT),
                                           router_b[:].unsqueeze(1).broadcast_to([P, NT, N_EXP]), ALU.add),
                         "router_logits")
                    for t in range(NT):
                        step(dve.max(top8[:, t, :], logit[:, t, :]))
                        step(dve.max_index(idx8[:, t, :].bitcast(U32), top8[:, t, :], logit[:, t, :]))
                    step(dve.tensor_copy(idxf[:], idx8.bitcast(U32)))
                    step(dve.tensor_tensor(e2, top8[:, :, 1], top8[:, :, 0], ALU.subtract), "router_gap")
                    dve.wait_ge(*ready("act", "router_exp"))
                    step(dve.tensor_scalar(wts[:, :, 0], e2, 1.0, None, ALU.add))
                    step(dve.reciprocal(wts[:, :, 0], wts[:, :, 0]))
                    step(dve.tensor_tensor(wts[:, :, 1], wts[:, :, 0], e2, ALU.mult))
                    step(dve.memset(turn_no, 0.0))
                ffn("ffn1" if l == 0 else "moe", l)
                layer_norm("ln2", l)
                barrier()

            step(dve.tensor_copy(ang[:, 0, 0:NT], pos[:]))
            for t in range(NT):
                step(dve.tensor_scalar(ang[:, 1, t * 8:t * 8 + 8], invf[:], ang[:, 0, t:t + 1], None, ALU.mult))
            for dst, quarter in ((1, 0.0), (2, 0.25)):
                src = ang[:, 1, :] if dst == 1 else ang[:, 0, :]
                if dst == 1:
                    step(dve.tensor_copy(ang[:, 0, :], ang[:, 1, :]))
                    src = ang[:, 0, :]
                step(dve.tensor_scalar(ang[:, dst, :], src, 1.0 / (2 * math.pi), quarter, ALU.mult, ALU.add))
                step(dve.tensor_copy(angi, ang[:, dst, :]))
                step(dve.tensor_copy(rope[:, 0, 0:16], angi))
                step(dve.tensor_scalar(ang[:, dst, :], rope[:, 0, 0:16], -TWO_PI_A, None, ALU.mult))
                step(dve.tensor_tensor(ang[:, dst, :], ang[:, dst, :], src, ALU.add))
                for cst in (TWO_PI_B, TWO_PI_C):
                    step(dve.scalar_tensor_tensor(out=ang[:, dst, :], in0=rope[:, 0, 0:16], scalar=-cst,
                                                  in1=ang[:, dst, :], op0=ALU.mult, op1=ALU.add))
                if dst == 2:
                    step(dve.tensor_scalar(ang[:, dst, :], ang[:, dst, :], math.pi / 2, None, ALU.add))
                step(dve.tensor_scalar(rope[:, 1, 0:16], ang[:, dst, :], math.pi, -2 * math.pi, ALU.is_gt, ALU.mult))
                step(dve.tensor_tensor(ang[:, dst, :], ang[:, dst, :], rope[:, 1, 0:16], ALU.add))
                step(dve.tensor_scalar(rope[:, 1, 0:16], ang[:, dst, :], -math.pi, 2 * math.pi, ALU.is_lt, ALU.mult))
                step(dve.tensor_tensor(ang[:, dst, :], ang[:, dst, :], rope[:, 1, 0:16], ALU.add))
                step(dve.tensor_scalar(ang[:, dst, :], ang[:, dst, :], PI_IN, -PI_IN, ALU.min, ALU.max), "angles")

            def rms_rows(which, l):
                for t in range(NT):
                    step(dve.tensor_tensor(tok_scaled[:, t, :], x[:, t, :], x[:, t, :], ALU.mult))
                    step(dve.tensor_reduce(ss16[:, t:t + 1], tok_scaled[:, t, :], AX, ALU.add), "ms", which, l)
                dve.wait_ge(*ready("act", "rms", which, l))
                step(dve.reciprocal(rs, sd))
                for t in range(NT):
                    step(dve.tensor_scalar(tok_scaled[:, t, :], x[:, t, :], rs[:, t:t + 1], None, ALU.mult),
                         "xs", which, l)

            def modulate(which, l, i):
                for j in range(4):
                    dve.wait_ge(*ready("pe_job", "xt", which, l, j))
                    for s in range(2):
                        k = 2 * j + s
                        free(dve.tensor_scalar(xT[:, k, :], psum[:, j, s * 256:s * 256 + 256], Amod[:, i, k:k + 1],
                                               modT[:, 16 * i + k:16 * i + k + 1], ALU.mult, ALU.add),
                             "modulated", which, l, j)

            for l in range(DEPTH):
                lam_init = 0.8 - 0.6 * math.exp(-0.3 * l)
                dve.wait_ge(*ready("gains", l))
                lp = gain("lambda").rearrange("p (i d) -> p i d", i=4)
                for i in range(2):
                    step(dve.tensor_tensor(lp[:, 2 * i, :], lp[:, 2 * i, :], lp[:, 2 * i + 1, :], ALU.mult))
                    step(dve.tensor_reduce(lam[:, i:i + 1], lp[:, 2 * i, :], AX, ALU.add), "lam_sums", l)
                dve.wait_ge(*ready("act", "lam", l))
                step(dve.tensor_tensor(lam[:, 4:5], lam[:, 3:4], lam[:, 2:3], ALU.subtract))
                step(dve.tensor_scalar(lam[:, 5:6], lam[:, 4:5], -lam_init, None, ALU.add))
                dve.wait_ge(*ready("pe_job", "mod", l))
                for seg_, c0 in ((0, 0), (1, 24)):
                    b0 = poff["b_mod"][0] + c0
                    step(dve.tensor_tensor(modT[:, 16 * seg_:16 * seg_ + 16], psum[:, 0, 16 * seg_:16 * seg_ + 16],
                                           par[:, l, b0:b0 + 16], ALU.add))
                for i, name in enumerate(("norm_mix", "norm_ffn")):
                    step(dve.scalar_tensor_tensor(out=Amod[:, i, :], in0=modT[:, 16 * i + 8:16 * i + 16], scalar=1.0,
                                                  in1=prm(l, name, 0, 8), op0=ALU.add, op1=ALU.mult))
                dve.wait_ge(*ready("rows", "bmod", l))
                for i in range(2):
                    for h in range(2):
                        hs = slice(h * 512, h * 512 + 512)
                        step(dve.tensor_tensor(grow[:, i, hs], psum[:, 1 + 2 * i + h, :], rows[:, i, hs], ALU.add))
                barrier()
                rms_rows("mix", l)
                modulate("mix", l, 0)
                barrier()
                for i in QK:
                    n = QK.index(i)
                    g = gain(("moba_q", "moba_k", "diff_q", "diff_k")[n // 2])
                    b = n % 2
                    q4 = tq[:, b, :].rearrange("p (h d) -> p h d", d=HD)
                    s8, r8, i8 = (v[:, 8 * b:8 * b + 8] for v in (ss16, rt16, ri16))
                    dve.wait_ge(*ready("act", "sq", l, i))
                    step(dve.tensor_reduce(s8, tsq[:, b, :].rearrange("p (h d) -> p h d", d=HD), AX, ALU.add),
                         "headsum", l, i)
                    dve.wait_ge(*ready("act", "headroot", l, i))
                    step(dve.reciprocal(i8, r8))
                    if n >= 2:
                        dve.wait_ge(*ready("pe_job", "qt", l, QK[n - 2]))
                    step(dve.tensor_tensor(q4, psum[:, i % 4, :].rearrange("p (h d) -> p h d", d=HD),
                                           i8.unsqueeze(2).broadcast_to([P, 8, HD]), ALU.mult), "normed", l, i)
                    step(dve.tensor_tensor(q4, q4, g.unsqueeze(1).broadcast_to([P, 8, HD]), ALU.mult))
                    qr = tq[:, b, :].rearrange("p (t h d) -> p t h d", t=NT, d=HD)
                    x1, x2 = qr[:, :, :, 0:8], qr[:, :, :, 8:16]
                    rp = [rope[:, k, :].rearrange("p (t h d) -> p t h d", t=NT, d=ROPE_HALF) for k in range(6)]
                    for t in range(NT):
                        c_, s_ = (v[:, t, :].unsqueeze(1).broadcast_to([P, 4, 8]) for v in (cosb, sinb))
                        step(dve.tensor_tensor(rp[0][:, t], x1[:, t], c_, ALU.mult))
                        step(dve.tensor_tensor(rp[1][:, t], x2[:, t], s_, ALU.mult))
                        step(dve.tensor_tensor(rp[2][:, t], x2[:, t], c_, ALU.mult))
                        step(dve.tensor_tensor(rp[3][:, t], x1[:, t], s_, ALU.mult))
                        step(dve.tensor_tensor(x1[:, t], rp[0][:, t], rp[1][:, t], ALU.subtract))
                        step(dve.tensor_tensor(x2[:, t], rp[2][:, t], rp[3][:, t], ALU.add), "roped", l, i)
                barrier()
                attention(l, "b2", Sm2)
                for t in range(NT):
                    step(dve.tensor_tensor(ys_tmp[:, 0, :], om[:, t, :], om[:, t, :], ALU.mult))
                    step(dve.tensor_reduce(ss16[:, 0:8], ys_tmp[:, 0, 0:512].rearrange("p (h d) -> p h d", d=HD),
                                           AX, ALU.add))
                    step(dve.tensor_reduce(ss16[:, 8:12], ys_tmp[:, 0, 512:1024].rearrange("p (h d) -> p h d", d=P),
                                           AX, ALU.add), "outsum", l, t)
                    dve.wait_ge(*ready("act", "outroot", l, t))
                    step(dve.reciprocal(ri16[:, 0:12], rt16[:, 0:12]))
                    step(dve.tensor_scalar(ri16[:, 8:12], ri16[:, 8:12], 1.0 - lam_init, None, ALU.mult))
                    for c0, nh, d, r0, name in ((0, 8, HD, 0, "moba_out"), (512, 4, P, 8, "diff_sub")):
                        o4 = om[:, t, c0:c0 + 512].rearrange("p (h d) -> p h d", d=d)
                        step(dve.tensor_tensor(o4, o4, ri16[:, r0:r0 + nh].unsqueeze(2).broadcast_to([P, nh, d]),
                                               ALU.mult))
                        step(dve.tensor_tensor(o4, o4, gain(name).unsqueeze(1).broadcast_to([P, nh, d]), ALU.mult))
                barrier()
                dve.wait_ge(*ready("pe_job", "out2", l, 3))
                for t in range(NT):
                    for h in range(2):
                        hs = slice(h * 512, h * 512 + 512)
                        step(dve.tensor_tensor(tok_scaled[:, t, hs], psum[:, 4 + 2 * t + h, :], grow[:, 0, hs],
                                               ALU.mult))
                        step(dve.tensor_tensor(x[:, t, hs], x[:, t, hs], tok_scaled[:, t, hs], ALU.add))
                rms_rows("ffn", l)
                modulate("ffn", l, 1)
                barrier()
                ffn("ffn2", l)
                if l == DEPTH - 1:
                    S.also("dve", "x", "end")
                barrier()

        return S


QK = [0, 1, 2, 3, 6, 7, 8, 9]
UNITS1 = [("swa", hp) for hp in range(4)] + [("fox", hp) for hp in range(2)] + [("dsa", hp) for hp in range(2)]
UNITS2 = [("moba", hp) for hp in range(4)] + [("diff", hp) for hp in range(4)]
G = [2, 1, 1, 2, (1, 1, 1, 1, 0), (1, 1, 0, 0), 2, (3, 6)]
assert G[0] + G[1] + G[2] + G[3] + sum(G[4]) + sum(G[5]) + G[6] + len(G[7]) == 16
N_BARRIERS = 1 + DEPTH * 6 + DEPTH * 6


_INS = ["x", "w_in", "swa_sinks", "rwkv_mu", "rwkv_w0", "rwkv_w_up", "rwkv_a0", "rwkv_a_up", "rwkv_g_up",
        "rwkv_k_k", "rwkv_k_a", "rwkv_r_k", "rwkv_gn_g", "rwkv_gn_b", "fox_f_bias", "gate_bias", "w_branch",
        "w_out", "ln_g", "ln_b", "ffn_w1", "ffn_w3", "ffn_w2", "router_w", "router_b", "exp_w1", "exp_w3",
        "exp_w2", "c_2", "positions_2", "w_mod_2", "b_mod_2", "norm_mix_2", "w_in_2", "moba_q_norm_2",
        "moba_k_norm_2", "moba_out_norm_2", "diff_q_norm_2", "diff_k_norm_2", "diff_lambda_2",
        "diff_subln_2", "w_out_2", "norm_ffn_2", "w_gate_2", "w_up_2", "w_down_2"]


def program(arrays, known, bacc):
    nc = bacc.Bacc("TRN2", target_bir_lowering=False, num_devices=1)
    a = {}
    for name in _INS:
        v = arrays["in_" + name]
        a[name] = nc.dram_tensor("in_" + name, v.shape, mybir.dt.from_np(v.dtype), kind="ExternalInput").ap()
    out = nc.dram_tensor("out_0", (1, SEQ, D), F32, kind="ExternalOutput").ap()
    return nc, build(nc, a, out, known)


def kernel(**inputs):
    import concourse.bacc as bacc
    from concourse.bass_utils import run_bass_kernel_spmd as run

    arrays = {"in_" + name: np.ascontiguousarray(inputs[name]) for name in _INS}
    _, known = program(arrays, None, bacc)
    nc, _ = program(arrays, known, bacc)
    r = run(nc, [arrays], core_ids=[0])
    return r.results[0]["out_0"]
```

```python
from contextlib import ExitStack, contextmanager
import math

import numpy as np
import concourse.bass as bass
from concourse import mybir

F32 = mybir.dt.float32
U32 = mybir.dt.uint32
I32 = mybir.dt.int32
ALU = mybir.AluOpType
ACT = mybir.ActivationFunctionType
AX = mybir.AxisListType.X

P = 128
D = 1024
KT = D // P
SEQ = 256
NT = SEQ // P
DEPTH = 2
HD = 64
CH = 64
NC = SEQ // CH
FF = 1408
FT = FF // P
STEPS = (FT + 1) // 2
N_EXP = 8
IN_SWA, IN_RWKV, IN_FOX, IN_DSA, IN_GATE = 0, 768, 1792, 2564, 3272
TOPK = 64
TWO_PI_A = 6.28125
TWO_PI_B = float(np.floor((2 * math.pi - TWO_PI_A) * 2.0 ** 21) / 2.0 ** 21)
TWO_PI_C = 2 * math.pi - TWO_PI_A - TWO_PI_B
PI_IN = 3.1415925
ALPHA = (2 * DEPTH) ** 0.25
LN_EPS = 1e-5
GN_EPS = 64e-5
RMS_EPS = 1e-6
SCALE = HD ** -0.5
DECAY = math.exp(-0.5)
NEG = -1e30
TAKEN = -3e38
ROPE_HALF = 8
ROPE_THETA = 500000.0
SLOTS = 6
SLOT = 2048
UNIT = 256
PACK = 3 * P
KEYS = [(0, P), (P, SEQ)]
MOD_UNITS = 6 * D // UNIT

PARAMS = [("mu", 8), ("w0", 2), ("a0", 2), ("k_k", 2), ("k_a", 2), ("r_k", 2), ("gn_g", 2), ("gn_b", 2),
          ("gate_b", 32), ("norm_mix", 8), ("norm_ffn", 8), ("b_mod", 48)]
N_PAR = sum(n for _, n in PARAMS)
N_PARAM_LOADS = DEPTH * (len(PARAMS) + 5) + 4
GAINS = [("moba_q", 64), ("moba_k", 64), ("diff_q", 64), ("diff_k", 64), ("moba_out", 64), ("diff_sub", 128),
         ("lambda", 256)]


CREDITED = ("x_pe", "x_act", "x_dve")


class Signals:

    def __init__(self, nc, ctx, known):
        self.nc, self.ctx = nc, ctx
        self.sems, self.count, self.value, self.per_turn = {}, {}, {}, {}
        self.known = known
        self.turn = None

    def sem(self, kind):
        if kind not in self.sems:
            self.sems[kind] = self.ctx.enter_context(self.nc.semaphore(kind))
        return self.sems[kind]

    def made(self, kind, *key, by=1):
        self.count[kind] = self.count.get(kind, 0) + by
        self.value[(kind, key)] = (self.count[kind], self.turn is not None)
        return self.sem(kind), by

    def also(self, kind, *key):
        self.value[(kind, key)] = (self.count[kind], self.turn is not None)

    def credit(self, kind):
        return self.known.per_turn[kind] if self.known and kind in CREDITED else 0

    def ready(self, kind, *key, back=0):
        value, looped = self.known.value[(kind, key)] if self.known else (1, False)
        if looped:
            step = self.known.per_turn[kind]
            return self.sem(kind), self.turn * step + (value + self.credit(kind) - back * step)
        return self.sem(kind), value

    @contextmanager
    def turns(self, eng, n, inner=None):
        before = dict(self.count)
        with eng.Fori(0, n) as turn:
            if inner is None:
                self.turn = turn
                yield turn
            else:
                with eng.Fori(0, inner) as place:
                    self.turn = turn * inner + place
                    yield place
        self.turn = None
        for kind, c in self.count.items():
            if c > before.get(kind, 0):
                self.per_turn[kind] = c - before.get(kind, 0)


def build(nc, a, out, known):
    with ExitStack() as ctx:
        S = Signals(nc, ctx, known)
        made, ready = S.made, S.ready

        def sb(name, shape, dt=F32):
            return ctx.enter_context(nc.sbuf_tensor(name, shape, dt))

        ring = sb("ring", [P, SLOTS, SLOT])
        x = sb("x", [P, NT, D])
        xT = sb("xT", [P, KT, SEQ])
        oT = sb("oT", [P, 10, SEQ])
        rows = sb("rows", [P, 2, D])
        par = sb("par", [P, DEPTH, sum(n for _, n in PARAMS)])
        lora = sb("lora", [P, DEPTH, 2, 256])
        sinks = sb("sinks", [P, DEPTH, 8])
        fbias = sb("fbias", [4, DEPTH])
        router = sb("router", [P, KT, N_EXP])
        router_b = sb("router_b", [P, N_EXP])
        cond = sb("cond", [P, KT])
        pos = sb("pos", [P, NT], I32)
        ident = sb("ident", [P, P])
        block_ones = sb("block_ones", [P, P])
        mask = sb("mask", [P, 3, PACK])
        ones = sb("ones", [P, P])
        tri = sb("tri", [P, 2, CH])
        level = sb("level", [P, 6, CH])
        level0 = sb("level0", [P, CH])
        eye = sb("eye", [P, CH])
        chunk_gate = sb("chunk_gate", [P, SEQ])
        eps = sb("eps", [P, 4])
        invf = sb("invf", [P, ROPE_HALF])
        small = sb("small", [P, 256])
        ARENA = 27700
        arena = sb("arena", [P, ARENA])
        psum = ctx.enter_context(nc.psum_tensor("psum", [P, 8, 512], F32))

        top = [0]

        def view(*shape, parts=P, at=None):
            n = int(np.prod(shape))
            o = top[0] if at is None else at
            if at is None:
                top[0] += n
            assert o + n <= ARENA, (o, n)
            v = arena[0:parts, o:o + n]
            names = "abcd"[:len(shape)]
            if len(shape) > 1:
                v = v.rearrange("p (%s) -> p %s" % (" ".join(names), " ".join(names)),
                                **{k: s for k, s in zip(names, shape)})
            return v

        swa_q, swa_k, swa_v = view(4, SEQ), view(2, SEQ), view(NT, P)
        fox_q, fox_k, fox_v = view(2, SEQ), view(2, SEQ), view(NT, 256)
        fox_f = view(1, SEQ, parts=4)
        dsa_q, dsa_k, dsa_qi, dsa_ki = view(2, SEQ), view(SEQ), view(2, SEQ), view(SEQ)
        dsa_v, dsa_wi = view(NT, HD), view(NT, 4)
        branch_end = top[0]
        raw_at = top[0]
        raw = view(8, SEQ + 1)
        AB = view(2 * NC, 2, CH, at=raw_at)
        mix = view(8, SEQ)
        mix_at = raw_at + 8 * (SEQ + 1)
        T, TT = view(2 * NC, CH, at=top[0]), view(2 * NC, CH, at=top[0] + 2 * SEQ)
        Bh, kh = view(2, SEQ), view(2, SEQ)
        U = view(2 * NC, CH, at=top[0])
        kk, sw, L, Wc = [view(2, SEQ) for _ in range(4)]
        BT = [view(2 * NC, CH, at=o) for o in (mix_at, mix_at + 512, top[0], top[0] + 512, top[0] + 1024)]
        Wp, Wi, av, gv, sq, kp = [view(2, SEQ) for _ in range(6)]
        KR = view(2, NC, 2, CH)
        GR = view(2 * NC, 2, CH)
        tanh_w = view(SEQ, at=top[0])
        tokV, tokB, tokK = [view(2 * NC, CH) for _ in range(3)]
        RS, SA = view(2, 2, CH, at=mix_at + 6 * SEQ), view(2, 2, CH, at=mix_at + 7 * SEQ)
        Z = view(2, 2, CH)
        yv, yn = L, sw
        gate_at = ARENA - 4 * KT * SEQ
        assert top[0] <= gate_at, top[0]
        par_rows = view(DEPTH, P, at=ARENA - DEPTH * P)
        zb = view(4, KT, SEQ, at=gate_at)
        top[0] = branch_end
        fox_t = view(4, SEQ)
        score, picked, part = view(SEQ), view(NT, SEQ), view(SEQ)
        dsa_bias = view(PACK)
        Sm = view(4, 2, PACK)
        PT = view(2, 2, PACK)
        assert top[0] <= gate_at - 5 * D, top[0]
        wb_first = view(5, D, at=gate_at - 5 * D)
        top[0] = 0
        wb_last = view(5, D)
        prod = view(2, 2, 512)
        mergedT = view(KT, SEQ, at=10 * D)
        top[0] = 0
        sil = view(2, 512)
        gT = view(3, 512)
        xgT, yb = view(KT, P), view(D)
        gather, scatter, scatterT = view(NT, P), view(NT, P), view(NT, P)
        acc = view(NT, D)
        number, before = view(P), view(P)
        number_i = view(P).bitcast(I32)
        onehot, ranked, assigned = view(NT, 2, N_EXP), view(NT, 2, N_EXP), view(NT, N_EXP)
        rank, over, turn_of, slot1, found, found_slot, found_wt = [view(NT, 2) for _ in range(7)]
        most, slot_now, wt_now, rounds = view(2), view(NT), view(NT), view(2)
        rounds_i = view(2).bitcast(I32)
        stat = small[:, 0:24].rearrange("p (t h s) -> p t h s", t=NT, h=2)
        mv = small[:, 24:28].rearrange("p (t s) -> p t s", t=NT)
        sd, rs = small[:, 28:30], small[:, 30:32]
        logit = small[:, 32:48].rearrange("p (t e) -> p t e", t=NT)
        top8 = small[:, 48:64].rearrange("p (t e) -> p t e", t=NT)
        idx8 = small[:, 64:80].rearrange("p (t e) -> p t e", t=NT)
        idxf = small[:, 80:96].rearrange("p (t e) -> p t e", t=NT)
        wts = small[:, 96:100].rearrange("p (t e) -> p t e", t=NT)
        e2, turn_no = small[:, 100:102], small[:, 102:103]
        comb, picks = small[:, 104:106], small[:, 106:110].rearrange("p (t e) -> p t e", t=NT)
        mx, nm, den, es, rc = [small[:, 208 + 8 * i:216 + 8 * i].rearrange("p (b q h) -> p b q h", b=2, q=NT)
                               for i in range(5)]
        m8 = small[:, 144:152]
        ss16, rt16, ri16 = [small[:, 152 + 16 * i:168 + 16 * i] for i in range(3)]
        lam = small[:, 200:208]
        top[0] = 3000
        gains = view(sum(n for _, n in GAINS))
        grow = view(2, D)
        modT, Amod = view(32), view(2, KT)
        cosb, sinb = view(NT, ROPE_HALF), view(NT, ROPE_HALF)
        ang = view(4, NT * ROPE_HALF)
        vtm, om = view(NT, D), view(NT, D)
        tok_scaled = vtm
        qT = view(16, SEQ)
        ys_tmp = view(NT, D, at=top[0])
        tq, tsq = view(2, 512), view(2, 512)
        rope = view(6, NT * 4 * ROPE_HALF)
        angi = ang[:, 3, :].bitcast(I32)
        Sm2, PT2 = view(4, 2, PACK), view(2, 2, PACK)
        mod_at = ARENA - 3 * SLOT - MOD_UNITS * UNIT
        modw = view(3, SLOT, at=mod_at)
        pmod = view(MOD_UNITS, UNIT, at=mod_at + 3 * SLOT)
        ys_tmp = tok_scaled
        oT8 = oT[:, 0:8, :]

        def units_of(seg):
            return UNITS1 if seg == "b1" else UNITS2

        def o_bank(seg, i):
            return 6 if seg == "b1" else 6 + i % 2

        def in_bank(i):
            return (4 + i) % 8

        def in_copied(ready, l, i):
            return ready("act" if i in (0, 1, 3, 5, 7, 9, 10) else "dve", "in", l, i)

        poff = {}
        o = 0
        for name, n in PARAMS:
            poff[name] = (o, n)
            o += n
        goff = {}
        o = 0
        for name, n in GAINS:
            goff[name] = (o, n)
            o += n

        def prm(l, name, i=0, n=1):
            return par[:, l, poff[name][0] + i:poff[name][0] + i + n]

        def gain(name):
            return gains[:, goff[name][0]:goff[name][0] + goff[name][1]]

        def kview(w):
            return w.rearrange("(k p) c -> p k c", p=P)

        def hb(h):
            return slice(HD * (h % 2), HD * (h % 2) + HD)

        units1 = ([IN_SWA + UNIT * i for i in range(3)] + [IN_RWKV + UNIT * i for i in range(4)]
                  + [IN_FOX + UNIT * i for i in range(3)] + [IN_DSA, None, IN_DSA + 384])

        def unit_list(segment):
            kind, l = segment
            if kind == "in":
                w = kview(a["w_in"][l])
                for i, c in enumerate(units1):
                    if c is None:
                        yield ("in", l, i), [(0, 128, w[:, :, IN_DSA + 256:IN_DSA + 384]),
                                             (128, 68, w[:, :, IN_DSA + 640:IN_DSA + 708]),
                                             (196, 4, w[:, :, IN_FOX + 768:IN_FOX + 772])]
                    else:
                        yield ("in", l, i), [(0, 256, w[:, :, c:c + 256])]
            elif kind == "gate":
                w = kview(a["w_in"][l])
                for cp in range(4):
                    for b in range(4):
                        c = IN_GATE + b * D + cp * 256
                        yield ("gate", l, cp, b), [(0, 256, w[:, :, c:c + 256])]
            elif kind in ("out", "out2"):
                w = kview(a["w_out" if kind == "out" else "w_out_2"][l])
                for k in range(4):
                    yield (kind, l, k), [(None, D, w[:, 2 * k:2 * k + 2, :])]
            elif kind == "in2":
                w = kview(a["w_in_2"][l])
                for i in range(12):
                    yield ("in2", l, i), [(0, 256, w[:, :, UNIT * i:UNIT * i + 256])]

        def ffn_units(name, w1, w3, w2):
            for s in range(STEPS):
                n = min(2, FT - 2 * s)
                yield (name, "w1", s), [(0, n * P, kview(w1)[:, :, s * 256:s * 256 + n * P])]
                yield (name, "w3", s), [(0, n * P, kview(w3)[:, :, s * 256:s * 256 + n * P])]
                yield (name, "w2", s), [(None, D, kview(w2)[:, 2 * s:2 * s + n, :])]

        segments = []
        for l in range(DEPTH):
            segments += [("in", l), ("gate", l), ("out", l), ("ffn1", l) if l == 0 else ("moe", l)]
        for l in range(DEPTH):
            segments += [("in2", l), ("out2", l), ("ffn2", l)]

        def piece_weights(seg, l, p):
            if seg == "ffn1":
                return [a["ffn_w1"][0][:, p * FF:(p + 1) * FF], a["ffn_w3"][0][:, p * FF:(p + 1) * FF],
                        a["ffn_w2"][0][p * FF:(p + 1) * FF, :]]
            if seg == "ffn2":
                return [a["w_gate_2"][l][:, p * FF:(p + 1) * FF], a["w_up_2"][l][:, p * FF:(p + 1) * FF],
                        a["w_down_2"][l][p * FF:(p + 1) * FF, :]]
            return [a["exp_w1"][0, p], a["exp_w3"][0, p], a["exp_w2"][0, p]]

        def slot_of():
            n = [0]

            def take():
                n[0] += 1
                return (n[0] - 1) % SLOTS
            return take

        def barrier_of(eng):
            n = [0]

            def come():
                n[0] += 1
                eng.drain()
                eng.sem_inc(S.sem("phase_over"), 1)
                eng.wait_ge(S.sem("phase_over"), 4 * n[0])
            return come

        block = ctx.enter_context(nc.Block())

        def gate_place(j):
            return j // 4, j % 4

        @block.sync
        def _(sp):
            take = slot_of()
            order = []
            sp.dma_start(x[:], a["x"][0].rearrange("(t p) d -> p t d", p=P)).then_inc(*made("x_in", by=16))

            def load(unit, parts, loop=""):
                slot = take()
                if len(order) >= SLOTS:
                    old, old_back = order[-SLOTS]
                    sp.wait_ge(*ready("x_pe" if loop else "pe_job", "unit", *old, back=old_back))
                for c0, n, src in parts:
                    k = src.shape[1]
                    if c0 is None:
                        dst = ring[:, slot, 0:k * D].rearrange("p (k c) -> p k c", k=k)
                    else:
                        dst = ring[:, slot, :].rearrange("p (k c) -> p k c", k=KT)[:, :, c0:c0 + n]
                    inc = made(loop + "slot%d" % slot, "unit", *unit, by=16)
                    sp.dma_start(dst, src).then_inc(*inc)
                order.append((unit, 0))

            for seg, l in segments:
                if seg in ("ffn1", "ffn2"):
                    for p in range(2):
                        for unit, parts in ffn_units((seg, l, p), *piece_weights(seg, l, p)):
                            load(unit, parts)
                elif seg == "moe":
                    sp.wait_ge(*ready("pe_job", "unit", *order[-1][0]))
                    sp.wait_ge(*ready("dve", "rounds"))
                    n_rounds = sp.value_load(rounds_i[0:1, 0:1], min_val=1, max_val=2)
                    with S.turns(sp, n_rounds, N_EXP) as e:
                        here = list(ffn_units(("moe", l), a["exp_w1"][0, e], a["exp_w3"][0, e], a["exp_w2"][0, e]))
                        del order[:]
                        order.extend([(unit, 1) for unit, _ in here[-SLOTS:]])
                        for unit, parts in here:
                            load(unit, parts, "x_")
                    sp.wait_ge(S.sem("phase_over"), 4 * 2 * BARRIERS_1)
                    del order[:]
                else:
                    for unit, parts in unit_list((seg, l)):
                        load(unit, parts)
            sp.wait_ge(*ready("dve", "x", "end"))
            sp.dma_start(out[0].rearrange("(t p) d -> p t d", p=P), x[:]).then_inc(S.sem("stored"), 16)
            sp.wait_ge(S.sem("stored"), 16)

        @block.gpsimd
        def _(pool):
            barrier = barrier_of(pool)

            def step(ins):
                ins.then_inc(*made("pool"))
                pool.wait_ge(S.sem("pool"), S.count["pool"])

            def fill_where(t, pattern, cm, base, fill, op=ALU.not_equal):
                step(pool.affine_select(out=t, in_=t, compare_op=op, fill=fill, base=base,
                                        pattern=pattern, channel_multiplier=cm))

            step(pool.memset(ident[:], 0.0))
            pool.affine_select(out=ident[:], in_=ident[:], compare_op=ALU.not_equal, fill=1.0, base=0,
                               pattern=[[-1, P]], channel_multiplier=1).then_inc(*made("pool", "ident"))
            for t in (block_ones, eye, level, level0):
                step(pool.memset(t[:], 0.0))
            step(pool.memset(ones[:], 1.0))
            step(pool.memset(chunk_gate[:], 1.0))
            step(pool.memset(chunk_gate[:, 0:SEQ:CH], 0.0))
            for i in range(2):
                step(pool.memset(block_ones[HD * i:HD * i + HD, HD * i:HD * i + HD], 1.0))
            step(pool.memset(tri[:], 1.0))
            for p0 in (0, CH):
                ps = slice(p0, p0 + CH)
                fill_where(eye[ps, :], [[-1, CH]], 1, 0, 1.0)
                fill_where(tri[ps, 0, :], [[1, CH]], -1, -1, 0.0, ALU.is_ge)
                fill_where(tri[ps, 1, :], [[1, CH]], -1, 0, 0.0, ALU.is_ge)
                for l in range(6):
                    B = 2 ** l
                    v = level[ps, l, :].rearrange("s (k h j) -> s k h j", h=2, j=B)[:, :, 1, :]
                    step(pool.memset(v, -1.0))
                    fill_where(v, [[-2 * B, CH // (2 * B)], [0, B]], 1, 0, 0.0, ALU.is_ge)
                    fill_where(v, [[2 * B, CH // (2 * B)], [0, B]], -1, B - 1, 0.0, ALU.is_ge)
                fill_where(level0[ps, 0:CH:2], [[-2, CH // 2]], 1, -1, -1.0)
            for i, e in enumerate((LN_EPS, GN_EPS, RMS_EPS, 1e-12)):
                step(pool.memset(eps[:, i:i + 1], e))
            for i in range(ROPE_HALF):
                inv = np.float32(ROPE_THETA) ** (-np.float32(2 * i) / np.float32(2 * ROPE_HALF))
                step(pool.memset(invf[:, i:i + 1], float(np.float32(inv))))
            step(pool.memset(mask[:], NEG))
            step(pool.memset(mask[:, 1, :], 0.0))
            for kind in (0, 2):
                for t in range(NT):
                    for half in range(2):
                        c = 2 * t + half
                        lo = max(0, c - 2) * CH if kind == 0 else 0
                        k0 = KEYS[t][0]
                        step(pool.memset(mask[HD * half:HD * half + HD, kind, k0 + lo:k0 + (c + 1) * CH], 0.0))
            for t in range(NT):
                k0, nk = KEYS[t]
                fill_where(mask[:, 1, k0:k0 + nk], [[-1, nk]], 1, P * t, NEG, ALU.is_ge)
            def modulation(l):
                w_mod = kview(a["w_mod_2"][l])

                def fetch(j):
                    pool.dma_start(modw[:, j % 3, :].rearrange("p (k c) -> p k c", k=KT),
                                   w_mod[:, :, j * UNIT:(j + 1) * UNIT]).then_inc(S.sem("modw%d" % (j % 3)), 16)

                fetch(0)
                fetch(1)
                for j in range(MOD_UNITS):
                    if j + 2 < MOD_UNITS:
                        if j >= 1:
                            pool.wait_ge(*ready("pool", "mod", l, j - 1))
                        fetch(j + 2)
                    pool.wait_ge(S.sem("modw%d" % (j % 3)), 16 * (MOD_UNITS // 3 * l + j // 3 + 1))
                    w = modw[:, j % 3, :]
                    step(pool.tensor_tensor(w.rearrange("p (k c) -> p k c", k=KT),
                                            w.rearrange("p (k c) -> p k c", k=KT),
                                            cond[:].unsqueeze(2).broadcast_to([P, KT, UNIT]), ALU.mult))
                    step(pool.tensor_tensor(w[:, 0:1024], w[:, 0:1024], w[:, 1024:2048], ALU.add))
                    step(pool.tensor_tensor(w[:, 0:512], w[:, 0:512], w[:, 512:1024], ALU.add))
                    pool.tensor_tensor(pmod[:, j, :], w[:, 0:256], w[:, 256:512], ALU.add)\
                        .then_inc(*made("pool", "mod", l, j))

            for kind in CREDITED:
                if known:
                    pool.sem_inc(S.sem(kind), known.per_turn[kind])
            for b in range(N_BARRIERS):
                barrier()
                if b == 2 * BARRIERS_1 - 2:
                    step(pool.iota(number_i[:], [[1, P]], base=0, channel_multiplier=0))
                    step(pool.tensor_copy(number[:], number_i[:]))
                    step(pool.memset(before[:], 1.0))
                    pool.affine_select(out=before[:], in_=before[:], compare_op=ALU.is_ge, fill=0.0, base=-1,
                                       pattern=[[1, P]], channel_multiplier=-1).then_inc(*made("pool", "numbers"))
                    modulation(0)
                if b == 2 * BARRIERS_1 + 1:
                    modulation(1)

        @block.scalar
        def _(act):
            barrier = barrier_of(act)

            def step(ins, *key):
                ins.then_inc(*made("act", *key))

            def dma(dst, src):
                act.dma_start(dst, src).then_inc(*made("param", by=16))

            def load_rows(l, g, b, *key):
                for i, r in enumerate((g, b)):
                    act.dma_start(rows[:, i, :], r.rearrange("(o d) -> o d", o=1).broadcast_to([P, D]))\
                        .then_inc(*made("rows", *key, by=16))

            def transposed(tag):
                for j in range(4):
                    act.wait_ge(*ready("pe_job", "xt", *tag, j))
                    step(act.copy(xT[:, 2 * j:2 * j + 2, :], bank_view(tag, j)), "xt", *tag, j)

            def bank_view(tag, j):
                return psum[:, j, :].rearrange("p (a b) -> p a b", a=2)

            def ffn_piece(name, l, p, key, back):
                for s in range(STEPS):
                    n = 256 * min(2, FT - 2 * s)
                    act.wait_ge(*ready("pe_job", "h1", *key, s))
                    if not (p == 0 and s < 2):
                        act.wait_ge(*ready("dve", "g", *(key if s >= 2 else back[0]), (s - 2) % STEPS,
                                           back=0 if s >= 2 else back[1]))
                    step(act.activation(sil[:, s % 2, 0:n], psum[:, (2 * s) % 4, 0:n], ACT.Silu),
                         "silu", *key, s)

            def ffn(seg, l):
                if seg == "moe":
                    act.wait_ge(*ready("pe_job", "gather0"))
                    step(act.copy(xgT[:].rearrange("p (b k) c -> p b (k c)", b=2), psum[:, 6:8, :]), "xg0")
                    act.wait_ge(*ready("dve", "rounds"))
                    n_turns = act.value_load(rounds_i[0:1, 1:2], min_val=N_EXP, max_val=2 * N_EXP)
                    with S.turns(act, n_turns):
                        for s in range(STEPS):
                            n = P * min(2, FT - 2 * s)
                            act.wait_ge(*ready("x_pe", "h1", s))
                            act.wait_ge(*ready("x_dve", "g", (s - 2) % STEPS, back=0 if s >= 2 else 1))
                            act.activation(sil[:, s % 2, 0:n], psum[:, (2 * s) % 4, 0:n], ACT.Silu)\
                                .then_inc(*made("x_act", "silu", s))
                        act.wait_ge(*ready("x_pe", "down", STEPS - 1))
                        act.copy(yb[:].rearrange("p (b c) -> p b c", b=2), psum[:, 4:6, :])\
                            .then_inc(*made("x_act", "yb"))
                        act.wait_ge(*ready("x_pe", "gather"))
                        act.copy(xgT[:].rearrange("p (b k) c -> p b (k c)", b=2), psum[:, 6:8, :])\
                            .then_inc(*made("x_act", "xg"))
                else:
                    for p in range(2):
                        ffn_piece(seg, l, p, (seg, l, p), ((seg, l, p - 1), 0))

            def gates(l, n, banks):
                for _ in range(n):
                    j = gates_done[0] % 16
                    gates_done[0] += 1
                    cp, b = gate_place(j)
                    act.wait_ge(*ready("pe_job", "gate", l, j))
                    for i in range(2):
                        c = 2 * cp + i
                        step(act.activation(zb[:, b, c, :], psum[:, banks[j % len(banks)], i * 256:i * 256 + 256],
                                            ACT.Identity, bias=prm(l, "gate_b", b * KT + c)), "zb", l, j)

            gates_done = [0]

            def norm_roots(*key):
                for t in range(NT):
                    act.wait_ge(*ready("dve", "var", *key, t))
                    step(act.activation(sd[:, t:t + 1], mv[:, t, 1:2], ACT.Sqrt, bias=eps[:, 0:1]), "sd", *key, t)

            def attention(l, units, Sb, PTb, seg):
                n = len(units)
                for i in range(n + 2):
                    if i < n:
                        u, b = units[i], i % 2
                        act.wait_ge(*ready("dve", "nm", seg, l, u))
                        for qt, (k0, nk) in enumerate(KEYS):
                            for h in range(2):
                                s = Sb[:, i % 4, h, k0:k0 + nk]
                                step(act.activation(s, s, ACT.Exp, bias=nm[:, b, qt, h:h + 1],
                                                    accum_out=den[:, b, qt, h:h + 1]), "exp", seg, l, u)
                        if u[0] == "swa":
                            step(act.activation(es[:, b], es[:, b], ACT.Exp), "exp", seg, l, u)
                    if seg == "b1" and i in G[7]:
                        gates(l, 1, (7,))
                    if i >= 2:
                        turned(units[i - 2], l, seg, i - 2, PTb)

            def turned(v, l, seg, i, PTb):
                act.wait_ge(*ready("pe_job", "pt", seg, l, v))
                if i >= 2:
                    act.wait_ge(*ready("pe_job", "o", seg, l, units_of(seg)[i - 2]))
                nh = 1 if v[0] == "diff" else 2
                step(act.copy(PTb[:, i % 2, 0:nh, :], psum[:, 4:4 + nh, 0:PACK]), "pt", seg, l, v)

            def load_params():
                act.wait_ge(*ready("slot2", "unit", "in", 0, 2))
                colmaj = {"mu": "rwkv_mu", "w0": "rwkv_w0", "a0": "rwkv_a0", "k_k": "rwkv_k_k", "k_a": "rwkv_k_a",
                          "gn_g": "rwkv_gn_g", "gn_b": "rwkv_gn_b", "norm_mix": "norm_mix_2",
                          "norm_ffn": "norm_ffn_2", "b_mod": "b_mod_2"}
                with nc.allow_non_contiguous_dma(reason="a few vectors of at most 1024 numbers"):
                    for l in range(DEPTH):
                        for name, n in PARAMS:
                            if name == "r_k":
                                src = a["rwkv_r_k"][l].rearrange("(t h) d -> t (h d)", t=2)
                            elif name == "gate_b":
                                src = a["gate_bias"][l].rearrange("b (t p) -> (b t) p", p=P)
                            else:
                                src = a[colmaj[name]][l].rearrange("(t p) -> t p", p=P)
                            c0 = poff[name][0]
                            dma(par_rows[c0:c0 + n, l, :], src)
                        dma(lora[0:64, l, 0, :], a["rwkv_w_up"][l])
                        dma(lora[64:128, l, 0, :], a["rwkv_a_up"][l])
                        dma(lora[:, l, 1, :], a["rwkv_g_up"][l])
                        dma(sinks[:, l, :], a["swa_sinks"][l].rearrange("(o d) -> o d", o=1).broadcast_to([P, 8]))
                        dma(fbias[:, l:l + 1], a["fox_f_bias"][l].rearrange("(d o) -> d o", o=1))
                    dma(router[:], kview(a["router_w"][0]))
                    dma(router_b[:], a["router_b"].broadcast_to([P, N_EXP]))
                    dma(cond[:], a["c_2"].rearrange("o (k p) -> p (o k)", p=P))
                    dma(pos[:], a["positions_2"].rearrange("o (t p) -> p (o t)", p=P))

            for l in range(DEPTH):
                transposed(("b1", l))
                if l == 0:
                    load_params()
                load_rows(l, a["ln_g"][l, 0], a["ln_b"][l, 0], "ln1", l)
                for i, dst in ((0, swa_q[:, 0:2, :]), (1, swa_q[:, 2:4, :]), (3, raw[:, 0:2, 1:]),
                               (5, raw[:, 4:6, 1:]), (7, fox_q[:]), (9, fox_v[:]), (10, dsa_q[:])):
                    act.wait_ge(*ready("pe_job", "in", l, i))
                    step(act.copy(dst, psum[:, in_bank(i), :].rearrange("p (a b) -> p a b", a=2)), "in", l, i)
                if l == 0:
                    act.wait_ge(*ready("pe_job", "par"))
                    step(act.copy(par[:], psum[:, in_bank(14), 0:DEPTH * P].rearrange("p (l c) -> p l c", l=DEPTH)
                                  [:, :, 0:N_PAR]), "par")
                    step(act.activation(cond[:], cond[:], ACT.Silu), "cond")
                barrier()
                gates(l, G[0], (6,))
                act.wait_ge(*ready("dve", "mix", l))
                step(act.activation(tanh_w[0:64, :], mix[0:64, 6, :], ACT.Tanh), "tanh", l)
                step(act.activation(mix[:, 7, :], mix[:, 7, :], ACT.Sigmoid), "sig_g", l)
                act.wait_ge(*ready("pe_job", "w_up", l))
                for ct in range(2):
                    step(act.activation(sw[:, ct, :], psum[:, 0, ct * 256:ct * 256 + 256], ACT.Sigmoid,
                                        bias=prm(l, "w0", ct)), "sw", l)
                act.wait_ge(*ready("pe_job", "a_up", l))
                for ct in range(2):
                    step(act.activation(av[:, ct, :], psum[:, 1, ct * 256:ct * 256 + 256], ACT.Sigmoid,
                                        bias=prm(l, "a0", ct)), "a", l)
                act.wait_ge(*ready("pe_job", "g_up", l))
                step(act.copy(gv[:], psum[:, 2, :].rearrange("p (a b) -> p a b", a=2)), "g", l)
                gates(l, G[1], (6,))
                act.wait_ge(*ready("pe_job", "kk", l))
                step(act.activation(sq[:], psum[:, 3, :].rearrange("p (a b) -> p a b", a=2), ACT.Sqrt,
                                    bias=eps[:, 3:4]), "kk_norm", l)
                gates(l, G[2], (6,))
                act.wait_ge(*ready("dve", "decay", l))
                step(act.activation(Wc[:], L[:], ACT.Exp, scale=-DECAY), "W", l)
                step(act.activation(Wi[:], L[:], ACT.Exp, scale=DECAY), "W", l)
                step(act.activation(Wp[:], Wp[:], ACT.Exp, scale=-DECAY), "W", l)
                for i, t in enumerate((tokV, tokB, tokK)):
                    for g in range(2):
                        if i == 1 and g == 0:
                            gates(l, G[3], (6,))
                        act.wait_ge(*ready("pe_job", "tok", l, i, g))
                        for odd in range(2):
                            step(act.copy(t[hb(odd), 4 * g:4 * g + 4, :],
                                          psum[0:CH, (3, 7)[g], :].rearrange("p (m o d) -> p m o d", m=4, o=2)
                                          [:, :, odd, :]), "tok", l, i, g)
                gates(l, G[10], (6,))
                for lv in range(1, 6):
                    for g in range(2):
                        act.wait_ge(*ready("pe_job", "U", l, lv, g))
                        step(act.copy(U[:, 4 * g:4 * g + 4, :].rearrange("p m c -> p (m c)"),
                                      psum[:, 4 * g, 0:256]), "U", l, lv, g)
                    gates(l, G[4][lv - 1], (6, 7))
                for c in range(NC):
                    act.wait_ge(*ready("pe_job", "X", l, c))
                    step(act.activation(RS[:, c % 2].rearrange("p h v -> p (h v)"), psum[:, 0, 0:P],
                                        ACT.Copy, scale=-1.0), "RS", l, c)
                    gates(l, G[5][c], (6, 7))
                    act.wait_ge(*ready("pe_job", "SA", l, c))
                    step(act.copy(SA[:, c % 2].rearrange("p h v -> p (h v)"), psum[:, 1, 0:P]), "SA", l, c)
                    act.wait_ge(*ready("pe_job", "Y", l, c))
                    step(act.copy(yv[:, :, c * CH:(c + 1) * CH],
                                  psum[:, 2, 0:2 * CH].rearrange("p (a b) -> p a b", a=2)), "y", l, c)
                act.wait_ge(*ready("pe_job", "var", l))
                step(act.activation(sq[:], psum[:, 5, :].rearrange("p (a b) -> p a b", a=2), ACT.Sqrt,
                                    bias=eps[:, 1:2], scale=1.0 / HD), "gn", l)
                gates(l, G[9], (6,))
                barrier()
                w = kview(a["w_branch"][l])
                act.dma_start(wb_first[:], w[:, 0:5, :]).then_inc(*made("wb", l, by=16))
                act.wait_ge(*ready("dve", "fox_abs", l))
                step(act.activation(fox_t[0:4, 1, :], fox_t[0:4, 1, :], ACT.Exp, scale=-1.0), "fox_exp", l)
                act.wait_ge(*ready("act", "fox_exp", l))
                step(act.activation(fox_t[0:4, 1, :], fox_t[0:4, 1, :], ACT.Ln, bias=1.0), "fox_ln", l)
                gates(l, G[6], (0, 1))
                attention(l, UNITS1, Sm, PT, "b1")
                barrier()
                act.dma_start(wb_last[:], w[:, 5:10, :]).then_inc(*made("wb", l, by=16))
                gates(l, G[8], (0, 1))
                act.wait_ge(*ready("act", "zb", l, 15))
                for c in range(KT):
                    step(act.activation(zb[:, :, c, :], zb[:, :, c, :], ACT.Sigmoid), "sig", l, c)
                barrier()
                norm_roots("ln1", l)
                act.wait_ge(*ready("dve", "ln", "ln1", l, NT - 1))
                load_rows(l, a["ln_g"][l, 1], a["ln_b"][l, 1], "ln2", l)
                transposed(("f1", l))
                if l == 1:
                    act.wait_ge(*ready("dve", "router_gap"))
                    step(act.activation(e2, e2, ACT.Exp), "router_exp")
                ffn("ffn1" if l == 0 else "moe", l)
                norm_roots("ln2", l)
                barrier()

            def row_roots(which, l):
                for t in range(NT):
                    if which == "ffn":
                        act.wait_ge(*ready("dve", "res", l, t))
                    step(act.activation(tok_scaled[:, t, :], x[:, t, :], ACT.Square,
                                        accum_out=ss16[:, t:t + 1]), "ms", which, l, t)
                    act.wait_ge(*ready("act", "ms", which, l, t))
                    step(act.activation(sd[:, t:t + 1], ss16[:, t:t + 1], ACT.Sqrt, bias=eps[:, 2:3],
                                        scale=1.0 / D), "rms", which, l, t)

            act.wait_ge(*ready("dve", "angles"))
            step(act.activation(sinb[:].rearrange("p a b -> p (a b)"), ang[:, 1, :], ACT.Sin), "rope")
            step(act.activation(cosb[:].rearrange("p a b -> p (a b)"), ang[:, 2, :], ACT.Sin), "rope")
            for l in range(DEPTH):
                row_roots("mix", l)
                load_rows(l, a["b_mod_2"][l][2 * D:3 * D], a["b_mod_2"][l][5 * D:6 * D], "bmod", l)
                off = 0
                for name, key in (("moba_q_norm_2", 64), ("moba_k_norm_2", 64), ("diff_q_norm_2", 64),
                                  ("diff_k_norm_2", 64), ("moba_out_norm_2", 64), ("diff_subln_2", 128)):
                    act.dma_start(gains[:, off:off + key],
                                  a[name][l].rearrange("(o d) -> o d", o=1).broadcast_to([P, key]))\
                        .then_inc(*made("gains", l, by=16))
                    off += key
                act.dma_start(gains[:, off:off + 256], a["diff_lambda_2"][l].rearrange("i d -> (i d)")
                              .rearrange("(o d) -> o d", o=1).broadcast_to([P, 256])).then_inc(*made("gains", l, by=16))
                act.wait_ge(*ready("dve", "lam_sums", l))
                step(act.activation(lam[:, 2:4], lam[:, 0:2], ACT.Exp), "lam", l)
                for i in range(12):
                    act.wait_ge(*ready("pe_job", "in2", l, i))
                    bank = psum[:, i % 4, :].rearrange("p (t b) -> p t b", t=2)
                    if i in (4, 5, 10, 11):
                        v0 = {4: 0, 5: 256, 10: 512, 11: 768}[i]
                        step(act.copy(vtm[:, :, v0:v0 + 256], bank), "in2", l, i)
                    else:
                        if QK.index(i) >= 2:
                            act.wait_ge(*ready("dve", "headsum", l, QK[QK.index(i) - 2]))
                        n = QK.index(i) % 2
                        step(act.activation(tsq[:, n, :], psum[:, i % 4, :], ACT.Square), "sq", l, i)
                        act.wait_ge(*ready("dve", "headsum", l, i))
                        step(act.activation(rt16[:, 8 * n:8 * n + 8], ss16[:, 8 * n:8 * n + 8], ACT.Sqrt,
                                            bias=eps[:, 2:3], scale=1.0 / HD), "headroot", l, i)
                        act.wait_ge(*ready("pe_job", "qt", l, i))
                        step(act.copy(qT[:, 2 * QK.index(i):2 * QK.index(i) + 2, :],
                                      psum[:, 4 + n, :].rearrange("p (a b) -> p a b", a=2)), "qt", l, i)
                barrier()
                attention(l, UNITS2, Sm2, PT2, "b2")
                for kind, _, nh, d, _ in OUT_NORMS:
                    act.wait_ge(*ready("dve", "outsum", l, kind))
                    step(act.activation(rt16[:, 0:NT * nh], ss16[:, 0:NT * nh], ACT.Sqrt, bias=eps[:, 2:3],
                                        scale=1.0 / d), "outroot", l, kind)
                barrier()
                for j in range(4):
                    act.wait_ge(*ready("pe_job", "xt", "o2", l, j))
                    step(act.copy(oT8[:, 2 * j:2 * j + 2, :], bank_view(None, j)), "xt", "o2", l, j)
                row_roots("ffn", l)
                ffn("ffn2", l)
                barrier()

        @block.tensor
        def _(pe):
            barrier = barrier_of(pe)
            take = slot_of()

            def job(ins, *key):
                ins.then_inc(*made("pe_job", *key))

            def unit(*key):
                slot = take()
                pe.wait_ge(*ready("slot%d" % slot, "unit", *key))
                return ring[:, slot, :]

            def used(*key):
                S.also("pe_job", "unit", *key)

            def turn(src, tag, made_by):
                for t in range(NT):
                    if made_by is not None:
                        pe.wait_ge(*ready("dve", *made_by, t))
                    for j in range(4):
                        for i in range(2):
                            k = 2 * j + i
                            ins = pe.transpose(psum[:, j, i * 256 + t * P:i * 256 + t * P + P],
                                               src[:, t, k * P:k * P + P], ident[:])
                        if t == NT - 1:
                            job(ins, "xt", *tag, j)

            def gates(l, n, banks):
                for _ in range(n):
                    j = gates_done[0] % 16
                    gates_done[0] += 1
                    bank = banks[j % len(banks)]
                    if bank in gate_in:
                        pe.wait_ge(*ready("act", "zb", l, gate_in[bank]))
                    w = unit("gate", l, *gate_place(j))
                    for i in range(2):
                        ins = channel_tile(psum[:, bank, i * 256:i * 256 + 256], w, i * P, P)
                    job(ins, "gate", l, j)
                    used("gate", l, *gate_place(j))
                    gate_in[bank] = j

            gates_done, gate_in = [0], {}

            def channel_tile(dst, w, c0, m, act_t=xT):
                for k in range(KT):
                    ins = pe.matmul(dst, w[:, k * 256 + c0:k * 256 + c0 + m], act_t[:, k, :],
                                    start=(k == 0), stop=(k == KT - 1))
                return ins

            def token_tile(dst, w, c0, n, t, act_t=xT):
                for k in range(KT):
                    ins = pe.matmul(dst, act_t[:, k, t * P:t * P + P], w[:, k * 256 + c0:k * 256 + c0 + n],
                                    start=(k == 0), stop=(k == KT - 1))
                return ins

            def down(key, s, w2):
                n = min(2, FT - 2 * s)
                pe.wait_ge(*ready("dve", "g", *key, s))
                for f in range(n):
                    for t in range(NT):
                        for h in range(2):
                            ins = pe.matmul(psum[:, 4 + 2 * t + h, :],
                                            gT[:, s % 3, f * 256 + t * P:f * 256 + t * P + P],
                                            w2[:, f * D + h * 512:f * D + h * 512 + 512],
                                            start=(s == 0 and f == 0), stop=(s == STEPS - 1 and f == n - 1))
                        if s == STEPS - 1 and f == n - 1 and t == 0:
                            job(ins, "sum", *key)
                job(ins, "down", *key, s)
                used(key, "w2", s)

            def ffn_piece(key, p, back):
                w2 = None
                for s in range(STEPS):
                    n = min(2, FT - 2 * s)
                    for i, (w, what, eng) in enumerate((("w1", "silu", "act"), ("w3", "g", "dve"))):
                        b = (2 * s + i) % 4
                        if s >= 2:
                            pe.wait_ge(*ready(eng, what, *key, s - 2))
                        elif p > 0:
                            pe.wait_ge(*ready(eng, what, *back[0], s + STEPS - 2, back=back[1]))
                        wt = unit(key, w, s)
                        for f in range(n):
                            ins = channel_tile(psum[:, b, f * 256:f * 256 + 256], wt, f * P, P)
                        job(ins, "h1" if i == 0 else "h3", *key, s)
                        used(key, w, s)
                    if s == 1 and p > 0:
                        pe.wait_ge(*ready("dve", "acc", *back[0], back=back[1]))
                    if s >= 1:
                        down(key, s - 1, w2)
                    w2 = unit(key, "w2", s)
                down(key, STEPS - 1, w2)

            def ffn(seg, l):
                if seg == "moe":
                    experts()
                else:
                    for p in range(2):
                        ffn_piece((seg, l, p), p, ((seg, l, p - 1), 0))

            def gather_tokens():
                for k in range(KT):
                    for t in range(NT):
                        ins = pe.matmul(psum[:, 6 + k // 4, (k % 4) * P:(k % 4) * P + P], x[:, t, k * P:k * P + P],
                                        gather[:, t, :], start=(t == 0), stop=(t == NT - 1))
                return ins

            def turn_scatter():
                for t in range(NT):
                    ins = pe.transpose(psum[:, 4, t * P:t * P + P], scatter[:, t, :], ident[:])
                return ins

            def experts():
                pe.wait_ge(*ready("pool", "numbers"))
                pe.wait_ge(*ready("dve", "assigned"))
                pe.matmul(psum[:, 5, 0:8], before[:], assigned[:, 0, :], start=True, stop=True)
                pe.matmul(psum[:, 5, 8:16], ones[:], assigned[:, 0, :], start=True, stop=False)
                pe.matmul(psum[:, 5, 8:16], before[:], assigned[:, 1, :], start=False, stop=True)
                pe.matmul(psum[:, 5, 16:24], ones[:], assigned[:, 0, :], start=True, stop=False)
                job(pe.matmul(psum[:, 5, 16:24], ones[:], assigned[:, 1, :], start=False, stop=True), "ranks")
                pe.wait_ge(*ready("dve", "rounds"))
                pe.wait_ge(*ready("dve", "matrices0"))
                job(gather_tokens(), "gather0")
                job(turn_scatter(), "turned0")
                pe.wait_ge(*ready("act", "xg0"))
                pe.wait_ge(*ready("dve", "scatterT0"))
                n_turns = pe.value_load(rounds_i[0:1, 1:2], min_val=N_EXP, max_val=2 * N_EXP)

                def xjob(ins, *key):
                    ins.then_inc(*made("x_pe", *key))

                def xunit(*key):
                    slot = take()
                    pe.wait_ge(*ready("x_slot%d" % slot, "unit", *key))
                    return ring[:, slot, :]

                def down(s, w2):
                    n = min(2, FT - 2 * s)
                    pe.wait_ge(*ready("x_dve", "g", s))
                    for f in range(n):
                        for h in range(2):
                            ins = pe.matmul(psum[:, 4 + h, :], gT[:, s % 3, f * P:f * P + P],
                                            w2[:, f * D + h * 512:f * D + h * 512 + 512],
                                            start=(s == 0 and f == 0), stop=(s == STEPS - 1 and f == n - 1))
                    xjob(ins, "down", s)
                    S.also("x_pe", "unit", ("moe", 1), "w2", s)

                with S.turns(pe, n_turns):
                    pe.wait_ge(*ready("x_act", "xg", back=1))
                    w2 = None
                    for s in range(STEPS):
                        n = min(2, FT - 2 * s)
                        for i, (w, what, eng) in enumerate((("w1", "silu", "x_act"), ("w3", "g", "x_dve"))):
                            b = (2 * s + i) % 4
                            if s < 2:
                                pe.wait_ge(*ready("x_dve", "acc", s, back=1))
                            else:
                                pe.wait_ge(*ready(eng, what, s - 2))
                            wt = xunit(("moe", 1), w, s)
                            for f in range(n):
                                ins = channel_tile(psum[:, b, f * P:f * P + P], wt, f * P, P, xgT)
                            xjob(ins, "h1" if i == 0 else "h3", s)
                            S.also("x_pe", "unit", ("moe", 1), w, s)
                        if s == 1:
                            pe.wait_ge(*ready("x_act", "yb", back=1))
                        if s >= 1:
                            down(s - 1, w2)
                        w2 = xunit(("moe", 1), "w2", s)
                    down(STEPS - 1, w2)
                    pe.wait_ge(*ready("x_dve", "matrices"))
                    xjob(gather_tokens(), "gather")
                    pe.wait_ge(*ready("x_act", "yb"))
                    for t in range(NT):
                        for h in range(2):
                            ins = pe.matmul(psum[:, 2 * t + h, :], scatterT[:, t, :], yb[:, h * 512:h * 512 + 512],
                                            start=True, stop=True)
                        xjob(ins, "scattered", t)
                    xjob(turn_scatter(), "turned")

            def out_rows(kind, l, src):
                ws = []
                for t in range(NT):
                    for k2 in range(4):
                        if t == 0:
                            ws.append(unit(kind, l, k2))
                        for i in range(2):
                            k = 2 * k2 + i
                            for h in range(2):
                                ins = pe.matmul(psum[:, 4 + 2 * t + h, :], src[:, k, t * P:t * P + P],
                                                ws[k2][:, i * D + h * 512:i * D + h * 512 + 512],
                                                start=(k == 0), stop=(k == KT - 1))
                        if t == NT - 1 and k2 < 3:
                            job(ins, kind, l, "row", k2)
                            used(kind, l, k2)
                    job(ins, kind, l, t)
                used(kind, l, 3)

            def scores(l, seg, i, u):
                kind, hp = u
                if i >= 2:
                    pe.wait_ge(*ready("dve", "sm", seg, l, units_of(seg)[i - 2]))
                q, k = qk_of(kind, hp)
                for h in range(2):
                    hd = 2 * hp + h
                    four = slice(HD * h, HD * h + 4)
                    head = ident[four, HD * h + hd:HD * h + hd + 1]
                    for qt, (k0, nk) in enumerate(KEYS):
                        dst = psum[:, 2 * (i % 2) + h, k0:k0 + nk]
                        ins = pe.matmul(dst, q[hb(h), qt * P:qt * P + P], k[hb(h), 0:nk],
                                        start=True, stop=(kind != "fox"))
                        if kind == "fox":
                            pe.matmul(dst, head.broadcast_to([4, P]), fox_t[four, 1, 0:nk], start=False, stop=False)
                            ins = pe.matmul(dst, fox_t[four, 0, qt * P:qt * P + P], head.broadcast_to([4, nk]),
                                            start=False, stop=True)
                job(ins, "s", seg, l, u)

            def qk_of(kind, hp):
                if kind == "swa":
                    return swa_q[:, hp, :], swa_k[:, hp // 2, :]
                if kind == "fox":
                    return fox_q[:, hp, :], fox_k[:, hp, :]
                if kind == "dsa":
                    return dsa_q[:, hp, :], dsa_k
                if kind == "moba":
                    return qT[:, hp, :], qT[:, 4 + hp, :]
                return qT[:, 8 + hp, :], qT[:, 12 + hp, :]

            def v_of(kind, hp, h, k):
                hd = 2 * hp + h
                if kind == "swa":
                    g = hp // 2
                    return swa_v[:, k, g * HD:g * HD + HD]
                if kind == "fox":
                    return fox_v[:, k, hd * HD:hd * HD + HD]
                if kind == "dsa":
                    return dsa_v[:, k, :]
                if kind == "moba":
                    return vtm[:, k, hd * HD:hd * HD + HD]
                return vtm[:, k, 512 + hp * P:512 + hp * P + P]

            def turn_probs(l, seg, i, u, Sb):
                kind, hp = u
                pe.wait_ge(*ready("dve", "p", seg, l, u))
                if i >= 1:
                    pe.wait_ge(*ready("act", "pt", seg, l, units_of(seg)[i - 1]))
                for h in range(1 if kind == "diff" else 2):
                    for o in range(0, PACK, P):
                        ins = pe.transpose(psum[:, 4 + h, o:o + P], Sb[:, i % 4, h, o:o + P], ident[:])
                job(ins, "pt", seg, l, u)

            def weigh(l, seg, i, u, PTb):
                kind, hp = u
                pe.wait_ge(*ready("act", "pt", seg, l, u))
                lag = 1 if seg == "b1" else 2
                if i >= lag:
                    pe.wait_ge(*ready("dve", "o", seg, l, units_of(seg)[i - lag]))
                b = o_bank(seg, i)
                for qt, (k0, nk) in enumerate(KEYS):
                    for h in range(1 if kind == "diff" else 2):
                        for k in range(qt + 1):
                            probs = PTb[:, i % 2, h, k0 + k * P:k0 + k * P + P]
                            if seg == "b1":
                                ins = pe.matmul(psum[hb(h), b, qt * P:qt * P + P], v_of(kind, hp, h, k), probs,
                                                start=(k == 0), stop=(k == qt))
                            else:
                                n = P if kind == "diff" else HD
                                o = qt * P + h * HD
                                ins = pe.matmul(psum[:, b, o:o + n], probs, v_of(kind, hp, h, k),
                                                start=(k == 0), stop=(k == qt))
                job(ins, "o", seg, l, u)

            def attention(l, seg, Sb, PTb):
                units = units_of(seg)
                n = len(units)
                for i in range(n + 3):
                    if i < n:
                        if units[i] == ("fox", 0):
                            pe.wait_ge(*ready("dve", "fox_c", l))
                        scores(l, seg, i, units[i])
                    if seg == "b1" and i in G[7]:
                        gates(l, 1, (7,))
                    if 2 <= i < n + 2:
                        turn_probs(l, seg, i - 2, units[i - 2], Sb)
                    if i >= 3:
                        weigh(l, seg, i - 3, units[i - 3], PTb)

            def turn_qk(l, i):
                n = QK.index(i)
                pe.wait_ge(*ready("dve", "roped", l, i))
                if n >= 2:
                    pe.wait_ge(*ready("act", "qt", l, QK[n - 2]))
                elif n == 0:
                    pe.wait_ge(*ready("dve", "mod_read", l))
                for ct in range(2):
                    for t in range(NT):
                        ins = pe.transpose(psum[:, 4 + n % 2, ct * 256 + t * P:ct * 256 + t * P + P],
                                           tq[:, n % 2, t * 256 + ct * P:t * 256 + ct * P + P], ident[:])
                job(ins, "qt", l, i)

            for l in range(DEPTH):
                if l == 0:
                    pe.wait_ge(*ready("pool", "ident"))
                    pe.wait_ge(S.sem("x_in"), 16)
                turn(x, ("b1", l), None)
                for i in range(13):
                    b = in_bank(i)
                    if i >= 4 and i < 8:
                        pe.wait_ge(*ready("act", "xt", "b1", l, i - 4))
                    elif i >= 8:
                        pe.wait_ge(*in_copied(ready, l, i - 8))
                    if i == 0:
                        pe.wait_ge(*ready("act", "xt", "b1", l, 3))
                    w = unit("in", l, i)
                    if i == 2:
                        channel_tile(psum[:, b, 0:256], w, 0, P)
                        for t in range(NT):
                            ins = token_tile(psum[:, b, 256 + t * P:256 + t * P + P], w, P, P, t)
                    elif i == 9:
                        for t in range(NT):
                            ins = token_tile(psum[:, b, t * 256:t * 256 + 256], w, 0, 256, t)
                    elif i == 11:
                        channel_tile(psum[0:HD, b, 0:256], w, 0, HD)
                        ins = channel_tile(psum[0:HD, b, 256:512], w, 128, HD)
                        job(ins, "in", l, i)
                        pe.wait_ge(*in_copied(ready, l, 5))
                        b = 1
                        for t in range(NT):
                            token_tile(psum[:, b, t * HD:t * HD + HD], w, HD, HD, t)
                            token_tile(psum[:, b, 128 + t * 4:128 + t * 4 + 4], w, 192, 4, t)
                        ins = channel_tile(psum[0:4, b, 256:512], w, 196, 4)
                        job(ins, "in", l, 13)
                        used("in", l, i)
                        continue
                    else:
                        for j in range(2):
                            ins = channel_tile(psum[:, b, j * 256:j * 256 + 256], w, j * P, P)
                    job(ins, "in", l, i)
                    used("in", l, i)
                if l == 0:
                    pe.wait_ge(*in_copied(ready, l, 6))
                    pe.wait_ge(S.sem("param"), N_PARAM_LOADS * 16)
                    for i in range(DEPTH):
                        ins = pe.transpose(psum[:, in_bank(14), i * P:i * P + N_PAR], par_rows[0:N_PAR, i, :],
                                           ident[0:N_PAR, 0:N_PAR])
                    job(ins, "par")
                barrier()

                gate_in.clear()
                gates(l, G[0], (6,))
                pe.wait_ge(*ready("act", "tanh", l))
                for ct in range(2):
                    ins = pe.matmul(psum[:, 0, ct * 256:ct * 256 + 256], lora[0:64, l, 0, ct * P:ct * P + P],
                                    tanh_w[0:64, :], start=True, stop=True)
                job(ins, "w_up", l)
                for ct in range(2):
                    ins = pe.matmul(psum[:, 1, ct * 256:ct * 256 + 256], lora[64:128, l, 0, ct * P:ct * P + P],
                                    mix[64:128, 6, :], start=True, stop=True)
                job(ins, "a_up", l)
                pe.wait_ge(*ready("act", "sig_g", l))
                for ct in range(2):
                    ins = pe.matmul(psum[:, 2, ct * 256:ct * 256 + 256], lora[:, l, 1, ct * P:ct * P + P],
                                    mix[:, 7, :], start=True, stop=True)
                job(ins, "g_up", l)
                gates(l, G[1], (6,))
                pe.wait_ge(*ready("dve", "kk_sq", l))
                ins = pe.matmul(psum[:, 3, :], block_ones[:], sq[:], start=True, stop=True)
                job(ins, "kk", l)
                gates(l, G[2], (6,))
                pe.wait_ge(*ready("dve", "rkr", l))
                ins = pe.matmul(psum[:, 4, :], block_ones[:], yn[:], start=True, stop=True)
                job(ins, "bonus", l)

                def token_copy(i, g):
                    src = (mix[:, 4:6, :], Bh[:], kh[:])[i]
                    if i > 0:
                        pe.wait_ge(*ready("act", "tok", l, i - 1, g))
                    elif g == 0:
                        pe.wait_ge(*ready("act", "kk_norm", l))
                    for cc in range(2):
                        for ct in range(2):
                            c = 2 * g + cc
                            ins = pe.transpose(psum[0:CH, (3, 7)[g], cc * 256 + ct * P:cc * 256 + ct * P + P],
                                               src[:, ct, c * CH:(c + 1) * CH], ident[:])
                    job(ins, "tok", l, i, g)

                for g in range(2):
                    token_copy(0, g)
                gates(l, G[3], (6,))
                pe.wait_ge(*ready("dve", "scaled", l))
                for i in (1, 2):
                    for g in range(2):
                        token_copy(i, g)
                pe.wait_ge(*ready("dve", "bonus", l))
                pe.wait_ge(*ready("act", "a", l))
                pe.wait_ge(*ready("act", "g", l))
                for c in range(NC):
                    b = (0, 1, 4, 5)[c]
                    for h in range(4):
                        ct, s_ = h // 2, slice(c * CH, (c + 1) * CH)
                        kr = KR[hb(h), ct, c, :, :]
                        pe.matmul(psum[hb(h), b, ct * P:ct * P + P], Bh[hb(h), ct, s_], kr, start=True, stop=True)
                        pe.matmul(psum[hb(h), b, 256 + ct * P:256 + ct * P + P], kh[hb(h), ct, s_], kr,
                                  start=True, stop=True)
                        m = 2 * c + ct
                        ins = pe.matmul(psum[hb(h), 2, m * CH:m * CH + CH], KR[hb(h), ct, c, 0, :],
                                        Bh[hb(h), ct, s_], start=True, stop=True)
                    job(ins, "gram", l, c)
                gates(l, G[10], (6,))
                pe.wait_ge(*ready("act", "tok", l, 2, 1))
                for lv in range(1, 6):
                    for g in range(2):
                        pe.wait_ge(*(ready("dve", "BT", l, 1) if lv == 1 else ready("dve", "T", l, lv - 1, g)))
                        for m in range(4 * g, 4 * g + 4):
                            for odd in range(2):
                                o = (m % 4) * CH
                                ins = pe.matmul(psum[hb(odd), 4 * g, o:o + CH], BT[lv - 1][hb(odd), m, :],
                                                T[hb(odd), m, :], start=True, stop=True)
                        job(ins, "U", l, lv, g)
                    gates(l, G[4][lv - 1], (6, 7))
                    if lv == 1:
                        pe.wait_ge(*ready("dve", "TT", l))
                    for g in range(2):
                        pe.wait_ge(*ready("act", "U", l, lv, g))
                        for m in range(4 * g, 4 * g + 4):
                            for odd in range(2):
                                o = (m % 4) * CH
                                pe.matmul(psum[hb(odd), 4 * g + 1, o:o + CH], TT[hb(odd), m, :], U[hb(odd), m, :],
                                          start=True, stop=True)
                                ins = pe.matmul(psum[hb(odd), 4 * g + 1, 256 + o:256 + o + CH], U[hb(odd), m, :],
                                                TT[hb(odd), m, :], start=True, stop=True)
                        job(ins, "TUT", l, lv, g)
                for c in range(NC):
                    z = (c + 1) % 2
                    if c == 0:
                        pe.wait_ge(*ready("dve", "T", l, 5, 0))
                        pe.wait_ge(*ready("dve", "T", l, 5, 1))
                    else:
                        pe.wait_ge(*ready("dve", "Z", l, c - 1))
                    for h in range(4):
                        ct, r_ = h // 2, hb(h)
                        m, dst = 2 * c + ct, psum[r_, 0, ct * CH:ct * CH + CH]
                        if c > 0:
                            pe.matmul(dst, KR[r_, ct, c, 0, :], Z[r_, z, ct, :], start=True, stop=False)
                        ins = pe.matmul(dst, GR[r_, m, 0, :], tokV[r_, m, :], start=(c == 0), stop=True)
                    job(ins, "X", l, c)
                    gates(l, G[5][c], (6, 7))
                    pe.wait_ge(*ready("act", "RS", l, c))
                    for h in range(4):
                        ct, r_ = h // 2, hb(h)
                        ins = pe.matmul(psum[r_, 1, ct * CH:ct * CH + CH], TT[r_, 2 * c + ct, :],
                                        RS[r_, c % 2, ct, :], start=True, stop=True)
                    job(ins, "SA", l, c)
                    pe.wait_ge(*ready("act", "SA", l, c))
                    if c < NC - 1:
                        for h in range(4):
                            ct, r_ = h // 2, hb(h)
                            m, dst = 2 * c + ct, psum[r_, 3, ct * CH:ct * CH + CH]
                            pe.matmul(dst, tokB[r_, m, :], SA[r_, c % 2, ct, :], start=True, stop=False)
                            ins = pe.matmul(dst, tokK[r_, m, :], tokV[r_, m, :], start=False, stop=True)
                        job(ins, "Znew", l, c)
                    if c >= 1:
                        pe.wait_ge(*ready("act", "y", l, c - 1))
                    for h in range(4):
                        ct, r_ = h // 2, hb(h)
                        m, dst = 2 * c + ct, psum[r_, 2, ct * CH:ct * CH + CH]
                        if c > 0:
                            pe.matmul(dst, Z[r_, z, ct, :], KR[r_, ct, c, 1, :], start=True, stop=False)
                        pe.matmul(dst, SA[r_, c % 2, ct, :], AB[r_, m, 1, :], start=(c == 0), stop=False)
                        ins = pe.matmul(dst, tokV[r_, m, :], GR[r_, m, 1, :], start=False, stop=True)
                    job(ins, "Y", l, c)
                pe.wait_ge(*ready("act", "y", l, NC - 1))
                ins = pe.matmul(psum[:, 4, :], block_ones[:], yv[:], start=True, stop=True)
                job(ins, "mean", l)
                pe.wait_ge(*ready("dve", "y_sq", l))
                ins = pe.matmul(psum[:, 5, :], block_ones[:], sq[:], start=True, stop=True)
                job(ins, "var", l)
                gates(l, G[9], (6,))
                barrier()

                gate_in.clear()
                for qt in range(NT):
                    nk = P * (qt + 1)
                    for h2 in range(2):
                        for h in range(2):
                            ins = pe.matmul(psum[:, 4 + 2 * qt + h, h2 * 256:h2 * 256 + nk],
                                            dsa_qi[hb(h), h2, qt * P:qt * P + P], dsa_ki[hb(h), 0:nk],
                                            start=True, stop=True)
                    job(ins, "idx", l, qt)
                gates(l, G[6], (0, 1))
                for b in (0, 1):
                    if b in gate_in:
                        pe.wait_ge(*ready("act", "zb", l, gate_in[b]))
                pe.wait_ge(*ready("dve", "pick", l, NT - 1))
                attention(l, "b1", Sm, PT)
                barrier()

                gate_in.clear()
                gates(l, G[8], (0, 1))
                pe.wait_ge(*ready("wb", l))
                for c in range(KT):
                    if c >= 2:
                        pe.wait_ge(*ready("dve", "prod", l, c - 2))
                    for b in range(4):
                        rows_of = (range(0, 4), range(4, 6), range(6, 8), range(8, 10))[b]
                        dst = psum[:, 4 + 2 * (c % 2) + b // 2, (b % 2) * 256:(b % 2) * 256 + 256]
                        for k in rows_of:
                            ins = pe.matmul(dst, (wb_first[:, k] if k < 5 else wb_last[:, k - 5])[:, c * P:c * P + P], oT[:, k, :],
                                            start=(k == rows_of[0]), stop=(k == rows_of[-1]))
                    job(ins, "branch", l, c)
                barrier()
                out_rows("out", l, mergedT)
                turn(x, ("f1", l), ("ln", "ln1", l))
                pe.wait_ge(*ready("act", "xt", "f1", l, 3))
                if l == 1:
                    for t in range(NT):
                        for k in range(KT):
                            ins = pe.matmul(psum[:, 4, t * 8:t * 8 + 8], xT[:, k, t * P:t * P + P], router[:, k, :],
                                            start=(k == 0), stop=(k == KT - 1))
                    job(ins, "router")
                    pe.wait_ge(*ready("dve", "router_logits"))
                ffn("ffn1" if l == 0 else "moe", l)
                barrier()

            for l in range(DEPTH):
                for part_, q in [(part_, q) for part_ in (0, 1, 3, 4) for q in range(4)]:
                    col = {0: 0, 1: 8, 3: 16, 4: 24}[part_] + 2 * q
                    for s in range(2):
                        ins = pe.matmul(psum[:, 0, col + s:col + s + 1], pmod[:, 4 * part_ + q, s * P:s * P + P],
                                        ones[:, 0:1], start=True, stop=True)
                job(ins, "mod_columns", l)
                for i, part_ in enumerate((2, 5)):
                    for q in range(4):
                        ins = pe.matmul(psum[:, 4 + 2 * i + q // 2, (q % 2) * 256:(q % 2) * 256 + 256], ones[:],
                                        pmod[:, 4 * part_ + q, :], start=True, stop=True)
                job(ins, "mod", l)
                pe.wait_ge(*ready("dve", "mod_columns", l))
                turn(tok_scaled, ("mix", l), ("xs", "mix", l))
                pe.wait_ge(*ready("dve", "modulated", "mix", l, 3))
                for i in range(12):
                    b = i % 4
                    if i >= 4:
                        j = i - 4
                        pe.wait_ge(*(ready("act", "in2", l, j) if j in (4, 5) else ready("dve", "normed", l, j)))
                    w = unit("in2", l, i)
                    for t in range(NT):
                        ins = token_tile(psum[:, b, t * 256:t * 256 + 256], w, 0, 256, t)
                    job(ins, "in2", l, i)
                    used("in2", l, i)
                    if i >= 1 and (i - 1) in QK:
                        turn_qk(l, i - 1)
                barrier()
                attention(l, "b2", Sm2, PT2)
                barrier()
                turn(om, ("o2", l), None)
                pe.wait_ge(*ready("act", "xt", "o2", l, 3))
                out_rows("out2", l, oT8)
                turn(tok_scaled, ("ffn", l), ("xs", "ffn", l))
                pe.wait_ge(*ready("dve", "modulated", "ffn", l, 3))
                ffn("ffn2", l)
                barrier()

        @block.vector
        def _(dve):
            barrier = barrier_of(dve)

            def step(ins, *key):
                ins.then_inc(*made("dve", *key))
                dve.wait_ge(S.sem("dve"), S.count["dve"])

            def xstep(ins, *key):
                ins.then_inc(*made("x_dve", *key))
                value = S.count["x_dve"] + S.credit("x_dve")
                dve.wait_ge(S.sem("x_dve"), S.turn * (known.per_turn["x_dve"] if known else 1) + value)

            def free(ins, *key):
                ins.then_inc(*made("dve", *key))

            def two(v):
                return v.rearrange("p (a b) -> p a b", a=2)

            def layer_norm(src, *key, add=None):
                def root(t):
                    dve.wait_ge(*ready("act", "sd", *key, t))
                    step(dve.reciprocal(rs[:, t:t + 1], sd[:, t:t + 1]))
                    step(dve.scalar_tensor_tensor(out=x[:, t, :], in0=src[:, t, :], scalar=mv[:, t, 0:1],
                                                  in1=rows[:, 0, :], op0=ALU.subtract, op1=ALU.mult))
                    step(dve.scalar_tensor_tensor(out=x[:, t, :], in0=x[:, t, :], scalar=rs[:, t:t + 1],
                                                  in1=rows[:, 1, :], op0=ALU.mult, op1=ALU.add), "ln", *key, t)

                dve.wait_ge(*ready("rows", *key))
                for t in range(NT):
                    if add is not None:
                        add(t)
                    if t > 0 and key[0] == "ln2":
                        root(t - 1)
                    for h in range(2):
                        free(dve.bn_stats(stat[:, t, h, :], src[:, t, h * 512:h * 512 + 512]))
                    dve.wait_ge(S.sem("dve"), S.count["dve"])
                    step(dve.bn_aggr(mv[:, t, :], stat[:, t, :, :].rearrange("p h s -> p (h s)")), "var", *key, t)
                    if t == NT - 1 or key[0] == "ln1":
                        root(t)

            def ffn_piece(key):
                for s in range(STEPS):
                    n = 256 * min(2, FT - 2 * s)
                    dve.wait_ge(*ready("act", "silu", *key, s))
                    dve.wait_ge(*ready("pe_job", "h3", *key, s))
                    if s >= 3:
                        dve.wait_ge(*ready("pe_job", "down", *key, s - 3))
                    free(dve.tensor_tensor(gT[:, s % 3, 0:n], sil[:, s % 2, 0:n], psum[:, (2 * s + 1) % 4, 0:n],
                                           ALU.mult), "g", *key, s)

            def add_piece(seg, l, p, t):
                key = (seg, l, p)
                dve.wait_ge(*(ready("pe_job", "sum", *key) if t == 0 else ready("pe_job", "down", *key, STEPS - 1)))
                for h in range(2):
                    xs = x[:, t, h * 512:h * 512 + 512]
                    ys = psum[:, 4 + 2 * t + h, :]
                    if seg == "ffn1":
                        step(dve.tensor_tensor(xs, ys, xs, ALU.add), "acc", *key)
                    else:
                        gs = vtm[:, t, h * 512:h * 512 + 512]
                        step(dve.tensor_tensor(gs, ys, grow[:, 1, h * 512:h * 512 + 512], ALU.mult))
                        step(dve.tensor_tensor(xs, gs, xs, ALU.add), "acc", *key)

            def ffn(seg, l):
                if seg == "moe":
                    experts()
                else:
                    for p in range(2):
                        ffn_piece((seg, l, p))
                        if p == 0 or seg == "ffn2":
                            for t in range(NT):
                                add_piece(seg, l, p, t)

            def matrices(do):
                do(dve.tensor_scalar(found[:], turn_of[:], turn_no, None, ALU.is_equal))
                do(dve.tensor_tensor(found_slot[:], found[:], slot1[:], ALU.mult))
                do(dve.tensor_reduce(slot_now[:], found_slot[:], AX, ALU.add))
                do(dve.tensor_tensor(found_wt[:], found[:], wts, ALU.mult))
                do(dve.tensor_reduce(wt_now[:], found_wt[:], AX, ALU.add))
                do(dve.tensor_scalar(slot_now[:], slot_now[:], -1.0, None, ALU.add))
                do(dve.tensor_scalar(turn_no, turn_no, 1.0, None, ALU.add))
                for t in range(NT):
                    do(dve.tensor_scalar(gather[:, t, :], number[:], slot_now[:, t:t + 1], None, ALU.is_equal))
                    do(dve.tensor_scalar(scatter[:, t, :], number[:], slot_now[:, t:t + 1], wt_now[:, t:t + 1],
                                         ALU.is_equal, ALU.mult), "matrices" if do is xstep else "matrices0")

            def experts():
                dve.wait_ge(*ready("pool", "numbers"))
                step(dve.tensor_tensor(onehot[:], number[:, 0:N_EXP].unsqueeze(1).unsqueeze(1)
                                       .broadcast_to([P, NT, 2, N_EXP]),
                                       idxf[:, :, 0:2].unsqueeze(3).broadcast_to([P, NT, 2, N_EXP]), ALU.is_equal))
                step(dve.tensor_tensor(assigned[:], onehot[:, :, 0, :], onehot[:, :, 1, :], ALU.add), "assigned")
                dve.wait_ge(*ready("pe_job", "ranks"))
                for c in range(2):
                    step(dve.tensor_tensor(ranked[:, :, c, :], onehot[:, :, c, :],
                                           psum[:, 5, 0:16].rearrange("p (t e) -> p t e", t=NT), ALU.mult))
                step(dve.tensor_reduce(rank[:], ranked[:], AX, ALU.add))
                step(dve.tensor_scalar(over[:], rank[:], float(P), None, ALU.is_ge))
                step(dve.scalar_tensor_tensor(out=turn_of[:], in0=over[:], scalar=float(N_EXP), in1=idxf[:, :, 0:2],
                                              op0=ALU.mult, op1=ALU.add))
                step(dve.scalar_tensor_tensor(out=slot1[:], in0=over[:], scalar=-float(P), in1=rank[:],
                                              op0=ALU.mult, op1=ALU.add))
                step(dve.tensor_scalar(slot1[:], slot1[:], 1.0, None, ALU.add))
                step(dve.tensor_reduce(most[:, 0:1], psum[:, 5, 16:24], AX, ALU.max))
                step(dve.tensor_scalar(rounds[:, 0:1], most[:, 0:1], float(P), 1.0, ALU.is_gt, ALU.add))
                step(dve.tensor_scalar(rounds[:, 1:2], rounds[:, 0:1], float(N_EXP), None, ALU.mult))
                step(dve.tensor_copy(rounds_i[:], rounds[:]), "rounds")
                matrices(step)
                dve.wait_ge(*ready("pe_job", "turned0"))
                step(dve.tensor_copy(scatterT[:], two(psum[:, 4, 0:SEQ])), "scatterT0")
                n_turns = dve.value_load(rounds_i[0:1, 1:2], min_val=N_EXP, max_val=2 * N_EXP)
                with S.turns(dve, n_turns):
                    matrices(xstep)
                    for s in range(STEPS):
                        n = P * min(2, FT - 2 * s)
                        dve.wait_ge(*ready("x_act", "silu", s))
                        dve.wait_ge(*ready("x_pe", "h3", s))
                        dve.tensor_tensor(gT[:, s % 3, 0:n], sil[:, s % 2, 0:n], psum[:, (2 * s + 1) % 4, 0:n],
                                          ALU.mult).then_inc(*made("x_dve", "g", s))
                    for t in range(NT):
                        dve.wait_ge(*ready("x_pe", "scattered", t))
                        for h in range(2):
                            part_of = acc[:, t, h * 512:h * 512 + 512]
                            xstep(dve.tensor_tensor(part_of, part_of, psum[:, 2 * t + h, :], ALU.add), "acc", t)
                    dve.wait_ge(*ready("x_pe", "turned"))
                    xstep(dve.tensor_copy(scatterT[:], two(psum[:, 4, 0:SEQ])), "scatterT")

            def scores_in(l, seg, i, u, Sb):
                kind, hp = u
                b = i % 2
                dve.wait_ge(*ready("pe_job", "s", seg, l, u))
                if i >= 4:
                    dve.wait_ge(*ready("pe_job", "pt", seg, l, units_of(seg)[i - 4]))
                m = dsa_bias if kind == "dsa" else mask[:, 0 if kind == "swa" else 1, :]
                s = Sb[:, i % 4]
                step(dve.scalar_tensor_tensor(out=s, in0=psum[:, 2 * b:2 * b + 2, 0:PACK], scalar=SCALE,
                                              in1=m.unsqueeze(1).broadcast_to([P, 2, PACK]),
                                              op0=ALU.mult, op1=ALU.add), "sm", seg, l, u)
                for qt, (k0, nk) in enumerate(KEYS):
                    step(dve.tensor_reduce(mx[:, b, qt, :], s[:, :, k0:k0 + nk], AX, ALU.max))
                if kind == "swa":
                    sink = sinks[:, l, 2 * hp:2 * hp + 2].unsqueeze(1).broadcast_to([P, NT, 2])
                    step(dve.tensor_tensor(mx[:, b], mx[:, b], sink, ALU.max))
                    step(dve.tensor_tensor(es[:, b], sink, mx[:, b], ALU.subtract))
                step(dve.tensor_scalar(nm[:, b], mx[:, b], -1.0, None, ALU.mult), "nm", seg, l, u)

            def probs(l, seg, i, u, Sb):
                kind, hp = u
                b = i % 2
                dve.wait_ge(*ready("act", "exp", seg, l, u))
                if kind == "swa":
                    step(dve.tensor_tensor(den[:, b], den[:, b], es[:, b], ALU.add))
                step(dve.reciprocal(rc[:, b], den[:, b]))
                if kind == "diff":
                    step(dve.tensor_scalar(rc[:, b, :, 1], rc[:, b, :, 1], lam[:, 5:6], None, ALU.mult))
                for qt, (k0, nk) in enumerate(KEYS):
                    s = Sb[:, i % 4, :, k0:k0 + nk]
                    if kind == "diff":
                        step(dve.tensor_scalar(s[:, 1, :], s[:, 1, :], rc[:, b, qt, 1:2], None, ALU.mult))
                        step(dve.scalar_tensor_tensor(out=s[:, 0, :], in0=s[:, 0, :], scalar=rc[:, b, qt, 0:1],
                                                      in1=s[:, 1, :], op0=ALU.mult, op1=ALU.add), "p", seg, l, u)
                    else:
                        free(dve.tensor_tensor(s, s, rc[:, b, qt, :].unsqueeze(2).broadcast_to([P, 2, nk]),
                                               ALU.mult), "p", seg, l, u)

            def outs(l, seg, i, u):
                kind, hp = u
                dve.wait_ge(*ready("pe_job", "o", seg, l, u))
                bank = psum[:, o_bank(seg, i), 0:SEQ]
                if seg == "b1":
                    tile = {"swa": 0, "fox": 6, "dsa": 8}[kind] + hp
                    free(dve.tensor_copy(oT[:, tile, :], bank), "o", seg, l, u)
                else:
                    c0 = (0 if kind == "moba" else 512) + hp * P
                    step(dve.tensor_copy(om[:, :, c0:c0 + P], two(bank)), "o", seg, l, u)

            def out_sums(l, kind, c0, nh, d, name):
                o = om[:, :, c0:c0 + 512]
                step(dve.tensor_tensor(ys_tmp[:, :, 0:512], o, o, ALU.mult))
                step(dve.tensor_reduce(ss16[:, 0:NT * nh].rearrange("p (t h) -> p t h", t=NT),
                                       ys_tmp[:, :, 0:512].rearrange("p t (h d) -> p t h d", d=d), AX, ALU.add),
                     "outsum", l, kind)

            def out_norm(l, kind, c0, nh, d, name):
                dve.wait_ge(*ready("act", "outroot", l, kind))
                step(dve.reciprocal(ri16[:, 0:NT * nh], rt16[:, 0:NT * nh]))
                if kind == "diff":
                    step(dve.tensor_scalar(ri16[:, 0:NT * nh], ri16[:, 0:NT * nh], 1.0 - lambda_init(l), None,
                                           ALU.mult))
                o4 = om[:, :, c0:c0 + 512].rearrange("p t (h d) -> p t h d", d=d)
                shape = [P, NT, nh, d]
                step(dve.tensor_tensor(o4, o4, ri16[:, 0:NT * nh].rearrange("p (t h) -> p t h", t=NT)
                                       .unsqueeze(3).broadcast_to(shape), ALU.mult))
                step(dve.tensor_tensor(o4, o4, gain(name).unsqueeze(1).unsqueeze(1).broadcast_to(shape), ALU.mult))

            def attention(l, seg, Sb):
                units = units_of(seg)
                n = len(units)
                for i in range(n + 4):
                    if seg == "b2" and i == n + 3:
                        out_norm(l, *OUT_NORMS[0])
                    if i < n:
                        scores_in(l, seg, i, units[i], Sb)
                    if i >= 4:
                        outs(l, seg, i - 4, units[i - 4])
                    if 1 <= i < n + 1:
                        probs(l, seg, i - 1, units[i - 1], Sb)
                    if seg == "b2" and i == n:
                        out_sums(l, *OUT_NORMS[0])
                if seg == "b2":
                    out_sums(l, *OUT_NORMS[1])
                    out_norm(l, *OUT_NORMS[1])

            for l in range(DEPTH):
                step(dve.memset(raw[:, :, 0:1], 0.0))
                for i in (2, 4, 6, 8, 11, 12, 13):
                    b = in_bank(i)
                    dve.wait_ge(*ready("pe_job", "in", l, i))
                    bank = psum[:, b, :]
                    if i == 2:
                        for g in range(2):
                            for h in range(2):
                                free(dve.tensor_copy(swa_k[hb(h), g, :], psum[hb(g), b, 0:256]))
                        free(dve.tensor_copy(swa_v[:], two(psum[:, b, 256:512])), "in", l, i)
                    elif i in (4, 6):
                        r0 = {4: 2, 6: 6}[i]
                        step(dve.tensor_copy(raw[:, r0:r0 + 2, 1:], two(bank)), "in", l, i)
                    elif i == 8:
                        free(dve.tensor_copy(fox_k[:], two(bank)), "in", l, i)
                    elif i == 11:
                        for h in range(2):
                            free(dve.tensor_copy(dsa_k[hb(h), :], psum[0:HD, b, 0:256]))
                            free(dve.tensor_copy(dsa_ki[hb(h), :], psum[0:HD, b, 256:512]), "in", l, i)
                    elif i == 12:
                        free(dve.tensor_copy(dsa_qi[:], two(bank)), "in", l, i)
                    else:
                        free(dve.tensor_copy(dsa_v[:], two(psum[:, b, 0:128])))
                        free(dve.tensor_scalar(dsa_wi[:], two(psum[:, b, 128:136]), SCALE * 0.5, None, ALU.mult))
                        free(dve.tensor_copy(fox_f[:, 0, :], psum[0:4, b, 256:512]), "in", l, i)
                barrier()
                step(dve.tensor_tensor(mix[:], raw[:, :, 0:SEQ], raw[:, :, 1:], ALU.subtract))
                for i in range(8):
                    step(dve.scalar_tensor_tensor(out=mix[:, i, :], in0=mix[:, i, :], scalar=prm(l, "mu", i),
                                                  in1=raw[:, i, 1:], op0=ALU.mult, op1=ALU.add), "mix", l)
                r, k, v = mix[:, 0:2, :], mix[:, 2:4, :], mix[:, 4:6, :]
                for ct in range(2):
                    step(dve.tensor_scalar(kk[:, ct, :], k[:, ct, :], prm(l, "k_k", ct), None, ALU.mult))
                step(dve.tensor_tensor(sq[:], kk[:], kk[:], ALU.mult), "kk_sq", l)
                dve.wait_ge(*ready("act", "sw", l))
                for ct in range(2):
                    step(dve.tensor_tensor_scan(L[:, ct, :], chunk_gate[:], sw[:, ct, :], 0.0, ALU.mult, ALU.add))
                step(dve.tensor_tensor(Wp[:], L[:], sw[:], ALU.subtract), "decay", l)
                dve.wait_ge(*ready("act", "a", l))
                for ct in range(2):
                    step(dve.tensor_scalar(kp[:, ct, :], av[:, ct, :], -1.0, prm(l, "k_a", ct), ALU.add, ALU.mult))
                step(dve.scalar_tensor_tensor(out=kp[:], in0=kp[:], scalar=1.0, in1=k, op0=ALU.add, op1=ALU.mult))
                step(dve.tensor_tensor(yn[:], r, kp[:], ALU.mult))
                for ct in range(2):
                    step(dve.tensor_scalar(yn[:, ct, :], yn[:, ct, :], prm(l, "r_k", ct), None, ALU.mult), "rkr", l)
                dve.wait_ge(*ready("act", "kk_norm", l))
                step(dve.reciprocal(sq[:], sq[:]))
                step(dve.tensor_tensor(kk[:], kk[:], sq[:], ALU.mult))
                dve.wait_ge(*ready("act", "W", l))

                def chunks(t):
                    return t.rearrange("p a (c s) -> p a c s", c=NC)
                for ct in range(2):
                    def ch(t):
                        return t[:, ct, :].rearrange("p (c s) -> p c s", c=NC)
                    step(dve.tensor_tensor(KR[:, ct, :, 0, :], ch(kk), ch(Wp), ALU.mult))
                    step(dve.tensor_tensor(KR[:, ct, :, 1, :], ch(mix[:, 0:2, :]), ch(Wc), ALU.mult))
                step(dve.tensor_tensor(Bh[:], kk[:], av[:], ALU.mult))
                step(dve.tensor_tensor(Bh[:], Bh[:], Wi[:], ALU.mult))
                step(dve.tensor_tensor(kh[:], kp[:], Wi[:], ALU.mult), "scaled", l)
                dve.wait_ge(*ready("pe_job", "bonus", l))
                step(dve.tensor_tensor(kp[:], two(psum[:, 4, :]), v, ALU.mult), "bonus", l)
                both = tri[:].rearrange("p a b -> p (a b)").unsqueeze(1).broadcast_to([P, 2, P])
                for c in range(NC):
                    dve.wait_ge(*ready("pe_job", "gram", l, c))
                    for i, dst in enumerate((AB, GR)):
                        free(dve.tensor_tensor(dst[:, 2 * c:2 * c + 2].rearrange("p m a b -> p m (a b)"),
                                               two(psum[:, (0, 1, 4, 5)[c], 256 * i:256 * i + 256]), both, ALU.mult))

                def spread(m):
                    return m.unsqueeze(1).broadcast_to([P, 2 * NC, CH])
                step(dve.tensor_tensor(T[:], psum[:, 2, :].rearrange("p (m n) -> p m n", m=2 * NC), spread(level0[:]),
                                       ALU.mult))
                step(dve.tensor_tensor(T[:], T[:], spread(eye[:]), ALU.add))
                for lv in range(1, 6):
                    step(dve.tensor_tensor(BT[lv - 1][:], AB[:, :, 0, :], spread(level[:, lv, :]), ALU.mult),
                         "BT", l, lv)
                    if lv == 1:
                        step(dve.tensor_tensor(TT[:], AB[:, :, 0, :], spread(level[:, 0, :]), ALU.mult))
                        step(dve.tensor_tensor(TT[:], TT[:], spread(eye[:]), ALU.add), "TT", l)
                for lv in range(1, 6):
                    for g in range(2):
                        dve.wait_ge(*ready("pe_job", "TUT", l, lv, g))
                        for i, t in enumerate((T, TT)):
                            tg = t[:, 4 * g:4 * g + 4, :].rearrange("p m c -> p (m c)")
                            free(dve.tensor_tensor(tg, tg, psum[:, 4 * g + 1, 256 * i:256 * i + 256], ALU.add),
                                 "T", l, lv, g)
                for c in range(NC - 1):
                    z = c % 2
                    dve.wait_ge(*ready("pe_job", "Znew", l, c))
                    new = two(psum[:, 3, 0:2 * CH])
                    if c > 0:
                        step(dve.tensor_tensor(Z[:, z], new, Z[:, 1 - z], ALU.add))
                        new = Z[:, z]
                    for ct in range(2):
                        e = c * CH + CH - 1
                        step(dve.tensor_scalar(Z[:, z, ct, :], new[:, ct, :], Wc[:, ct, e:e + 1], None, ALU.mult),
                             "Z", l, c)
                dve.wait_ge(*ready("pe_job", "mean", l))
                step(dve.scalar_tensor_tensor(out=yv[:], in0=two(psum[:, 4, :]), scalar=-1.0 / HD, in1=yv[:],
                                              op0=ALU.mult, op1=ALU.add))
                step(dve.tensor_tensor(sq[:], yv[:], yv[:], ALU.mult), "y_sq", l)
                dve.wait_ge(*ready("act", "gn", l))
                step(dve.reciprocal(sq[:], sq[:]))
                step(dve.tensor_tensor(yv[:], yv[:], sq[:], ALU.mult))
                for ct in range(2):
                    step(dve.tensor_scalar(yv[:, ct, :], yv[:, ct, :], prm(l, "gn_g", ct), prm(l, "gn_b", ct),
                                           ALU.mult, ALU.add))
                step(dve.tensor_tensor(yv[:], yv[:], kp[:], ALU.add))
                step(dve.tensor_tensor(oT[:, 4:6, :], yv[:], gv[:], ALU.mult))
                barrier()

                low = slice(0, 4)
                step(dve.tensor_scalar(fox_t[low, 0, :], fox_f[:, 0, :], fbias[:, l:l + 1], None, ALU.add))
                step(dve.tensor_scalar(fox_t[low, 2, :], fox_t[low, 0, :], -1.0, None, ALU.mult))
                step(dve.tensor_tensor(fox_t[low, 1, :], fox_t[low, 0, :], fox_t[low, 2, :], ALU.max), "fox_abs", l)
                step(dve.tensor_scalar(fox_t[low, 0, :], fox_t[low, 0, :], 0.0, None, ALU.min))
                dve.wait_ge(*ready("act", "fox_ln", l))
                step(dve.tensor_tensor(fox_t[low, 0, :], fox_t[low, 0, :], fox_t[low, 1, :], ALU.subtract))
                step(dve.memset(fox_t[low, 2, :], 1.0))
                step(dve.tensor_tensor_scan(fox_t[low, 3, :], fox_t[low, 2, :], fox_t[low, 0, :], 0.0, ALU.mult,
                                            ALU.add))
                for i, val in enumerate((1.0 / SCALE, -1.0 / SCALE)):
                    for four in (low, slice(HD, HD + 4)):
                        step(dve.tensor_scalar(fox_t[four, i, :], fox_t[low, 3, :], val, None, ALU.mult), "fox_c", l)
                for qt, (k0, nk) in enumerate(KEYS):
                    dve.wait_ge(*ready("pe_job", "idx", l, qt))
                    for h2 in range(2):
                        for h in range(2):
                            dst = score if h2 + h == 0 else part
                            step(dve.tensor_scalar(dst[:, 0:nk],
                                                   psum[:, 4 + 2 * qt + h, h2 * 256:h2 * 256 + nk], 0.0,
                                                   dsa_wi[:, qt, 2 * h2 + h:2 * h2 + h + 1], ALU.max, ALU.mult),
                                 "pick", l, qt)
                            if h2 + h:
                                step(dve.tensor_tensor(score[:, 0:nk], score[:, 0:nk], part[:, 0:nk], ALU.add))
                    step(dve.tensor_tensor(score[:, 0:nk], score[:, 0:nk], mask[:, 2, k0:k0 + nk], ALU.add))
                    src = score[:, 0:nk]
                    for rnd in range(TOPK // 8):
                        step(dve.max(m8, src))
                        step(dve.match_replace(picked[:, rnd % 2, 0:nk], m8, src, TAKEN))
                        src = picked[:, rnd % 2, 0:nk]
                    step(dve.tensor_tensor(part[:, 0:nk], src, score[:, 0:nk], ALU.is_equal))
                    step(dve.tensor_scalar(dsa_bias[:, k0:k0 + nk], part[:, 0:nk], NEG, None, ALU.mult))
                attention(l, "b1", Sm)
                barrier()

                for c in range(KT):
                    dve.wait_ge(*ready("act", "sig", l, c))
                    dve.wait_ge(*ready("pe_job", "branch", l, c))
                    for b in range(2):
                        step(dve.tensor_tensor(two(prod[:, c % 2, b, :]), zb[:, 2 * b:2 * b + 2, c, :],
                                               two(psum[:, 4 + 2 * (c % 2) + b, :]), ALU.mult), "prod", l, c)
                    step(dve.tensor_tensor(prod[:, c % 2, 0, :], prod[:, c % 2, 0, :], prod[:, c % 2, 1, :], ALU.add))
                    step(dve.tensor_tensor(mergedT[:, c, :], prod[:, c % 2, 0, 0:256], prod[:, c % 2, 0, 256:512],
                                           ALU.add), "merged", l)
                barrier()
                def residual(t):
                    dve.wait_ge(*ready("pe_job", "out", l, t))
                    for h in range(2):
                        xs = x[:, t, h * 512:h * 512 + 512]
                        step(dve.scalar_tensor_tensor(out=xs, in0=xs, scalar=ALPHA, in1=psum[:, 4 + 2 * t + h, :],
                                                      op0=ALU.mult, op1=ALU.add))
                layer_norm(x, "ln1", l, add=residual)
                dve.wait_ge(*ready("pe_job", "xt", "f1", l, 3))
                for t in range(NT):
                    step(dve.tensor_scalar((x if l == 0 else acc)[:, t, :], x[:, t, :], ALPHA, None, ALU.mult))
                if l == 1:
                    dve.wait_ge(*ready("pe_job", "router"))
                    step(dve.tensor_tensor(logit[:], psum[:, 4, 0:16].rearrange("p (t e) -> p t e", t=NT),
                                           router_b[:].unsqueeze(1).broadcast_to([P, NT, N_EXP]), ALU.add),
                         "router_logits")
                    for t in range(NT):
                        step(dve.max(top8[:, t, :], logit[:, t, :]))
                        step(dve.max_index(idx8[:, t, :].bitcast(U32), top8[:, t, :], logit[:, t, :]))
                    step(dve.tensor_copy(idxf[:], idx8.bitcast(U32)))
                    step(dve.tensor_tensor(e2, top8[:, :, 1], top8[:, :, 0], ALU.subtract), "router_gap")
                    dve.wait_ge(*ready("act", "router_exp"))
                    step(dve.tensor_scalar(wts[:, :, 0], e2, 1.0, None, ALU.add))
                    step(dve.reciprocal(wts[:, :, 0], wts[:, :, 0]))
                    step(dve.tensor_tensor(wts[:, :, 1], wts[:, :, 0], e2, ALU.mult))
                    step(dve.memset(turn_no, 0.0))
                ffn("ffn1" if l == 0 else "moe", l)
                layer_norm(x if l == 0 else acc, "ln2", l,
                           add=(lambda t: add_piece("ffn1", 0, 1, t)) if l == 0 else None)
                barrier()

            step(dve.tensor_copy(ang[:, 0, 0:NT], pos[:]))
            for t in range(NT):
                step(dve.tensor_scalar(ang[:, 1, t * 8:t * 8 + 8], invf[:], ang[:, 0, t:t + 1], None, ALU.mult))
            for dst, quarter in ((1, 0.0), (2, 0.25)):
                src = ang[:, 1, :] if dst == 1 else ang[:, 0, :]
                if dst == 1:
                    step(dve.tensor_copy(ang[:, 0, :], ang[:, 1, :]))
                    src = ang[:, 0, :]
                step(dve.tensor_scalar(ang[:, dst, :], src, 1.0 / (2 * math.pi), quarter, ALU.mult, ALU.add))
                step(dve.tensor_copy(angi, ang[:, dst, :]))
                step(dve.tensor_copy(rope[:, 0, 0:16], angi))
                step(dve.tensor_scalar(ang[:, dst, :], rope[:, 0, 0:16], -TWO_PI_A, None, ALU.mult))
                step(dve.tensor_tensor(ang[:, dst, :], ang[:, dst, :], src, ALU.add))
                for cst in (TWO_PI_B, TWO_PI_C):
                    step(dve.scalar_tensor_tensor(out=ang[:, dst, :], in0=rope[:, 0, 0:16], scalar=-cst,
                                                  in1=ang[:, dst, :], op0=ALU.mult, op1=ALU.add))
                if dst == 2:
                    step(dve.tensor_scalar(ang[:, dst, :], ang[:, dst, :], math.pi / 2, None, ALU.add))
                step(dve.tensor_scalar(rope[:, 1, 0:16], ang[:, dst, :], math.pi, -2 * math.pi, ALU.is_gt, ALU.mult))
                step(dve.tensor_tensor(ang[:, dst, :], ang[:, dst, :], rope[:, 1, 0:16], ALU.add))
                step(dve.tensor_scalar(rope[:, 1, 0:16], ang[:, dst, :], -math.pi, 2 * math.pi, ALU.is_lt, ALU.mult))
                step(dve.tensor_tensor(ang[:, dst, :], ang[:, dst, :], rope[:, 1, 0:16], ALU.add))
                step(dve.tensor_scalar(ang[:, dst, :], ang[:, dst, :], PI_IN, -PI_IN, ALU.min, ALU.max), "angles")

            def rms_rows(which, l, add=None):
                if add is not None:
                    for t in range(NT):
                        add(t)
                for t in range(NT):
                    dve.wait_ge(*ready("act", "rms", which, l, t))
                    step(dve.reciprocal(rs[:, t:t + 1], sd[:, t:t + 1]))
                    step(dve.tensor_scalar(tok_scaled[:, t, :], x[:, t, :], rs[:, t:t + 1], None, ALU.mult),
                         "xs", which, l, t)

            def modulate(which, l, i):
                for j in range(4):
                    dve.wait_ge(*ready("pe_job", "xt", which, l, j))
                    for s in range(2):
                        k = 2 * j + s
                        free(dve.tensor_scalar(xT[:, k, :], psum[:, j, s * 256:s * 256 + 256], Amod[:, i, k:k + 1],
                                               modT[:, 16 * i + k:16 * i + k + 1], ALU.mult, ALU.add),
                             "modulated", which, l, j)

            for l in range(DEPTH):
                rms_rows("mix", l)
                dve.wait_ge(*ready("pe_job", "mod_columns", l))
                for seg_, c0 in ((0, 0), (1, 24)):
                    b0 = poff["b_mod"][0] + c0
                    step(dve.tensor_tensor(modT[:, 16 * seg_:16 * seg_ + 16], psum[:, 0, 16 * seg_:16 * seg_ + 16],
                                           par[:, l, b0:b0 + 16], ALU.add), "mod_columns", l)
                for i, name in enumerate(("norm_mix", "norm_ffn")):
                    step(dve.scalar_tensor_tensor(out=Amod[:, i, :], in0=modT[:, 16 * i + 8:16 * i + 16], scalar=1.0,
                                                  in1=prm(l, name, 0, 8), op0=ALU.add, op1=ALU.mult))
                modulate("mix", l, 0)
                dve.wait_ge(*ready("pe_job", "mod", l))
                dve.wait_ge(*ready("rows", "bmod", l))
                for i in range(2):
                    for h in range(2):
                        hs = slice(h * 512, h * 512 + 512)
                        step(dve.tensor_tensor(grow[:, i, hs], psum[:, 4 + 2 * i + h, :], rows[:, i, hs], ALU.add),
                             "mod_read", l)
                dve.wait_ge(*ready("gains", l))
                lp = gain("lambda").rearrange("p (i d) -> p i d", i=4)
                for i in range(2):
                    step(dve.tensor_tensor(lp[:, 2 * i, :], lp[:, 2 * i, :], lp[:, 2 * i + 1, :], ALU.mult))
                    step(dve.tensor_reduce(lam[:, i:i + 1], lp[:, 2 * i, :], AX, ALU.add), "lam_sums", l)
                dve.wait_ge(*ready("act", "lam", l))
                step(dve.tensor_tensor(lam[:, 4:5], lam[:, 3:4], lam[:, 2:3], ALU.subtract))
                step(dve.tensor_scalar(lam[:, 5:6], lam[:, 4:5], -lambda_init(l), None, ALU.add))
                for i in QK:
                    n = QK.index(i)
                    g = gain(("moba_q", "moba_k", "diff_q", "diff_k")[n // 2])
                    b = n % 2
                    q4 = tq[:, b, :].rearrange("p (h d) -> p h d", d=HD)
                    s8, r8, i8 = (v[:, 8 * b:8 * b + 8] for v in (ss16, rt16, ri16))
                    dve.wait_ge(*ready("act", "sq", l, i))
                    step(dve.tensor_reduce(s8, tsq[:, b, :].rearrange("p (h d) -> p h d", d=HD), AX, ALU.add),
                         "headsum", l, i)
                    dve.wait_ge(*ready("act", "headroot", l, i))
                    step(dve.reciprocal(i8, r8))
                    if n >= 2:
                        dve.wait_ge(*ready("pe_job", "qt", l, QK[n - 2]))
                    step(dve.tensor_tensor(q4, psum[:, i % 4, :].rearrange("p (h d) -> p h d", d=HD),
                                           i8.unsqueeze(2).broadcast_to([P, 8, HD]), ALU.mult), "normed", l, i)
                    step(dve.tensor_tensor(q4, q4, g.unsqueeze(1).broadcast_to([P, 8, HD]), ALU.mult))
                    qr = tq[:, b, :].rearrange("p (t h d) -> p t h d", t=NT, d=HD)
                    x1, x2 = qr[:, :, :, 0:8], qr[:, :, :, 8:16]
                    rp = [rope[:, k, :].rearrange("p (t h d) -> p t h d", t=NT, d=ROPE_HALF) for k in range(6)]
                    for t in range(NT):
                        c_, s_ = (v[:, t, :].unsqueeze(1).broadcast_to([P, 4, 8]) for v in (cosb, sinb))
                        step(dve.tensor_tensor(rp[0][:, t], x1[:, t], c_, ALU.mult))
                        step(dve.tensor_tensor(rp[1][:, t], x2[:, t], s_, ALU.mult))
                        step(dve.tensor_tensor(rp[2][:, t], x2[:, t], c_, ALU.mult))
                        step(dve.tensor_tensor(rp[3][:, t], x1[:, t], s_, ALU.mult))
                        step(dve.tensor_tensor(x1[:, t], rp[0][:, t], rp[1][:, t], ALU.subtract))
                        step(dve.tensor_tensor(x2[:, t], rp[2][:, t], rp[3][:, t], ALU.add), "roped", l, i)
                barrier()
                attention(l, "b2", Sm2)
                barrier()
                def residual2(t):
                    dve.wait_ge(*ready("pe_job", "out2", l, t))
                    for h in range(2):
                        hs = slice(h * 512, h * 512 + 512)
                        step(dve.tensor_tensor(tok_scaled[:, t, hs], psum[:, 4 + 2 * t + h, :], grow[:, 0, hs],
                                               ALU.mult))
                        step(dve.tensor_tensor(x[:, t, hs], x[:, t, hs], tok_scaled[:, t, hs], ALU.add), "res", l, t)
                rms_rows("ffn", l, add=residual2)
                modulate("ffn", l, 1)
                ffn("ffn2", l)
                if l == DEPTH - 1:
                    S.also("dve", "x", "end")
                barrier()

        return S


OUT_NORMS = [("moba", 0, 8, HD, "moba_out"), ("diff", 512, 4, 2 * HD, "diff_sub")]


def lambda_init(l):
    return 0.8 - 0.6 * math.exp(-0.3 * l)


QK = [0, 1, 2, 3, 6, 7, 8, 9]
UNITS1 = [("swa", hp) for hp in range(4)] + [("fox", hp) for hp in range(2)] + [("dsa", hp) for hp in range(2)]
UNITS2 = [("moba", hp) for hp in range(4)] + [("diff", hp) for hp in range(4)]
G = [2, 1, 1, 1, (1, 1, 1, 1, 0), (1, 1, 0, 0), 2, (4,), 1, 0, 1]
assert G[0] + G[1] + G[2] + G[3] + sum(G[4]) + sum(G[5]) + G[6] + len(G[7]) + G[8] + G[9] + G[10] == 16
BARRIERS_1, BARRIERS_2 = 5, 3
N_BARRIERS = DEPTH * (BARRIERS_1 + BARRIERS_2)


_INS = ["x", "w_in", "swa_sinks", "rwkv_mu", "rwkv_w0", "rwkv_w_up", "rwkv_a0", "rwkv_a_up", "rwkv_g_up",
        "rwkv_k_k", "rwkv_k_a", "rwkv_r_k", "rwkv_gn_g", "rwkv_gn_b", "fox_f_bias", "gate_bias", "w_branch",
        "w_out", "ln_g", "ln_b", "ffn_w1", "ffn_w3", "ffn_w2", "router_w", "router_b", "exp_w1", "exp_w3",
        "exp_w2", "c_2", "positions_2", "w_mod_2", "b_mod_2", "norm_mix_2", "w_in_2", "moba_q_norm_2",
        "moba_k_norm_2", "moba_out_norm_2", "diff_q_norm_2", "diff_k_norm_2", "diff_lambda_2",
        "diff_subln_2", "w_out_2", "norm_ffn_2", "w_gate_2", "w_up_2", "w_down_2"]


def program(arrays, known, bacc):
    nc = bacc.Bacc("TRN2", target_bir_lowering=False, num_devices=1)
    a = {}
    for name in _INS:
        v = arrays["in_" + name]
        a[name] = nc.dram_tensor("in_" + name, v.shape, mybir.dt.from_np(v.dtype), kind="ExternalInput").ap()
    out = nc.dram_tensor("out_0", (1, SEQ, D), F32, kind="ExternalOutput").ap()
    return nc, build(nc, a, out, known)


def kernel(**inputs):
    import concourse.bacc as bacc
    from concourse.bass_utils import run_bass_kernel_spmd as run

    arrays = {"in_" + name: np.ascontiguousarray(inputs[name]) for name in _INS}
    _, known = program(arrays, None, bacc)
    nc, _ = program(arrays, known, bacc)
    r = run(nc, [arrays], core_ids=[0])
    return r.results[0]["out_0"]
```
